# Optimizing a Trainium2 kernel written in Bass

```python
import jax, jax.numpy as jnp
from jax import lax
import numpy as np

D_MODEL = 1024
BATCH = 1
SEQ = 512
DEPTH = 2

CHUNK = 64
N_MIXERS = 2
N_A_LAYERS = (DEPTH + 1) // 2
N_B_LAYERS = DEPTH // 2
RMS_EPS = 1e-6

A_HEADS = 16
A_HEAD_DIM = D_MODEL // A_HEADS
A_KV_RANK = D_MODEL // 4
A_IDX_HEADS = 8
A_IDX_DIM = 64
A_TOPK_MAX = 256
A_QBLOCK = 128
A_SPLITS = [A_HEADS * A_HEAD_DIM,
            A_HEADS * A_HEAD_DIM + A_KV_RANK,
            A_HEADS * A_HEAD_DIM + A_KV_RANK + A_IDX_HEADS * A_IDX_DIM,
            A_HEADS * A_HEAD_DIM + A_KV_RANK + A_IDX_HEADS * A_IDX_DIM + A_IDX_DIM]
A_IN_COLS = A_SPLITS[-1] + A_IDX_HEADS

B_K_HEADS = 8
B_V_HEADS = 16
B_HEAD_DIM = 128
B_CONV = 4
B_KEY_WIDTH = B_K_HEADS * B_HEAD_DIM
B_VAL_WIDTH = B_V_HEADS * B_HEAD_DIM
B_CONV_WIDTH = 2 * B_KEY_WIDTH + B_VAL_WIDTH
B_IN_COLS = B_CONV_WIDTH + B_VAL_WIDTH + 2 * B_V_HEADS

P_HEADS = 8
P_N_KEYS = 128
P_N_EXPERTS = P_N_KEYS * P_N_KEYS
P_QUERY_DIM = 256
P_HALF = P_QUERY_DIM // 2
P_TOPK = 16
P_TOKEN_BLOCK = 128

kernel_name = "hybrid_dsa_gdn_peer_adaln"

def rms_norm(x, gain=None):
    xf = x.astype(jnp.float32)
    y = xf * lax.rsqrt(jnp.mean(xf * xf, axis=-1, keepdims=True) + RMS_EPS)
    if gain is not None:
        y = y * gain.astype(jnp.float32)
    return y.astype(x.dtype)

def l2_norm(x):
    xf = x.astype(jnp.float32)
    return xf * lax.rsqrt(jnp.sum(xf * xf, axis=-1, keepdims=True) + RMS_EPS)

def modulate(h, shift, scale):
    return h * (1.0 + scale[:, None, :]) + shift[:, None, :]

def dsa_mixer(h, w_in, kv_norm, w_uk, w_uv, w_out):
    b, t, _ = h.shape
    proj = h @ w_in
    q, c_kv, q_idx, k_idx, w_idx = jnp.split(proj, A_SPLITS, axis=-1)
    q = q.reshape(b, t, A_HEADS, A_HEAD_DIM)
    c_kv = rms_norm(c_kv, kv_norm)
    q_lat = jnp.einsum('bthd,rhd->bthr', q, w_uk) * (A_HEAD_DIM ** -0.5)
    q_idx = q_idx.reshape(b, t, A_IDX_HEADS, A_IDX_DIM)
    w_idx = w_idx * ((A_IDX_HEADS ** -0.5) * (A_IDX_DIM ** -0.5))
    n_sel = min(A_TOPK_MAX, t // 4)
    key_chunk = jnp.arange(t) // CHUNK

    def block(i):
        start = i * A_QBLOCK
        qi = lax.dynamic_slice_in_dim(q_idx, start, A_QBLOCK, axis=1)
        wi = lax.dynamic_slice_in_dim(w_idx, start, A_QBLOCK, axis=1)
        ql = lax.dynamic_slice_in_dim(q_lat, start, A_QBLOCK, axis=1)
        q_chunk = (start + jnp.arange(A_QBLOCK)) // CHUNK
        admissible = key_chunk[None, :] <= q_chunk[:, None]
        raw = jax.nn.relu(jnp.einsum('bqhd,bsd->bqhs', qi, k_idx))
        score = jnp.einsum('bqh,bqhs->bqs', wi, raw).astype(jnp.float32)
        score = jnp.where(admissible[None], score, -jnp.inf)
        top_val, top_idx = lax.top_k(score, n_sel)
        valid = jnp.isfinite(top_val)
        c_sel = jax.vmap(lambda cb, ib: cb[ib])(c_kv, top_idx)
        logits = jnp.einsum('bqhr,bqkr->bqhk', ql, c_sel).astype(jnp.float32)
        logits = jnp.where(valid[:, :, None, :], logits, -jnp.inf)
        p = jax.nn.softmax(logits, axis=-1).astype(h.dtype)
        o_lat = jnp.einsum('bqhk,bqkr->bqhr', p, c_sel)
        return jnp.einsum('bqhr,rhd->bqhd', o_lat, w_uv)

    out = lax.map(block, jnp.arange(t // A_QBLOCK))
    out = out.transpose(1, 0, 2, 3, 4).reshape(b, t, A_HEADS * A_HEAD_DIM)
    return out @ w_out

def chunk_gated_delta_rule(q, k, v, g, beta):
    b, t, nh, dk = q.shape
    dv = v.shape[-1]
    n = t // CHUNK
    f32 = jnp.float32

    def to_chunks(a):
        return a.astype(f32).reshape(b, n, CHUNK, nh, -1).transpose(0, 3, 1, 2, 4)

    def to_chunks_s(a):
        return a.astype(f32).reshape(b, n, CHUNK, nh).transpose(0, 3, 1, 2)

    q = to_chunks(q) * (dk ** -0.5)
    k = to_chunks(k)
    v = to_chunks(v)
    beta = to_chunks_s(beta)
    g = jnp.cumsum(to_chunks_s(g), axis=-1)
    tril = jnp.tril(jnp.ones((CHUNK, CHUNK), bool))
    strict = jnp.tril(jnp.ones((CHUNK, CHUNK), bool), -1)
    decay = jnp.exp(jnp.where(tril, g[..., :, None] - g[..., None, :], -jnp.inf))
    k_beta = k * beta[..., None]
    a_low = jnp.where(strict, jnp.einsum('bhncd,bhnsd->bhncs', k_beta, k) * decay, 0.0)
    lhs = a_low + jnp.eye(CHUNK, dtype=f32)
    rhs = jnp.concatenate([v * beta[..., None], k_beta * jnp.exp(g)[..., None]], axis=-1)
    sol = lax.linalg.triangular_solve(lhs, rhs, left_side=True, lower=True, unit_diagonal=True)
    u, w = sol[..., :dv], sol[..., dv:]
    attn = jnp.where(tril, jnp.einsum('bhncd,bhnsd->bhncs', q, k) * decay, 0.0)

    def step(state, inp):
        q_i, k_i, u_i, w_i, g_i, a_i = inp
        v_new = u_i - jnp.einsum('bhcd,bhde->bhce', w_i, state)
        o = jnp.einsum('bhcd,bhde->bhce', q_i * jnp.exp(g_i)[..., None], state) + \
            jnp.einsum('bhcs,bhse->bhce', a_i, v_new)
        g_last = g_i[..., -1]
        state = state * jnp.exp(g_last)[..., None, None] + jnp.einsum(
            'bhcd,bhce->bhde', k_i * jnp.exp(g_last[..., None] - g_i)[..., None], v_new)
        return state, o

    xs = tuple(jnp.moveaxis(a, 2, 0) for a in (q, k, u, w, g, attn))
    state0 = jnp.zeros((b, nh, dk, dv), f32)
    _, o = lax.scan(step, state0, xs)
    return o.transpose(1, 0, 3, 2, 4).reshape(b, t, nh, dv)

def gated_deltanet_mixer(h, w_in, conv_w, a_log, dt_bias, out_norm, w_out):
    b, t, _ = h.shape
    proj = h @ w_in
    qkv, z, beta_raw, a_raw = jnp.split(
        proj, [B_CONV_WIDTH, B_CONV_WIDTH + B_VAL_WIDTH, B_CONV_WIDTH + B_VAL_WIDTH + B_V_HEADS], axis=-1)
    qkv = lax.conv_general_dilated(qkv, conv_w.astype(qkv.dtype), window_strides=(1,),
                                   padding=[(B_CONV - 1, 0)],
                                   dimension_numbers=('NWC', 'WIO', 'NWC'),
                                   feature_group_count=B_CONV_WIDTH)
    qkv = jax.nn.silu(qkv)
    q, k, v = jnp.split(qkv, [B_KEY_WIDTH, 2 * B_KEY_WIDTH], axis=-1)
    rep = B_V_HEADS // B_K_HEADS
    q = jnp.repeat(l2_norm(q.reshape(b, t, B_K_HEADS, B_HEAD_DIM)), rep, axis=2)
    k = jnp.repeat(l2_norm(k.reshape(b, t, B_K_HEADS, B_HEAD_DIM)), rep, axis=2)
    v = v.reshape(b, t, B_V_HEADS, B_HEAD_DIM)
    beta = jax.nn.sigmoid(beta_raw.astype(jnp.float32))
    g = -jnp.exp(a_log.astype(jnp.float32)) * jax.nn.softplus(
        a_raw.astype(jnp.float32) + dt_bias.astype(jnp.float32))
    o = chunk_gated_delta_rule(q, k, v, g, beta)
    z = z.reshape(b, t, B_V_HEADS, B_HEAD_DIM).astype(jnp.float32)
    o = rms_norm(o, out_norm) * jax.nn.silu(z)
    return o.reshape(b, t, B_VAL_WIDTH).astype(h.dtype) @ w_out

def peer_ffn(h, w_q, sub_keys, u_tab, v_tab):
    b, t, d = h.shape
    n_tok = b * t
    x = h.reshape(n_tok, d)
    q = (x @ w_q).reshape(n_tok, P_HEADS, 2, P_HALF)
    s = jnp.einsum('nhpc,hpkc->nhpk', q, sub_keys).astype(jnp.float32)
    v1, i1 = lax.top_k(s[:, :, 0], P_TOPK)
    v2, i2 = lax.top_k(s[:, :, 1], P_TOPK)
    cand = (v1[..., :, None] + v2[..., None, :]).reshape(n_tok, P_HEADS, P_TOPK * P_TOPK)
    cand_idx = (i1[..., :, None] * P_N_KEYS + i2[..., None, :]).reshape(n_tok, P_HEADS, P_TOPK * P_TOPK)
    top_s, pos = lax.top_k(cand, P_TOPK)
    expert = jnp.take_along_axis(cand_idx, pos, axis=-1)
    gate = jax.nn.softmax(top_s, axis=-1).astype(h.dtype)
    n_blk = n_tok // P_TOKEN_BLOCK

    def blk(args):
        xb, eb, gb = args
        u = jnp.take(u_tab, eb, axis=0)
        act = jax.nn.gelu(jnp.einsum('td,thkd->thk', xb, u), approximate=False)
        vv = jnp.take(v_tab, eb, axis=0)
        return jnp.einsum('thk,thkd->td', gb * act, vv)

    y = lax.map(blk, (x.reshape(n_blk, P_TOKEN_BLOCK, d),
                      expert.reshape(n_blk, P_TOKEN_BLOCK, P_HEADS, P_TOPK),
                      gate.reshape(n_blk, P_TOKEN_BLOCK, P_HEADS, P_TOPK)))
    return y.reshape(b, t, d)

def setup_inputs(seed: int = 0) -> dict:
    key = jax.random.key(seed)
    ks = jax.random.split(key, 20)
    nrm = jax.random.normal
    D = D_MODEL
    dt = jnp.exp(jax.random.uniform(ks[10], (N_B_LAYERS, B_V_HEADS),
                                    minval=float(np.log(1e-3)), maxval=float(np.log(0.1))))
    return {
        "x": nrm(ks[0], (BATCH, SEQ, D), jnp.float32),
        "c": nrm(ks[1], (BATCH, D), jnp.float32),
        "a_w_in": nrm(ks[2], (N_A_LAYERS, D, A_IN_COLS)) * D ** -0.5,
        "a_kv_norm": 1.0 + 0.02 * nrm(ks[3], (N_A_LAYERS, A_KV_RANK)),
        "a_w_uk": nrm(ks[4], (N_A_LAYERS, A_KV_RANK, A_HEADS, A_HEAD_DIM)) * A_KV_RANK ** -0.5,
        "a_w_uv": nrm(ks[5], (N_A_LAYERS, A_KV_RANK, A_HEADS, A_HEAD_DIM)) * A_KV_RANK ** -0.5,
        "a_w_out": nrm(ks[6], (N_A_LAYERS, A_HEADS * A_HEAD_DIM, D)) * (A_HEADS * A_HEAD_DIM) ** -0.5,
        "b_w_in": nrm(ks[7], (N_B_LAYERS, D, B_IN_COLS)) * D ** -0.5,
        "b_conv": nrm(ks[8], (N_B_LAYERS, B_CONV, 1, B_CONV_WIDTH)) * B_CONV ** -0.5,
        "b_a_log": jnp.log(jax.random.uniform(ks[9], (N_B_LAYERS, B_V_HEADS), minval=1.0, maxval=16.0)),
        "b_dt_bias": dt + jnp.log(-jnp.expm1(-dt)),
        "b_out_norm": 1.0 + 0.02 * nrm(ks[11], (N_B_LAYERS, B_HEAD_DIM)),
        "b_w_out": nrm(ks[12], (N_B_LAYERS, B_VAL_WIDTH, D)) * B_VAL_WIDTH ** -0.5,
        "p_w_q": nrm(ks[13], (DEPTH, D, P_HEADS * P_QUERY_DIM)) * D ** -0.5,
        "p_sub_keys": nrm(ks[14], (DEPTH, P_HEADS, 2, P_N_KEYS, P_HALF)) * P_HALF ** -0.5,
        "p_u": nrm(ks[15], (DEPTH, P_N_EXPERTS, D)) * D ** -0.5,
        "p_v": nrm(ks[16], (DEPTH, P_N_EXPERTS, D)),
        "ada_w": nrm(ks[17], (DEPTH, D, 6 * D)) * (0.5 * D ** -0.5),
        "ada_b": 0.02 * nrm(ks[18], (DEPTH, 6 * D)),
        "final_norm": 1.0 + 0.02 * nrm(ks[19], (D,)),
    }

def reference(x, c, a_w_in, a_kv_norm, a_w_uk, a_w_uv, a_w_out, b_w_in, b_conv, b_a_log,
              b_dt_bias, b_out_norm, b_w_out, p_w_q, p_sub_keys, p_u, p_v, ada_w, ada_b,
              final_norm):
    cond = jax.nn.silu(c)
    for layer in range(DEPTH):
        mod = cond @ ada_w[layer] + ada_b[layer]
        sh_m, sc_m, g_m, sh_f, sc_f, g_f = jnp.split(mod, 6, axis=-1)
        h = modulate(rms_norm(x), sh_m, sc_m)
        j = layer // N_MIXERS
        if layer % N_MIXERS == 0:
            mix = dsa_mixer(h, a_w_in[j], a_kv_norm[j], a_w_uk[j], a_w_uv[j], a_w_out[j])
        else:
            mix = gated_deltanet_mixer(h, b_w_in[j], b_conv[j], b_a_log[j], b_dt_bias[j],
                                       b_out_norm[j], b_w_out[j])
        x = x + g_m[:, None, :] * mix
        h = modulate(rms_norm(x), sh_f, sc_f)
        x = x + g_f[:, None, :] * peer_ffn(h, p_w_q[layer], p_sub_keys[layer], p_u[layer], p_v[layer])
    return rms_norm(x, final_norm)


_drawn_inputs = setup_inputs


def setup_inputs(seed=0):
    import zlib

    import numpy as np

    out = dict(_drawn_inputs(seed))
    spreads = {}
    factors = {'a_kv_norm': 3.215, 'b_out_norm': 4.607, 'final_norm': 2.833}
    for name, (base, spread) in spreads.items():
        noise = np.random.default_rng([zlib.crc32(name.encode()), seed]).standard_normal(out[name].shape)
        drawn = base * np.exp(spread * noise) if base else spread * noise
        out[name] = __import__('jax').numpy.asarray(drawn.astype(out[name].dtype))
    for name, factor in factors.items():
        out[name] = (out[name] * factor).astype(out[name].dtype)
    return out
```

```python
import math
from contextlib import ExitStack, contextmanager

import concourse.bass as bass
from concourse import mybir
from concourse.alu_op_type import AluOpType as ALU

F32 = mybir.dt.float32
F32R = mybir.dt.float32r
BF16 = mybir.dt.bfloat16
U32 = mybir.dt.uint32
I32 = mybir.dt.int32
ACT = mybir.ActivationFunctionType
AX = mybir.AxisListType
ds = bass.ds

P = 128
T = 512
TT = T // P
D = 1024
KD = D // P
EPS = 1e-6
CHUNK = 64

HEADS, HD, RANK = 16, 64, 256
IH, ID = 8, 64
SEL = min(256, T // 4)
C_Q, C_KV, C_QI, C_KI = 0, HEADS * HD, HEADS * HD + RANK, HEADS * HD + RANK + IH * ID
C_WI = C_KI + ID
NEG, TAKEN = -1.0e30, -3.0e38

KH, VH, BD = 8, 16, 128
NCH = T // CHUNK
C_BETA = 2 * KH * BD + 2 * VH * BD
HB = 32

PH, NK, TOPK = 8, 128, 16
PM = 2 * PH
ROWS = [TOPK // (a + 1) for a in range(TOPK)]
NC_ = sum(ROWS)
GT = 8
NG = NK // GT

FREE_AT_START = {"conv_done": 1, "attn_raw": 1, "pack_ready": 1, "amat_ready": 1, "OT_ready": 1}
FREE_AT_START |= {f"split_done{s}": 1 for s in range(4)} | {f"scores_used{s}": 1 for s in range(2)}
FREE_AT_START |= {f"{n}{s}": 16 for n in ("gst_stored", "pack_stored", "amat_stored") for s in range(2)}

SH_M, SC_M, G_M, SH_F, SC_F, G_F = (KD * n for n in range(6))


class Tally:

    def __init__(self, eng):
        self.eng, self.n, self.loops = eng, {}, []

    def now(self, key):
        v = self.n.get(key, 0)
        for i, per in self.loops:
            if key in per:
                v = i * per[key] + v
        return v

    def turn(self, key, by=1):
        v = self.now(key)
        self.n[key] = self.n.get(key, 0) + by
        return v

    @contextmanager
    def loop(self, times, per):
        start = dict(self.n)
        with self.eng.Fori(0, times) as i:
            self.loops.append((i, per))
            yield i
            had = {k: v - start.get(k, 0) for k, v in self.n.items() if v != start.get(k, 0)}
            assert had == per, (had, per)
            self.loops.pop()
        for k, v in per.items():
            self.n[k] = start.get(k, 0) + times * v
def hybrid_trunk(nc, x_t, c_t, ada_w, ada_b, a_w_in, a_kv_norm, a_w_uk, a_w_uv, a_w_out, b_w_in, b_conv,
                 b_a_log, b_dt_bias, b_out_norm, b_w_out, p_w_q, p_keys_t, p_u_t, p_v, final_norm, out_t,
                 stop=99):
    ctx = ExitStack()
    sems = {}

    def sem(name):
        if name not in sems:
            sems[name] = ctx.enter_context(nc.semaphore(name))
        return sems[name]

    def sb(name, shape, dt=F32, where=None):
        return (where or ctx).enter_context(nc.sbuf_tensor(name, shape, dt))

    def dram(name, shape, dt=F32):
        return nc.dram_tensor(name, shape, dt).ap()

    with ctx:
        bank = [ctx.enter_context(nc.psum_tensor(f"bank{b}", [P, T], F32)) for b in range(8)]
        psum_full = [sem(f"psum_full{b}") for b in range(8)]
        psum_free = [sem(f"psum_free{b}") for b in range(8)]

        xT = sb("xT", [P, KD, T])
        hT = sb("hT", [P, KD, T])
        rstd = sb("rstd", [P, T])
        mods = sb("mods", [P, 2, 6 * KD])
        ident = sb("ident", [P, P])
        ones = sb("ones", [P, P])
        fnorm = sb("fnorm", [P, KD])
        kvn = sb("kvn", [P, 2])
        w_ring = sb("w_ring", [P, 2, KD, P])
        iota = sb("iota", [P, P])
        iota_b = sb("iota_b", [P, P], BF16)
        iota_i = sb("iota_i", [P, P], I32)

        part = ExitStack()
        condT = sb("condT", [P, KD], where=part)
        ada_ring = sb("ada_ring", [P, 2, KD, T], where=part)
        ada_row = sb("ada_row", [1, 2, 6 * D], where=part)
        ada_sq = sb("ada_sq", [2 * 6 * KD, P], where=part)
        adab = sb("adab", [P, 2, 6 * KD], where=part)
        part.close()
        ada_dram = dram("ada_scratch", [2 * 6 * KD, P])

        part = ExitStack()
        ckvT = sb("ckvT", [P, 2, T], where=part)
        ckv_sq = sb("ckv_sq", [P, 2, T], where=part)
        kidxT = sb("kidxT", [P, T], where=part)
        qidxT = sb("qidxT", [P, 4, T], where=part)
        widx = sb("widx", [P, TT, IH], where=part)
        relu = sb("relu", [P, 2, T], where=part)
        score = sb("score", [P, TT, T], where=part)
        top8 = sb("top8", [P, TT, 8], where=part)
        maskb = sb("maskb", [P, TT, T], where=part)
        w_ukv = sb("w_ukv", [P, 2, 2, HEADS * HD], where=part)
        qT = sb("qT", [P, KD, T], where=part)
        kT = sb("kT", [P, KD, T], where=part)
        vA = sb("vA", [P, TT, HEADS * HD], where=part)
        q_pair = sb("q_pair", [P, T], where=part)
        k_pair = sb("k_pair", [P, T], where=part)
        v_pair = sb("v_pair", [P, TT, P], where=part)
        lg = sb("lg", [P, 4, T], where=part)
        prob = sb("prob", [P, 4, T], where=part)
        mx = sb("mx", [P, 4], where=part)
        nmx = sb("nmx", [P, 4], where=part)
        rowsum = sb("rowsum", [P, 4], where=part)
        rinv = sb("rinv", [P, 4], where=part)
        probT = sb("probT", [P, 2, TT, T], where=part)
        oT = sb("oT", [P, KD, T], where=part)
        part.close()

        part = ExitStack()
        keys = sb("keys", [P, 2, NK], where=part)
        qm = sb("qm", [P, 2, T], where=part)
        sS = sb("sS", [P, 2, TT, NK], where=part)
        sW = sb("sW", [P, TT, NK], where=part)
        val = sb("val", [P, 2, TT, TOPK], where=part)
        idx = sb("idx", [P, 2, TT, TOPK], U32, where=part)
        V = sb("V", [P, TT, PM, TOPK], where=part)
        I = sb("I", [P, TT, PM, TOPK], where=part)
        cand = sb("cand", [P, TT * PH, NC_], where=part)
        code = sb("code", [P, TT * PH, NC_], where=part)
        cS = sb("cS", [P, PH, NC_], where=part)
        cW = sb("cW", [P, PH, NC_], where=part)
        topv = sb("topv", [P, PH, TOPK], where=part)
        topp = sb("topp", [P, 2, PH, TOPK], U32, where=part)
        posf = sb("posf", [P, 2, PH, TOPK], where=part)
        eq = sb("eq", [P, 2, PH, TOPK, NC_], where=part)
        iotac = sb("iotac", [P, NC_], where=part)
        iotac_i = sb("iotac_i", [P, NC_], I32, where=part)
        TS = sb("TS", [P, TT, PH, TOPK], where=part)
        E = sb("E", [P, TT, PH, TOPK], where=part)
        Ei = sb("Ei", [P, 2, TT * P], I32, where=part)
        Ef = sb("Ef", [P, 2, TT * P], where=part)
        tsum = sb("tsum", [P, TT * PH], where=part)
        part.close()

        part = ExitStack()
        gst = sb("gst", [P, 2, NK, P], where=part)
        gT = sb("gT", [P, T], where=part)
        iT = sb("iT", [P, 2, T], where=part)
        gp = sb("gp", [P, 3, T], where=part)
        gb = sb("gb", [P, T], BF16, where=part)
        oh1 = sb("oh1", [P, 2, 4, P], BF16, where=part)
        oh2 = sb("oh2", [P, 2, 4, 3, P], BF16, where=part)
        part.close()
        g_dram = dram("g_scratch", [NK, P, T])

        part = ExitStack()
        hx = sb("hx", [P, 2, KD, T], F32R, where=part)
        raw = sb("raw", [P, 4, KD, P], where=part)
        hl = sb("hl", [P, 4, 2, KD, P], F32R, where=part)
        gt = sb("gt", [P, 4, T], where=part)
        ga = sb("ga", [P, 2, T], where=part)
        wp = sb("wp", [P, 2, T], where=part)
        W = sb("W", [P, 2, 2, GT, T], F32R, where=part)
        part.close()

        part = ExitStack()
        tri = sb("tri", [P, P], where=part)
        strict = sb("strict", [P, P], where=part)
        samec = sb("samec", [P, P], where=part)
        decay_last = sb("decay_last", [P, 2, TT, VH], where=part)
        onorm = sb("onorm", [P, 1], where=part)
        OT = sb("OT", [P, VH, T], where=part)
        solve_ = ExitStack()
        gstat = sb("gstat", [P, 6, TT, VH], where=solve_)
        graw, gcum, eg, ekd, beta, bege = (gstat[:, n, :, :] for n in range(6))
        gtmp = sb("gtmp", [P, 3, TT, VH], where=solve_)
        alog = sb("alog", [P, VH], where=solve_)
        dtb = sb("dtb", [P, VH], where=solve_)
        convw = sb("convw", [P, 2 * KH + VH, 4], where=solve_)
        xs = sb("xs", [P, 2, 3 + T], where=solve_)
        cy = sb("cy", [P, 4, T], where=solve_)
        sq = sb("sq", [P, 2, T], where=solve_)
        rn = sb("rn", [P, 2, T], where=solve_)
        gsel = sb("gsel", [P, TT, 2], where=solve_)
        SG = sb("SG", [P, 2, TT, P], where=solve_)
        BS = sb("BS", [P, 2, TT, P], where=solve_)
        eD = sb("eD", [P, 2, TT, P], where=solve_)
        eDT = sb("eDT", [P, 2, TT, P], where=solve_)
        eG = sb("eG", [P, 2, T], where=solve_)
        ktok = sb("ktok", [P, TT, P], where=solve_)
        amat = sb("amat", [P, 2, TT, P], where=solve_)
        pack = sb("pack", [P, 2, 5, T], where=solve_)
        solve_.close()
        solve_ = ExitStack()
        SA = sb("SA", [P, 2, HB, HB], where=solve_)
        X = sb("X", [P, 2, HB, HB], where=solve_)
        prod = sb("prod", [P, 2 * HB * HB], where=solve_)
        solve_.close()
        vkb = sb("vkb", [P, 4, 2, T], where=part)
        kqa = sb("kqa", [P, 4, 3, T], where=part)
        Eb = sb("Eb", [P, 4, TT, P], where=part)
        Pb = sb("Pb", [P, 4, TT, P], where=part)
        Qs = sb("Qs", [P, 4, TT, P], where=part)
        Ys = sb("Ys", [P, 2, TT, P], where=part)
        us = sb("us", [P, 4, TT, P], where=part)
        wTs = sb("wTs", [P, 4, T], where=part)
        vn = sb("vn", [P, 4, P], where=part)
        S = sb("S", [P, 2, 4, P], where=part)
        oc = sb("oc", [P, 4, T], where=part)
        zs = sb("zs", [P, 4, T], where=part)
        o2 = sb("o2", [P, 4, T], where=part)
        part.close()
        a_dram = dram("a_scratch", [VH, NCH, CHUNK, CHUNK])
        t_dram = dram("t_scratch", [VH * NCH, 2, HB, HB])
        pack_dram = dram("pack_scratch", [VH, P, 5, T])

        block = ctx.enter_context(nc.Block())
        marks = {}

        @block.tensor
        def _(pe):
            t = Tally(pe)

            def mark(stage):
                marks[stage] = {k: v for k, v in t.n.items() if isinstance(k, int)}

            def take(b):
                pe.wait_ge(psum_free[b], t.turn(b))

            def slot_ready(s):
                pe.wait_ge(sem(f"w_loaded{s}"), t.turn(f"w{s}") * 16 + 16)

            def tile_product(s, rhs, out=None, m=P):
                slot_ready(s)
                take(s)
                for k in range(KD):
                    mm = nc.tensor.matmul(bank[s][0:m, :], w_ring[:, s, k, 0:m], rhs[:, k, :],
                                          start=(k == 0), stop=(k == KD - 1))
                mm.then_inc(psum_full[s], 1)

            def modulations():
                mark("mod")
                pe.wait_ge(sem("cond_ready"), 1)
                for n in range(24):
                    s = n % 2
                    pe.wait_ge(sem(f"ada_loaded{s}"), 16 * (n // 2 + 1))
                    take(s)
                    for k in range(KD):
                        mm = nc.tensor.matmul(bank[s][0:1, :], condT[:, k:k + 1], ada_ring[:, s, k, :],
                                              start=(k == 0), stop=(k == KD - 1))
                    mm.then_inc(psum_full[s], 1)
                pe.wait_ge(sem("ada_square"), 16)
                pe.wait_ge(sem("consts"), 2)
                take(2)
                nc.tensor.transpose(bank[2][:, 0:96], ada_sq[:, :], ident[0:96, 0:96]).then_inc(psum_full[2], 1)

            def norm(stage):
                mark(stage)
                pe.wait_ge(sem("squares"), t.turn("squares") + 1)
                take(2)
                for k in range(KD):
                    mm = nc.tensor.matmul(bank[2][:, :], ones[:, :], hT[:, k, :], start=(k == 0), stop=(k == KD - 1))
                mm.then_inc(psum_full[2], 1)

            def attention():
                mark("attn")
                pe.wait_ge(sem("h_ready"), t.turn("h_ready") + 1)
                tile_product(0, hT)
                tile_product(1, hT)
                tile_product(0, hT)
                pe.wait_ge(sem("ckv_squares"), 1)
                take(2)
                for r in range(2):
                    mm = nc.tensor.matmul(bank[2][:, :], ones[:, :], ckv_sq[:, r, :], start=(r == 0), stop=(r == 1))
                mm.then_inc(psum_full[2], 1)
                slot_ready(1)
                take(1)
                for tt in range(TT):
                    for k in range(KD):
                        mm = nc.tensor.matmul(bank[1][:, tt * IH:(tt + 1) * IH], hT[:, k, tt * P:(tt + 1) * P],
                                              w_ring[:, 1, k, 0:IH], start=(k == 0), stop=(k == KD - 1))
                mm.then_inc(psum_full[1], 1)
                for m in range(4):
                    tile_product(m % 2, hT)
                pe.wait_ge(sem("idx_ready"), 6)
                for n in range(TT * IH):
                    tt, h = n // IH, n % IH
                    r = ID * (h % 2)
                    b = 3 + n % 2
                    take(b)
                    nc.tensor.matmul(bank[b][:, 0:(tt + 1) * P], qidxT[r:r + ID, h // 2, tt * P:(tt + 1) * P],
                                     kidxT[r:r + ID, 0:(tt + 1) * P], start=True, stop=True).then_inc(psum_full[b], 1)
                with t.loop(KD // 2, {"w0": 1, "w1": 1, 0: 1, 1: 1}):
                    tile_product(0, hT)
                    tile_product(1, hT)
                pe.wait_ge(sem("ukv_loaded"), 32)
                pe.wait_ge(sem("ckv_ready"), 1)
                for m in range(KD):
                    b = 5 + m % 2
                    take(b)
                    for r in range(2):
                        mm = nc.tensor.matmul(bank[b][:, :], w_ukv[:, 0, r, m * P:(m + 1) * P], ckvT[:, r, :],
                                              start=(r == 0), stop=(r == 1))
                    mm.then_inc(psum_full[b], 1)
                for m in range(KD):
                    tt, c = m // 2, m % 2
                    b = 6 + m % 2
                    take(b)
                    for r in range(2):
                        mm = nc.tensor.matmul(bank[b][:, :], ckvT[:, r, tt * P:(tt + 1) * P],
                                              w_ukv[:, 1, r, c * T:(c + 1) * T], start=(r == 0), stop=(r == 1))
                    mm.then_inc(psum_full[b], 1)
                mark("heads")
                per = {0: 2, 1: 2, 2: 2, 3: 2, 4: 4, 5: 4, 6: 1, 7: 1, "pair": 1, "prob": 8, "probT": 8}
                with t.loop(HEADS // 2, per) as hp:
                    n0 = t.turn("pair")
                    pe.wait_ge(sem("qk_pair_ready"), n0 * 2 + 2)

                    def logits(n):
                        a, tt = n // TT, n % TT
                        r, b = HD * a, n % 4
                        take(b)
                        nc.tensor.matmul(bank[b][:, 0:(tt + 1) * P], q_pair[r:r + HD, tt * P:(tt + 1) * P],
                                         k_pair[r:r + HD, 0:(tt + 1) * P],
                                         start=True, stop=True).then_inc(psum_full[b], 1)

                    def turn_probs(n):
                        tt, b = n % TT, 4 + n % 2
                        pe.wait_ge(sem("prob_ready"), t.turn("prob") + 1)
                        take(b)
                        for st in range(tt + 1):
                            mm = nc.tensor.transpose(bank[b][:, st * P:(st + 1) * P], prob[:, n % 4, st * P:(st + 1) * P],
                                                     ident[:, :])
                        mm.then_inc(psum_full[b], 1)

                    def outputs(a):
                        r, b = HD * a, 6 + a
                        pe.wait_ge(sem("v_pair_ready"), n0 + 1)
                        pe.wait_ge(sem("probT_ready"), t.turn("probT", 4) + 4)
                        take(b)
                        for st in range(TT):
                            mm = nc.tensor.matmul(bank[b][r:r + HD, st * P:], v_pair[:, st, r:r + HD],
                                                  probT[:, a, st, st * P:], start=(st == 0), stop=(st == TT - 1))
                        mm.then_inc(psum_full[b], 1)

                    for n in range(8):
                        logits(n)
                        if n >= 3:
                            turn_probs(n - 3)
                        if n - 3 == 4:
                            outputs(0)
                    for n in range(5, 8):
                        turn_probs(n)
                    outputs(1)
                mark("attn_out")
                pe.wait_ge(sem("oT_ready"), HEADS)
                with t.loop(KD // 2, {"w0": 1, "w1": 1, 0: 1, 1: 1}):
                    tile_product(0, oT)
                    tile_product(1, oT)

            def peer(l):
                mark(f"router{l}")
                pe.wait_ge(sem("h_ready"), t.turn("h_ready") + 1)
                with t.loop(PM // 2, {"w0": 1, "w1": 1, 0: 1, 1: 1, 2: 1, 3: 1, "keys0": 1, "keys1": 1}):
                    for s in range(2):
                        tile_product(s, hT)
                    for s in range(2):
                        pe.wait_ge(psum_free[s], t.now(s))
                        pe.wait_ge(sem(f"keys_loaded{s}"), t.turn(f"keys{s}") * 16 + 16)
                        take(2 + s)
                        for tt in range(TT):
                            mm = nc.tensor.matmul(bank[2 + s][:, tt * NK:(tt + 1) * NK], qm[:, s, tt * P:(tt + 1) * P],
                                                  keys[:, s, :], start=True, stop=True)
                        mm.then_inc(psum_full[2 + s], 1)
                pe.wait_ge(sem("choices_ready"), l + 1)
                for n, src in enumerate((TS[:, :, :, :].rearrange("p t h k -> p (t h k)"), Ef[:, 0, :], Ef[:, 1, :])):
                    take(4 + n)
                    for tt in range(TT):
                        mm = nc.tensor.transpose(bank[4 + n][:, tt * P:(tt + 1) * P], src[:, tt * P:(tt + 1) * P], ident[:, :])
                    mm.then_inc(psum_full[4 + n], 1)
                mark(f"gates{l}")
                with t.loop(2, {2: 32, 3: 32, "oh2": 64}):
                    for _ in range(2):
                        with t.loop(16, {2: 1, 3: 1, "oh2": 2}):
                            for a in range(2):
                                pe.wait_ge(sem("oh2_ready"), t.turn("oh2") + 1)
                                take(2 + a)
                                for j in range(4):
                                    for q in range(3):
                                        mm = nc.tensor.matmul(bank[2 + a][:, j * NK:(j + 1) * NK], oh1[:, a, j, :],
                                                              oh2[:, a, j, q, :], start=(q == 0), stop=(q == 2))
                                mm.then_inc(psum_full[2 + a], 1)
                mark(f"experts{l}")
                pe.wait_ge(sem("hx_ready"), l + 1)

                def three(b, hi, lo, rhi, rlo, first, last):
                    nc.tensor.matmul(bank[b][:, :], hi, rhi, start=first, stop=False)
                    nc.tensor.matmul(bank[b][:, :], hi, rlo, start=False, stop=False)
                    return nc.tensor.matmul(bank[b][:, :], lo, rhi, start=False, stop=last)

                def up(s):
                    pe.wait_ge(sem(f"split_done{s}"), t.turn(f"split{s}") + 2)
                    take(s)
                    for k in range(KD):
                        mm = three(s, hl[:, s, 0, k, :], hl[:, s, 1, k, :], hx[:, 0, k, :], hx[:, 1, k, :],
                                   k == 0, k == KD - 1)
                    mm.then_inc(psum_full[s], 1)

                def down(s, par, j):
                    if j == 0:
                        pe.wait_ge(sem("w_ready"), t.turn("group", GT) + GT)
                    pe.wait_ge(sem(f"split_done{s}"), t.turn(f"split{s}") + 2)
                    take(s)
                    for k in range(GT):
                        mm = three(s, hl[:, s, 0, k, :], hl[:, s, 1, k, :], W[:, par, 0, k, :], W[:, par, 1, k, :],
                                   k == 0, k == GT - 1)
                    mm.then_inc(psum_full[s], 1)

                def phase(par):
                    for j in range(GT):
                        up(2 * j % 4)
                        down((2 * j + 1) % 4, 1 - par, j)

                for j in range(GT):
                    up(2 * j % 4)
                per = {k: 8 for k in (0, 1, 2, 3, "split0", "split1", "split2", "split3")}
                with t.loop(NG // 2 - 1, per | {"group": 2 * GT}):
                    phase(1)
                    phase(0)
                phase(1)
                for j in range(GT):
                    down((2 * j + 1) % 4, 1, j)

            def deltanet():
                mark("gdn")
                pe.wait_ge(sem("h_ready"), t.turn("h_ready") + 1)
                slot_ready(0)
                take(0)
                for tt in range(TT):
                    for k in range(KD):
                        mm = nc.tensor.matmul(bank[0][:, tt * 2 * VH:(tt + 1) * 2 * VH], hT[:, k, tt * P:(tt + 1) * P],
                                              w_ring[:, 0, k, 0:2 * VH], start=(k == 0), stop=(k == KD - 1))
                mm.then_inc(psum_full[0], 1)
                pe.wait_ge(sem("graw_ready"), 1)
                pe.wait_ge(sem("gdn_masks"), 3)
                g_all = graw.rearrange("p t h -> p (t h)")
                n = TT * VH
                take(2)
                nc.tensor.matmul(bank[2][:, 0:n], tri[:, :], g_all, start=True, stop=True)
                nc.tensor.matmul(bank[2][:, n:2 * n], samec[:, :], g_all, start=True, stop=True).then_inc(psum_full[2], 1)
                take(3)
                nc.tensor.matmul(bank[3][:, 0:n], ones[0:CHUNK, :], g_all[0:CHUNK, :], start=True, stop=True
                                 ).then_inc(psum_full[3], 1)
                take(4)
                nc.tensor.matmul(bank[4][:, 0:n], ones[CHUNK:P, :], g_all[CHUNK:P, :], start=True, stop=True
                                 ).then_inc(psum_full[4], 1)
                mark("gdn_heads")
                per = {"w0": 2, "w1": 2, 0: 2, 1: 2, 2: 2, 3: 2, 4: 3, 5: 4, 6: 1, 7: 1, "gsel": 1, "gsq": 2, "qk": 1,
                       "ktok": 1, "vs": 2}
                with t.loop(KH, per):
                    tile_product(0, hT)
                    tile_product(1, hT)
                    tile_product(0, hT)
                    for q in range(2):
                        pe.wait_ge(sem("gdn_squares"), t.turn("gsq") + 1)
                        take(5)
                        nc.tensor.matmul(bank[5][:, :], ones[:, :], sq[:, q, :], start=True, stop=True
                                         ).then_inc(psum_full[5], 1)
                    tile_product(1, hT)
                    pe.wait_ge(sem("gsel_ready"), t.turn("gsel") * 3 + 3)
                    for a in range(2):
                        take(2)
                        nc.tensor.matmul(bank[2][:, :], tri[:, :], SG[:, a, :, :].rearrange("p t c -> p (t c)"),
                                         start=True, stop=True).then_inc(psum_full[2], 1)
                        take(3)
                        for tt in range(TT):
                            mm = nc.tensor.matmul(bank[3][:, tt * P:(tt + 1) * P], SG[:, a, tt, :], tri[:, :],
                                                  start=True, stop=True)
                        mm.then_inc(psum_full[3], 1)
                        take(4)
                        for tt in range(TT):
                            mm = nc.tensor.matmul(bank[4][:, tt * P:(tt + 1) * P],
                                                  gsel[:, tt, a:a + 1].to_broadcast([P, P]), tri[:, :],
                                                  start=True, stop=True)
                        mm.then_inc(psum_full[4], 1)
                    pe.wait_ge(sem("qk_ready"), t.turn("qk") * 2 + 2)
                    for b, rhs in ((6, 1), (7, 0)):
                        take(b)
                        for tt in range(TT):
                            c = slice(tt * P, (tt + 1) * P)
                            mm = nc.tensor.matmul(bank[b][:, c], cy[:, 1, c], cy[:, rhs, c], start=True, stop=True)
                        mm.then_inc(psum_full[b], 1)
                    take(4)
                    for tt in range(TT):
                        mm = nc.tensor.transpose(bank[4][:, tt * P:(tt + 1) * P], cy[:, 1, tt * P:(tt + 1) * P], ident[:, :])
                    mm.then_inc(psum_full[4], 1)
                    t.turn("ktok")
                    for a in range(2):
                        pe.wait_ge(sem("v_silu"), t.turn("vs") + 1)
                        take(5)
                        for tt in range(TT):
                            mm = nc.tensor.transpose(bank[5][:, tt * P:(tt + 1) * P], cy[:, 2 + a, tt * P:(tt + 1) * P],
                                                     ident[:, :])
                        mm.then_inc(psum_full[5], 1)
                mark("gdn_groups")
                per = {"w0": 2, "w1": 2, 0: 2, 1: 2, 2: 14, 3: 8, 4: 14, 5: 4, 6: 4, 7: 4, "grp": 1, "S": 9}
                with t.loop(VH // 4, per):
                    g0 = t.turn("grp")
                    pe.wait_ge(sem("Pb_loaded"), g0 * 256 + 256)
                    pe.wait_ge(sem("Eb_loaded"), g0 * 128 + 128)
                    pe.wait_ge(sem("vkb_loaded"), g0 * 16 + 16)

                    def four(b, left, right, is_t=False):
                        take(b)
                        for tt in range(TT):
                            c = slice(tt * P, (tt + 1) * P)
                            if is_t:
                                mm = nc.tensor.transpose(bank[b][:, c], left(tt), right(tt))
                            else:
                                mm = nc.tensor.matmul(bank[b][:, c], left(tt), right(tt), start=True, stop=True)
                        mm.then_inc(psum_full[b], 1)

                    def turned(a):
                        four(5, lambda tt: Pb[:, a, tt, :], lambda tt: ident[:, :], True)

                    turned(0)
                    for a in range(4):
                        if a < 3:
                            turned(a + 1)
                        pe.wait_ge(psum_free[5], t.now(5) - (1 if a < 3 else 0))
                        four(6, lambda tt: Eb[:, a, tt, :], lambda tt: Qs[:, a, tt, :])
                        pe.wait_ge(psum_free[6], t.now(6))
                        four(4, lambda tt: Pb[:, a, tt, :], lambda tt: Ys[:, a % 2, tt, :])
                    for a in range(4):
                        pe.wait_ge(psum_free[4], t.now(4) - (3 - a))
                        four(2, lambda tt: Qs[:, a, tt, :], lambda tt: vkb[:, a, 0, tt * P:(tt + 1) * P])
                        four(7, lambda tt: vkb[:, a, 1, tt * P:(tt + 1) * P], lambda tt: Qs[:, a, tt, :])
                    pe.wait_ge(psum_free[7], t.now(7))
                    pe.wait_ge(sem("kqa_loaded"), g0 * 16 + 16)
                    for n in range(NCH):
                        r, tt, s = CHUNK * (n % 2), n // 2, n % 2
                        rows = slice(r, r + CHUNK)
                        tok = slice(n * CHUNK, (n + 1) * CHUNK)
                        pe.wait_ge(sem("state_ready"), t.turn("S") + 1)
                        take(2)
                        for a in range(4):
                            mm = nc.tensor.matmul(bank[2][rows, a * P:(a + 1) * P], wTs[:, a, tok], S[:, s, a, :],
                                                  start=True, stop=True)
                        mm.then_inc(psum_full[2], 1)
                        z = n // 2 % 2
                        if n % 2 == 0:
                            slot_ready(z)
                            take(z)
                        for k in range(4 * (n % 2), 4 * (n % 2) + 4):
                            mm = nc.tensor.matmul(bank[z][:, :], w_ring[:, z, k, :], hT[:, k, :],
                                                  start=(k == 0), stop=(k == KD - 1))
                        if n % 2:
                            mm.then_inc(psum_full[z], 1)
                        pe.wait_ge(psum_free[2], t.now(2))
                        take(4)
                        for a in range(4):
                            mm = nc.tensor.matmul(bank[4][:, a * P:(a + 1) * P], kqa[rows, a, 0, tt * P:(tt + 1) * P],
                                                  vn[rows, a, :], start=True, stop=True)
                        mm.then_inc(psum_full[4], 1)
                        take(3)
                        for a in range(4):
                            nc.tensor.matmul(bank[3][:, a * CHUNK:(a + 1) * CHUNK], S[:, s, a, :], kqa[:, a, 1, tok],
                                             start=True, stop=False)
                            mm = nc.tensor.matmul(bank[3][:, a * CHUNK:(a + 1) * CHUNK], vn[rows, a, :],
                                                  kqa[rows, a, 2, tt * P + r:tt * P + r + CHUNK], start=False, stop=True)
                        mm.then_inc(psum_full[3], 1)
                    t.turn("S")
                    pe.wait_ge(sem("o_squares"), g0 + 1)
                    for a in range(4):
                        b = 2 + 2 * (a % 2)
                        take(b)
                        nc.tensor.matmul(bank[b][:, :], ones[:, :], o2[:, a, :], start=True, stop=True
                                         ).then_inc(psum_full[b], 1)
                mark("gdn_out")
                pe.wait_ge(sem("OT_ready"), VH + 1)
                with t.loop(KD, {"w0": 1, "w1": 1, 0: 1, 1: 1}):
                    tile_product(0, OT[:, 0:KD, :])
                    tile_product(1, OT[:, KD:VH, :])

            modulations()
            norm("norm0")
            if stop > 0:
                attention()
            if stop > 1:
                norm("norm1")
                peer(0)
            if stop > 2:
                norm("norm2")
                deltanet()
            if stop > 3:
                norm("norm3")
                peer(1)
                norm("norm4")

        @block.sync
        def _(sp):
            t = Tally(sp)
            for name, turn in FREE_AT_START.items():
                sp.sem_inc(sem(name), turn)

            def load(s, src, wait=True, cols=P):
                n = t.turn(f"w{s}")
                sp.wait_ge(psum_full[s], n + w_base[s])
                sp.dma_start(w_ring[:, s, :, 0:cols], src).then_inc(sem(f"w_loaded{s}"), 16)

            w_base = [12, 12]

            def tile_of(w, m0, cols=P):
                return w[:, m0:m0 + cols].rearrange("(k p) c -> p k c", p=P)

            def tile_at(w, i, first=0):
                return w[:, ds(i * P + first, P)].rearrange("(k p) c -> p k c", p=P)

            sp.dma_start(condT[:, :], c_t).then_inc(sem("c_loaded"), 16)
            sp.dma_start(adab[:, :, :], ada_b).then_inc(sem("adab_loaded"), 16)
            for n in range(24):
                l, j, s = n // 12, n % 12, n % 2
                if n >= 2:
                    sp.wait_ge(psum_full[s], n // 2)
                sp.dma_start(ada_ring[:, s, :, :], ada_w[l, :, j * T:(j + 1) * T].rearrange("(k p) c -> p k c", p=P)
                             ).then_inc(sem(f"ada_loaded{s}"), 16)
                if n == 1:
                    sp.dma_start(xT[:, :, :], x_t.rearrange("(k p) t -> p k t", p=P)).then_inc(sem("x_loaded"), 16)
                    sp.dma_start(fnorm[:, :], final_norm).then_inc(sem("fnorm_loaded"), 16)
                    sp.dma_start(kvn[:, :], a_kv_norm).then_inc(sem("kvn_loaded"), 16)
            sp.wait_ge(sem("ada_rows"), 24)
            sp.dma_start(ada_dram.rearrange("(a r) c -> a (r c)", a=1), ada_row[:, :, :].rearrange("a l c -> a (l c)")
                         ).then_inc(sem("ada_stored"), 16)
            sp.wait_ge(sem("ada_stored"), 16)
            sp.dma_start(ada_sq[:, :], ada_dram).then_inc(sem("ada_square"), 16)

            def attention():
                load(0, tile_of(a_w_in, C_KV))
                load(1, tile_of(a_w_in, C_KV + P))
                n = t.turn("w0")
                sp.wait_ge(psum_full[0], n + w_base[0])
                kcols = a_w_in[:, C_KI:C_KI + ID].rearrange("(k p) c -> p k c", p=P)
                sp.dma_start(w_ring[:, 0, :, 0:ID], kcols).then_inc(sem("kidx_half"), 16)
                sp.dma_start(w_ring[:, 0, :, ID:P], kcols).then_inc(sem("w_loaded0"), 16)
                load(1, tile_of(a_w_in, C_WI, IH), cols=IH)
                for m in range(4):
                    load(m % 2, tile_of(a_w_in, C_QI + m * P))
                sp.dma_start(w_ukv[:, 0, :, :], a_w_uk.rearrange("(r p) c -> p r c", p=P)).then_inc(sem("ukv_loaded"), 16)
                sp.dma_start(w_ukv[:, 1, :, :], a_w_uv.rearrange("(r p) c -> p r c", p=P)).then_inc(sem("ukv_loaded"), 16)
                with t.loop(KD // 2, {"w0": 1, "w1": 1}) as i:
                    for s in range(2):
                        load(s, a_w_in[:, ds(i * 2 * P + s * P, P)].rearrange("(k p) c -> p k c", p=P))
                for s in range(2):
                    w_base[s] += HEADS
                with t.loop(KD // 2, {"w0": 1, "w1": 1}) as i:
                    for s in range(2):
                        load(s, a_w_out[:, ds(i * 2 * P + s * P, P)].rearrange("(k p) c -> p k c", p=P))

            def peer(l):
                for s in range(2):
                    w_base[s] = marks[f"router{l}"][s] - t.n[f"w{s}"]
                sp.wait_ge(sem("x_ready"), 2 * l + 1)
                with t.loop(PM // 2, {"w0": 1, "w1": 1, "keys0": 1, "keys1": 1}) as i:
                    for s in range(2):
                        load(s, p_w_q[l, :, ds(i * 2 * P + s * P, P)].rearrange("(k p) c -> p k c", p=P))
                        n = t.turn(f"keys{s}")
                        sp.wait_ge(psum_full[2 + s], n + marks[f"router{l}"].get(2 + s, 0) - l * PM // 2)
                        sp.dma_start(keys[:, s, :], p_keys_t[l, ds(i * 2 + s, 1)].rearrange("m c k -> c (m k)")
                                     ).then_inc(sem(f"keys_loaded{s}"), 16)
                gates = g_dram.rearrange("b a t -> a b t")
                with t.loop(2, {"gst": 2}) as i:
                    for par in range(2):
                        sp.wait_ge(sem("gst_ready"), t.turn("gst") + 1)
                        sp.dma_start(gates[:, :, ds(i * 2 * P + par * P, P)], gst[:, par, :, :]
                                     ).then_inc(sem(f"gst_stored{par}"), 16)
                for par in range(2):
                    sp.wait_ge(sem(f"gst_stored{par}"), 32 * (l + 1) + 16)
                def load_up(s, j, first):
                    tile = ds(first + j, 1)
                    sp.wait_ge(sem(f"split_done{s}"), t.turn(f"raw{s}") + 1)
                    sp.dma_start(raw[:, s, :, :], p_u_t[l, tile].rearrange("a p k c -> (a p) k c")
                                 ).then_inc(sem(f"raw_loaded{s}"), 16)
                    sp.wait_ge(sem(f"gt_used{j % 4}"), t.turn(f"gt{j % 4}"))
                    sp.dma_start(gt[:, j % 4, :], g_dram[tile].rearrange("a p t -> (a p) t")
                                 ).then_inc(sem(f"gt_loaded{j % 4}"), 16)

                def load_down(s, j, first):
                    sp.wait_ge(sem(f"split_done{s}"), t.turn(f"raw{s}") + 1)
                    sp.dma_start(raw[:, s, :, :], p_v[l][:, ds(first, GT), j * P:(j + 1) * P]
                                 ).then_inc(sem(f"raw_loaded{s}"), 16)

                def phase(up_first, down_first):
                    for j in range(GT):
                        load_up(2 * j % 4, j, up_first)
                        load_down((2 * j + 1) % 4, j, down_first)

                for j in range(GT):
                    load_up(2 * j % 4, j, 0)
                per = {k: 8 for k in ("raw0", "raw1", "raw2", "raw3")} | {k: 4 for k in ("gt0", "gt1", "gt2", "gt3")}
                with t.loop(NG // 2 - 1, per) as i:
                    phase(i * 2 * GT + GT, i * 2 * GT)
                    phase(i * 2 * GT + 2 * GT, i * 2 * GT + GT)
                phase(NK - GT, NK - 2 * GT)
                for j in range(GT):
                    load_down((2 * j + 1) % 4, j, NK - GT)

            def deltanet():
                for s in range(2):
                    w_base[s] = marks["gdn"][s] - t.n[f"w{s}"]
                sp.wait_ge(sem("x_ready"), 2)
                load(0, tile_of(b_w_in, C_BETA, 2 * VH), cols=2 * VH)
                sp.dma_start(alog[:, :], b_a_log.partition_broadcast(P).rearrange("p a h -> p (a h)")
                             ).then_inc(sem("gdn_params"), 16)
                sp.dma_start(dtb[:, :], b_dt_bias.partition_broadcast(P).rearrange("p a h -> p (a h)")
                             ).then_inc(sem("gdn_params"), 16)
                sp.dma_start(convw[:, :, :], b_conv).then_inc(sem("gdn_params"), 16)
                sp.dma_start(onorm[:, :], b_out_norm).then_inc(sem("gdn_params"), 16)
                with t.loop(KH, {"w0": 2, "w1": 2, "packs": 2}) as i:
                    def store(a):
                        n = t.turn("packs")
                        head = ds(i * 2 + a, 1)
                        sp.wait_ge(sem("amat_ready"), n + 2)
                        for half in range(2):
                            rows = slice(half * CHUNK, (half + 1) * CHUNK)
                            sp.dma_start(a_dram[head].rearrange("a (t u) c s -> u c (a t) s", u=2)[half],
                                         amat[rows, a, :, half * CHUNK:(half + 1) * CHUNK]
                                         ).then_inc(sem(f"amat_stored{a}"), 16)
                        sp.wait_ge(sem("pack_v"), n + 1)
                        sp.wait_ge(sem("pack_ready"), n * 4 + 5)
                        sp.dma_start(pack_dram[head].rearrange("a p f t -> p (a f) t"), pack[:, a, :, :]
                                     ).then_inc(sem(f"pack_stored{a}"), 16)

                    load(0, b_w_in[:, ds(i * P, P)].rearrange("(k p) c -> p k c", p=P))
                    load(1, b_w_in[:, ds(i * P + KH * BD, P)].rearrange("(k p) c -> p k c", p=P))
                    load(0, b_w_in[:, ds(i * 2 * P + 2 * KH * BD, P)].rearrange("(k p) c -> p k c", p=P))
                    load(1, b_w_in[:, ds(i * 2 * P + 2 * KH * BD + P, P)].rearrange("(k p) c -> p k c", p=P))
                    store(0)
                    store(1)
                for a in range(2):
                    sp.wait_ge(sem(f"amat_stored{a}"), 32 * KH + 16)
                    sp.wait_ge(sem(f"pack_stored{a}"), 16 * KH + 16)
                for q in range(2):
                    c = slice(q * HB, (q + 1) * HB)
                    sp.dma_start(SA[:, q, :, :], a_dram.rearrange("h n c s -> (h n) c s")[:, c, c]).then_inc(sem("SA_loaded"), 16)
                sp.wait_ge(sem("X_ready"), 1)
                sp.dma_start(t_dram, X[:, :, :, :]).then_inc(sem("X_stored"), 16)
                sp.wait_ge(sem("X_stored"), 16)
                sp.wait_ge(sem("blocks_zero"), 2)
                T_v = t_dram.rearrange("(h t u) q i j -> u q i h t j", u=2, t=TT)
                E_v = a_dram.rearrange("h (t u) c s -> u c h t s", u=2)
                pv = pack_dram.rearrange("h p f t -> p h f t")
                with t.loop(VH // 4, {"w0": 2, "w1": 2, "grp": 1}) as i:
                    g0 = t.turn("grp")
                    hs = ds(i * 4, 4)
                    sp.wait_ge(psum_full[7], g0 * 4 + marks["gdn_groups"][7])
                    for half in range(2):
                        for q in range(2):
                            r = half * CHUNK + q * HB
                            for a in range(4):
                                sp.dma_start(Pb[r:r + HB, a, :, r:r + HB],
                                             T_v[half, q][:, ds(i * 4 + a, 1)].rearrange("i a t j -> i (a t) j")
                                             ).then_inc(sem("Pb_loaded"), 16)
                    for half in range(2):
                        r = half * CHUNK
                        for a in range(4):
                            sp.dma_start(Eb[r + HB:r + 2 * HB, a, :, r:r + HB],
                                         E_v[half][HB:, ds(i * 4 + a, 1), :, 0:HB].rearrange("c a t s -> c (a t) s")
                                         ).then_inc(sem("Eb_loaded"), 16)
                    sp.dma_start(vkb[:, :, :, :], pv[:, hs, 0:2, :]).then_inc(sem("vkb_loaded"), 16)
                    sp.wait_ge(psum_full[3], g0 * NCH + marks["gdn_groups"][3])
                    sp.dma_start(kqa[:, :, :, :], pv[:, hs, 2:5, :]).then_inc(sem("kqa_loaded"), 16)
                    for a in range(4):
                        load(a % 2, b_w_in[:, ds(i * 4 * P + a * P + 2 * KH * BD + VH * BD, P)
                                           ].rearrange("(k p) c -> p k c", p=P))
                with t.loop(KD, {"w0": 1, "w1": 1}) as i:
                    for s in range(2):
                        load(s, b_w_out[s * D:(s + 1) * D, ds(i * P, P)].rearrange("(k p) c -> p k c", p=P))

            if stop > 0:
                attention()
            if stop > 1:
                peer(0)
            if stop > 2:
                deltanet()
            if stop > 3:
                peer(1)
                sp.wait_ge(sem("h_ready"), 5)
                sp.dma_start(out_t.rearrange("(k p) t -> p k t", p=P), hT[:, :, :]).then_inc(sem("out_stored"), 16)
                sp.wait_ge(sem("out_stored"), 16)

        @block.gpsimd
        def _(pool):
            nc.gpsimd.memset(ones[:, :], 1.0).then_inc(sem("consts"), 1)
            nc.gpsimd.memset(ident[:, :], 0.0).then_inc(sem("ident_zero"), 1)
            pool.wait_ge(sem("ident_zero"), 1)
            nc.gpsimd.affine_select(out=ident[:, :], in_=ident[:, :], compare_op=ALU.not_equal, fill=1.0, base=0,
                                    pattern=[[-1, P]], channel_multiplier=1).then_inc(sem("consts"), 1)
            nc.gpsimd.iota(iota_i[:, :], [[1, P]], base=0, channel_multiplier=0).then_inc(sem("iota_int"), 1)
            pool.wait_ge(sem("iota_int"), 1)
            nc.gpsimd.tensor_copy(iota[:, :], iota_i[:, :]).then_inc(sem("iota_ready"), 1)
            nc.gpsimd.tensor_copy(iota_b[:, :], iota_i[:, :]).then_inc(sem("iota_ready"), 1)
            pool.wait_ge(sem("mods_ready"), 1)
            nc.gpsimd.memset(maskb[:, 0, 0:P], 0.0).then_inc(sem("mask_zero"), 1)
            pool.wait_ge(sem("mask_zero"), 1)
            nc.gpsimd.memset(maskb[0:CHUNK, 0, CHUNK:P], NEG).then_inc(sem("mask_first"), 1)

            t = Tally(pool)

            def attention():
                t.n.update(marks["heads"])
                pool.wait_ge(sem("qkv_ready"), 1)
                with t.loop(HEADS // 2, {3: 2, "v": 1}) as hp:
                    pool.wait_ge(psum_full[3], t.turn(3, 2))
                    nc.gpsimd.tensor_copy(q_pair[:, :], qT[:, ds(hp, 1), :]).then_inc(sem("qk_pair_ready"), 1)
                    nc.gpsimd.tensor_copy(k_pair[:, :], kT[:, ds(hp, 1), :]).then_inc(sem("qk_pair_ready"), 1)
                    pool.wait_ge(psum_full[7], t.turn("v") + marks["heads"][7])
                    nc.gpsimd.tensor_copy(v_pair[:, :, :], vA[:, :, ds(hp * P, P)]).then_inc(sem("v_pair_ready"), 1)

            def step(ins):
                ins.then_inc(sem("pool_step"), 1)
                pool.wait_ge(sem("pool_step"), t.turn("pool_step") + 1)

            def candidates(out, src, sem_name):
                one = src[:, :, :, :].rearrange("p t (h q) k -> p (t h) q k", q=2)
                off = 0
                for a in range(TOPK // 2):
                    n = ROWS[a]
                    nc.gpsimd.tensor_tensor(out[:, :, off:off + n], one[:, :, 0, a:a + 1].to_broadcast([P, TT * PH, n]),
                                            one[:, :, 1, 0:n], ALU.add)
                    off += n
                nc.gpsimd.tensor_tensor(out[:, :, off:NC_], one[:, :, 0, TOPK // 2:TOPK],
                                        one[:, :, 1, 0:1].to_broadcast([P, TT * PH, TOPK // 2]), ALU.add
                                        ).then_inc(sem(sem_name), 1)

            def peer(l):
                pool.wait_ge(sem("x_ready"), 2 * l + 1)
                step(nc.gpsimd.iota(iotac_i[:, :], [[1, NC_]], base=0, channel_multiplier=0))
                nc.gpsimd.tensor_copy(iotac[:, :], iotac_i[:, :]).then_inc(sem("iotac_ready"), 1)
                pool.wait_ge(sem("codes_ready"), l + 1)
                candidates(code, I, "code_ready")
                with t.loop(2, {"eq": 2}) as i:
                    for e in range(2):
                        pool.wait_ge(sem("eq_ready"), t.turn("eq") + 1)
                        nc.gpsimd.tensor_tensor(eq[:, e, :, :, :], eq[:, e, :, :, :],
                                                code[:, ds(i * 2 * PH + e * PH, PH), :].unsqueeze(2).to_broadcast(
                                                    [P, PH, TOPK, NC_]), ALU.mult).then_inc(sem("picked"), 1)

            def deltanet():
                pool.wait_ge(sem("x_ready"), 2)
                for m in (tri, strict, samec):
                    ins = nc.gpsimd.memset(m[:, :], 1.0)
                step(ins)
                step(nc.gpsimd.affine_select(out=tri[:, :], in_=tri[:, :], compare_op=ALU.is_ge, fill=0.0, base=0,
                                             pattern=[[1, P]], channel_multiplier=-1))
                step(nc.gpsimd.affine_select(out=strict[:, :], in_=strict[:, :], compare_op=ALU.is_gt, fill=0.0, base=0,
                                             pattern=[[-1, P]], channel_multiplier=1))
                step(nc.gpsimd.memset(samec[0:CHUNK, CHUNK:P], 0.0))
                step(nc.gpsimd.memset(samec[CHUNK:P, 0:CHUNK], 0.0))
                step(nc.gpsimd.memset(tri[0:CHUNK, CHUNK:P], 0.0))
                step(nc.gpsimd.memset(strict[CHUNK:P, 0:CHUNK], 0.0))
                pool.sem_inc(sem("gdn_masks"), 3)
                nc.gpsimd.memset(xs[:, :, 0:3], 0.0).then_inc(sem("xs_pad"), 1)
                pool.wait_ge(sem("gdn_masks"), 3)
                pool.wait_ge(sem("gstat_ready"), 1)
                t.n.update(marks["gdn_heads"])
                per = {3: 2, 4: 3, "gsq": 1, "kt": 1, "at": 2, "stored0": 1, "stored1": 1, "BS": 1}
                wide = [P, TT, P]

                with t.loop(KH, per) as i:
                    def column(of, a):
                        return of[:, :, ds(i * 2 + a, 1)].to_broadcast(wide)

                    pool.wait_ge(psum_full[3], t.turn(3, 2))
                    pool.wait_ge(psum_full[4], t.now(4))
                    nc.gpsimd.tensor_copy(gsel[:, :, :], graw[:, :, ds(i * 2, 2)]).then_inc(sem("gsel_ready"), 1)
                    for a in range(2):
                        nc.gpsimd.tensor_tensor(SG[:, a, :, :], strict[:, :].unsqueeze(1).to_broadcast(wide),
                                                column(graw, a), ALU.mult).then_inc(sem("gsel_ready"), 1)
                    pool.wait_ge(sem("amat_ready"), t.turn("BS") * 2 + 1)
                    for a in range(2):
                        nc.gpsimd.tensor_tensor(BS[:, a, :, :], strict[:, :].unsqueeze(1).to_broadcast(wide),
                                                column(beta, a), ALU.mult).then_inc(sem("BS_ready"), 1)
                    pool.wait_ge(sem("ktok_ready"), t.turn("kt") + 1)
                    for a in range(2):
                        pool.wait_ge(sem(f"pack_stored{a}"), t.turn(f"stored{a}") * 16 + 16)
                        for f, by in ((1, bege), (2, ekd)):
                            nc.gpsimd.tensor_tensor(pack[:, a, f, :].rearrange("p (t c) -> p t c", c=P), ktok[:, :, :],
                                                    column(by, a), ALU.mult).then_inc(sem("pack_ready"), 1)
                        nc.gpsimd.tensor_tensor(pack[:, a, 3, :], cy[:, 0, :], eG[:, a, :], ALU.mult
                                                ).then_inc(sem("pack_ready"), 1)
                        pool.wait_ge(sem("attn_raw"), t.turn("at") + 2)
                        at = pack[:, a, 4, :].rearrange("p (t c) -> p t c", c=P)
                        nc.gpsimd.tensor_tensor(at, at, tri[:, :].unsqueeze(1).to_broadcast(wide), ALU.mult
                                                ).then_inc(sem("pack_ready"), 1)
                    t.turn(4, 3), t.turn("gsq")
                for a in range(2):
                    pool.wait_ge(sem(f"pack_stored{a}"), 16 * KH + 16)
                    pool.wait_ge(sem(f"amat_stored{a}"), 32 * KH + 16)
                pool.wait_ge(sem("X_stored"), 16)
                nc.gpsimd.memset(Eb[:, :, :, :], 0.0).then_inc(sem("blocks_zero"), 1)
                nc.gpsimd.memset(Pb[:, :, :, :], 0.0).then_inc(sem("blocks_zero"), 1)

            if stop > 0:
                attention()
            if stop > 1:
                peer(0)
            if stop > 2:
                deltanet()
            if stop > 3:
                peer(1)

        @block.scalar
        def _(act):
            t = Tally(act)

            def sync(stage):
                t.n.update(marks[stage])

            def full(b):
                act.wait_ge(psum_full[b], t.turn(b) + 1)

            def step(ins):
                ins.then_inc(sem("act_step"), 1)
                act.wait_ge(sem("act_step"), t.turn("act_step") + 1)

            def modulations():
                sync("mod")
                act.wait_ge(sem("c_loaded"), 16)
                nc.scalar.activation(condT[:, :], condT[:, :], ACT.Silu).then_inc(sem("cond_ready"), 1)
                for n in range(24):
                    l, j, s = n // 12, n % 12, n % 2
                    full(s)
                    nc.scalar.activation(ada_row[0:1, l, j * T:(j + 1) * T], bank[s][0:1, :], ACT.Copy
                                         ).then_inc(psum_free[s], 1)
                act.wait_ge(psum_free[1], 12)
                act.sem_inc(sem("ada_rows"), 24)

            def norm(stage, gain=None, l=0, sh=0, sc=0):
                sync(stage)
                nc.scalar.activation(hT[:, :, :], xT[:, :, :], ACT.Square).then_inc(sem("squares"), 1)
                act.wait_ge(sem("var_ready"), t.turn("var") + 1)
                nc.scalar.activation(rstd[:, :], rstd[:, :], ACT.Sqrt).then_inc(sem("std_ready"), 1)
                act.wait_ge(sem("hn_ready"), t.turn("hn") + 1)
                for k in range(KD):
                    if gain is None:
                        ins = nc.scalar.activation(hT[:, k, :], hT[:, k, :], ACT.Identity,
                                                   bias=mods[:, l, sh + k:sh + k + 1], scale=mods[:, l, sc + k:sc + k + 1])
                    else:
                        ins = nc.scalar.activation(hT[:, k, :], hT[:, k, :], ACT.Copy, scale=gain[:, k:k + 1])
                ins.then_inc(sem("h_ready"), 1)

            def evac(b, dst, src=None, func=ACT.Copy):
                full(b)
                nc.scalar.activation(dst, bank[b][:, :] if src is None else src, func).then_inc(psum_free[b], 1)

            def attention():
                sync("attn")
                evac(0, ckvT[:, 0, :])
                evac(1, ckvT[:, 1, :])
                act.wait_ge(psum_free[0], t.now(0))
                act.wait_ge(psum_free[1], t.now(1))
                nc.scalar.activation(ckv_sq[:, :, :], ckvT[:, :, :], ACT.Square).then_inc(sem("ckv_squares"), 1)
                full(0)
                nc.scalar.activation(kidxT[:, :], bank[0][:, :], ACT.Copy).then_inc(sem("idx_ready"), 1)
                act.wait_ge(sem("idx_ready"), 1)
                act.sem_inc(psum_free[0], 1)
                act.wait_ge(sem("ckv_var"), 1)
                nc.scalar.activation(rstd[:, :], rstd[:, :], ACT.Sqrt).then_inc(sem("ckv_std"), 1)
                full(1)
                nc.scalar.activation(widx[:, :, :], bank[1][:, 0:TT * IH].rearrange("p (t h) -> p t h", h=IH), ACT.Copy,
                                     scale=(IH ** -0.5) * (ID ** -0.5)).then_inc(sem("idx_ready"), 1)
                act.wait_ge(sem("idx_ready"), 2)
                act.sem_inc(psum_free[1], 1)
                for m in range(4):
                    b = m % 2
                    full(b)
                    nc.scalar.activation(qidxT[:, m, :], bank[b][:, :], ACT.Copy).then_inc(sem("idx_ready"), 1)
                    act.wait_ge(sem("idx_ready"), 3 + m)
                    act.sem_inc(psum_free[b], 1)
                for n in range(TT * IH):
                    N = (n // IH + 1) * P
                    b = 3 + n % 2
                    full(b)
                    if n >= 2:
                        act.wait_ge(sem("relu_used"), n - 1)
                    nc.scalar.activation(relu[:, n % 2, 0:N], bank[b][:, 0:N], ACT.Relu).then_inc(psum_free[b], 1)
                with t.loop(KD // 2, {0: 1, 1: 1}) as i:
                    evac(0, qT[:, ds(i * 2, 1), :])
                    evac(1, qT[:, ds(i * 2 + 1, 1), :])
                for m in range(KD):
                    evac(5 + m % 2, kT[:, m, :])
                for m in range(KD):
                    evac(6 + m % 2, vA[:, m // 2, (m % 2) * T:(m % 2 + 1) * T])
                sync("heads")
                act.wait_ge(psum_free[0], t.now(0))
                act.wait_ge(psum_free[1], t.now(1))
                act.wait_ge(psum_free[5], t.now(5))
                act.wait_ge(psum_free[6], t.now(6))
                act.wait_ge(psum_free[7], t.now(7))
                act.sem_inc(sem("qkv_ready"), 1)
                per = {4: 4, 5: 4, 6: 1, 7: 1, "pair": 1, "nmx": 8, "expd": 8}
                with t.loop(HEADS // 2, per) as hp:
                    n0 = t.turn("pair")

                    def exponentials(n):
                        tt, s = n % TT, n % 4
                        N = (tt + 1) * P
                        act.wait_ge(sem("nmx_ready"), t.turn("nmx") + 1)
                        nc.scalar.activation(prob[:, s, 0:N], lg[:, s, 0:N], ACT.Exp, bias=nmx[:, s:s + 1],
                                             scale=HD ** -0.5, accum_out=rowsum[:, s:s + 1]).then_inc(sem("exp_ready"), 1)

                    def turned(n):
                        a, tt = n // TT, n % TT
                        b = 4 + n % 2
                        full(b)
                        nc.scalar.activation(probT[:, a, 0:tt + 1, tt * P:(tt + 1) * P],
                                             bank[b][:, 0:(tt + 1) * P].rearrange("p (s c) -> p s c", c=P), ACT.Copy
                                             ).then_inc(sem("probT_ready"), 1)
                        act.wait_ge(sem("probT_ready"), t.turn("expd") + 1)
                        act.sem_inc(psum_free[b], 1)

                    def outputs(a):
                        b, r = 6 + a, HD * a
                        full(b)
                        nc.scalar.activation(oT[r:r + HD, ds(hp, 1), :], bank[b][r:r + HD, :], ACT.Copy
                                             ).then_inc(sem("oT_ready"), 1)
                        act.wait_ge(sem("oT_ready"), n0 * 2 + a + 1)
                        act.sem_inc(psum_free[b], 1)

                    for n in range(8):
                        exponentials(n)
                        if n >= 2:
                            turned(n - 2)
                        if n == 6:
                            outputs(0)
                    turned(6)
                    turned(7)
                    outputs(1)

            def peer(l):
                sync(f"router{l}")
                with t.loop(PM // 2, {0: 1, 1: 1, 2: 1, 3: 1, "top": 1}):
                    for s in range(2):
                        evac(s, qm[:, s, :])
                    n = t.turn("top")
                    for s in range(2):
                        act.wait_ge(sem(f"scores_used{s}"), n + 1)
                        evac(2 + s, sS[:, s, :, :].rearrange("p t k -> p (t k)"))
                act.wait_ge(sem("shifted"), l + 1)
                nc.scalar.activation(TS[:, :, :, :], TS[:, :, :, :], ACT.Exp).then_inc(sem("exps"), 1)
                for n, dst in enumerate((gT[:, :], iT[:, 0, :], iT[:, 1, :])):
                    full(4 + n)
                    nc.scalar.activation(dst, bank[4 + n][:, :], ACT.Copy).then_inc(sem("iT_ready"), 1)
                    act.wait_ge(sem("iT_ready"), 3 * l + n + 1)
                    act.sem_inc(psum_free[4 + n], 1)
                with t.loop(2, {2: 32, 3: 32, "out0": 1, "out1": 1}):
                    for par in range(2):
                        act.wait_ge(sem(f"gst_stored{par}"), t.turn(f"out{par}") * 16 + 16)
                        with t.loop(16, {2: 1, 3: 1}) as i:
                            for a in range(2):
                                full(2 + a)
                                nc.scalar.activation(gst[:, par, :, ds(i * 8 + a * 4, 4)],
                                                     bank[2 + a][:, :].rearrange("p (t c) -> p c t", c=NK), ACT.Copy
                                                     ).then_inc(psum_free[2 + a], 1)
                        for a in range(2):
                            act.wait_ge(psum_free[2 + a], t.now(2 + a))
                        act.sem_inc(sem("gst_ready"), 1)
                for par in range(2):
                    act.wait_ge(sem(f"gst_stored{par}"), 32 * (l + 1) + 16)
                nc.scalar.activation(hx[:, 0, :, :], hT[:, :, :], ACT.Copy).then_inc(sem("hx_high"), 1)

                def high(s):
                    act.wait_ge(sem(f"raw_loaded{s}"), t.turn(f"raw{s}") * 16 + 16)
                    act.wait_ge(psum_full[s], t.now(f"raw{s}") - 1 + split0[s])
                    nc.scalar.activation(hl[:, s, 0, :, :], raw[:, s, :, :], ACT.Copy).then_inc(sem(f"high_done{s}"), 1)

                split0 = {s: marks[f"experts{l}"].get(s, 0) - t.n.get(f"raw{s}", 0) for s in range(4)}

                def gelu(s, j):
                    full(s)
                    act.wait_ge(sem(f"gated{j % 2}"), t.turn(f"gated{j % 2}"))
                    nc.scalar.activation(ga[:, j % 2, :], bank[s][:, :], ACT.Gelu).then_inc(psum_free[s], 1)

                def w_high(par, j):
                    act.wait_ge(sem(f"gated{j % 2}"), t.now(f"gated{j % 2}"))
                    nc.scalar.activation(W[:, par, 0, j, :], wp[:, j % 2, :], ACT.Copy).then_inc(sem("w_high"), 1)

                def phase(par, nxt=2):
                    for j in range(GT):
                        s = 2 * j % 4
                        if 2 * j + 2 < 2 * GT or nxt > 0:
                            high((s + 2) % 4)
                        gelu(s, j)
                        if 2 * j + 3 < 2 * GT or nxt > 1:
                            high((s + 3) % 4)
                        t.turn(s + 1)
                        w_high(par, j)

                high(0)
                for j in range(GT):
                    s = 2 * j % 4
                    high((s + 2) % 4 if j < GT - 1 else 0)
                    gelu(s, j)
                    w_high(0, j)
                high(1)
                per = {k: 8 for k in (0, 1, 2, 3, "raw0", "raw1", "raw2", "raw3", "gated0", "gated1")}
                with t.loop(NG // 2 - 1, per):
                    phase(1)
                    phase(0)
                phase(1, nxt=0)
                high(1)
                for j in range(GT):
                    s = (2 * j + 1) % 4
                    if j < GT - 1:
                        high((s + 2) % 4)
                    t.turn(s)

            def deltanet():
                sync("gdn")
                act.wait_ge(sem("gdn_params"), 64)
                full(0)
                ba = bank[0][:, 0:TT * 2 * VH].rearrange("p (t c) -> p t c", c=2 * VH)
                step(nc.scalar.activation(beta, ba[:, :, 0:VH], ACT.Sigmoid))
                step(nc.scalar.activation(alog[:, :], alog[:, :], ACT.Exp))
                act.sem_inc(sem("beta_ready"), 1)
                act.wait_ge(sem("dt_added"), 1)
                step(nc.scalar.activation(gtmp[:, 1, :, :], gtmp[:, 0, :, :], ACT.Abs))
                step(nc.scalar.activation(gtmp[:, 1, :, :], gtmp[:, 1, :, :], ACT.Exp, scale=-1.0))
                nc.scalar.activation(gtmp[:, 1, :, :], gtmp[:, 1, :, :], ACT.Ln, bias=1.0).then_inc(sem("ln_ready"), 1)
                act.wait_ge(sem("gdiff_ready"), 1)
                nc.scalar.activation(eg, gcum, ACT.Exp)
                nc.scalar.activation(ekd, gtmp[:, 2, :, :], ACT.Exp)
                for u in range(2):
                    full(3 + u)
                    nc.scalar.activation(decay_last[:, u, :, :].rearrange("p t h -> p (t h)"),
                                         bank[3 + u][:, 0:TT * VH], ACT.Exp).then_inc(psum_free[3 + u], 1)
                act.wait_ge(psum_free[3], t.now(3))
                act.wait_ge(psum_free[4], t.now(4))
                act.sem_inc(sem("eg_ready"), 1)
                act.wait_ge(sem("xs_pad"), 1)
                act.wait_ge(sem("gstat_ready"), 1)
                sync("gdn_heads")
                per = {0: 2, 1: 2, 2: 2, 3: 2, 4: 3, "conv": 4, "lens": 1, "act_step": 3, "exps": 1, "pk": 1}
                with t.loop(KH, per):
                    def tile_in(i):
                        s = i % 2
                        full(s)
                        act.wait_ge(sem("conv_done"), (c0 if i < 2 else c0 + i - 1) + 1)
                        nc.scalar.activation(xs[:, s, 3:3 + T], bank[s][:, :], ACT.Copy).then_inc(psum_free[s], 1)

                    def silu(i):
                        act.wait_ge(sem("conv_done"), c0 + i + 2)
                        ins = nc.scalar.activation(cy[:, i, :], cy[:, i, :], ACT.Silu)
                        if i < 2:
                            step(ins)
                            nc.scalar.activation(sq[:, i, :], cy[:, i, :], ACT.Square).then_inc(sem("gdn_squares"), 1)
                        else:
                            ins.then_inc(sem("v_silu"), 1)

                    c0 = t.turn("conv", 4)
                    tile_in(0)
                    tile_in(1)
                    silu(0)
                    silu(1)
                    tile_in(2)
                    tile_in(3)
                    silu(2)
                    silu(3)
                    act.wait_ge(sem("lens_ready"), t.turn("lens") * 2 + 2)
                    step(nc.scalar.activation(rn[:, :, :], rn[:, :, :], ACT.Sqrt))
                    act.sem_inc(sem("rn_sqrt"), 1)
                    x0 = t.turn("exps")
                    act.wait_ge(sem("attn_raw"), x0 * 2 + 1)
                    act.wait_ge(sem("pack_ready"), x0 * 8 + 1)
                    for a in range(2):
                        for b, dst in ((2, eD), (3, eDT)):
                            full(b)
                            nc.scalar.activation(dst[:, a, :, :].rearrange("p t c -> p (t c)"), bank[b][:, :], ACT.Exp
                                                 ).then_inc(psum_free[b], 1)
                        full(4)
                        nc.scalar.activation(eG[:, a, :], bank[4][:, :], ACT.Exp).then_inc(psum_free[4], 1)
                    full(4)
                    nc.scalar.activation(ktok[:, :, :].rearrange("p t c -> p (t c)"), bank[4][:, :], ACT.Copy
                                         ).then_inc(psum_free[4], 1)
                    act.wait_ge(psum_free[4], t.now(4))
                    act.wait_ge(psum_free[3], t.now(3))
                    act.sem_inc(sem("ktok_ready"), 1)
                    t.turn("pk")
                sync("gdn_groups")
                per = {0: 2, 1: 2, 3: 8, 5: 4, 6: 4, 7: 4, "grp": 1}
                with t.loop(VH // 4, per):
                    g0 = t.turn("grp")

                    def copy(b, dst):
                        full(b)
                        nc.scalar.activation(dst, bank[b][:, :], ACT.Copy).then_inc(psum_free[b], 1)

                    def flat(x):
                        return x.rearrange("p t c -> p (t c)")

                    copy(5, flat(Qs[:, 0, :, :]))
                    for a in range(4):
                        if a < 3:
                            copy(5, flat(Qs[:, a + 1, :, :]))
                        copy(6, flat(Ys[:, a % 2, :, :]))
                    for a in range(4):
                        copy(7, wTs[:, a, :])
                    act.wait_ge(sem("OT_ready"), g0 * 4 + 1)
                    for n in range(NCH):
                        if n % 2:
                            z = n // 2
                            full(z % 2)
                            nc.scalar.activation(zs[:, z, :], bank[z % 2][:, :], ACT.Silu).then_inc(psum_free[z % 2], 1)
                        full(3)
                        nc.scalar.activation(oc[:, :, n * CHUNK:(n + 1) * CHUNK],
                                             bank[3][:, 0:4 * CHUNK].rearrange("p (a c) -> p a c", c=CHUNK), ACT.Copy
                                             ).then_inc(psum_free[3], 1)
                    act.wait_ge(psum_free[3], t.now(3))
                    act.wait_ge(psum_free[1], t.now(1))
                    nc.scalar.activation(o2[:, :, :], oc[:, :, :], ACT.Square).then_inc(sem("o_squares"), 1)
                    act.wait_ge(sem("o_vars"), g0 * 4 + 4)
                    nc.scalar.activation(o2[:, :, :], o2[:, :, :], ACT.Sqrt).then_inc(sem("o_stds"), 1)

            modulations()
            act.wait_ge(sem("x_loaded"), 16)
            act.wait_ge(sem("mods_ready"), 1)
            norm("norm0", l=0, sh=SH_M, sc=SC_M)
            if stop > 0:
                attention()
            if stop > 1:
                act.wait_ge(sem("x_ready"), 1)
                norm("norm1", l=0, sh=SH_F, sc=SC_F)
                peer(0)
            if stop > 2:
                act.wait_ge(sem("x_ready"), 2)
                norm("norm2", l=1, sh=SH_M, sc=SC_M)
                deltanet()
            if stop > 3:
                act.wait_ge(sem("x_ready"), 3)
                norm("norm3", l=1, sh=SH_F, sc=SC_F)
                peer(1)
                act.wait_ge(sem("x_ready"), 4)
                act.wait_ge(sem("fnorm_loaded"), 16)
                norm("norm4", gain=fnorm)

        @block.vector
        def _(dve):
            t = Tally(dve)

            def sync(stage):
                t.n.update(marks[stage])

            def full(b):
                dve.wait_ge(psum_full[b], t.turn(b) + 1)

            def step(ins):
                ins.then_inc(sem("dve_step"), 1)
                dve.wait_ge(sem("dve_step"), t.turn("dve_step") + 1)

            def carry():
                dve.sem_inc(sem("dve_seen"), 1)

            def modulations():
                sync("mod")
                full(2)
                dve.wait_ge(sem("adab_loaded"), 16)
                nc.vector.tensor_tensor(mods[:, :, :], bank[2][:, 0:96].rearrange("p (l c) -> p l c", l=2), adab[:, :, :],
                                        ALU.add).then_inc(psum_free[2], 1)
                dve.wait_ge(psum_free[2], t.now(2))
                step(nc.vector.tensor_scalar(mods[:, :, SC_M:SC_M + KD], mods[:, :, SC_M:SC_M + KD], 1.0, None, ALU.add))
                nc.vector.tensor_scalar(mods[:, :, SC_F:SC_F + KD], mods[:, :, SC_F:SC_F + KD], 1.0, None, ALU.add
                                        ).then_inc(sem("mods_ready"), 1)

            def norm(stage):
                sync(stage)
                full(2)
                nc.vector.tensor_scalar(rstd[:, :], bank[2][:, :], 1.0 / D, EPS, ALU.mult, ALU.add
                                        ).then_inc(sem("var_ready"), 1)
                dve.wait_ge(sem("var_ready"), t.turn("var") + 1)
                dve.sem_inc(psum_free[2], 1)
                dve.wait_ge(sem("std_ready"), t.turn("std") + 1)
                step(nc.vector.reciprocal(rstd[:, :], rstd[:, :]))
                nc.vector.tensor_tensor(hT[:, :, :], xT[:, :, :], rstd[:, :].unsqueeze(1).to_broadcast([P, KD, T]),
                                        ALU.mult).then_inc(sem("hn_ready"), 1)

            def attention():
                sync("attn")
                full(2)
                nc.vector.tensor_scalar(rstd[:, :], bank[2][:, :], 1.0 / RANK, EPS, ALU.mult, ALU.add
                                        ).then_inc(sem("ckv_var"), 1)
                dve.wait_ge(sem("ckv_var"), 1)
                dve.sem_inc(psum_free[2], 1)
                dve.wait_ge(sem("ckv_std"), 1)
                step(nc.vector.reciprocal(rstd[:, :], rstd[:, :]))
                dve.wait_ge(sem("kvn_loaded"), 16)
                for r in range(2):
                    ins = nc.vector.scalar_tensor_tensor(ckvT[:, r, :], ckvT[:, r, :], kvn[:, r:r + 1], rstd[:, :],
                                                         ALU.mult, ALU.mult)
                ins.then_inc(sem("ckv_ready"), 1)
                for n in range(TT * IH):
                    tt, h = n // IH, n % IH
                    N = (tt + 1) * P
                    b = 3 + n % 2
                    dve.wait_ge(psum_free[b], t.turn(b) + 1)
                    if n == 0:
                        dve.wait_ge(sem("idx_ready"), 6)
                    w = widx[:, tt, h:h + 1]
                    if h == 0:
                        ins = nc.vector.tensor_scalar(score[:, tt, 0:N], relu[:, n % 2, 0:N], w, None, ALU.mult)
                    else:
                        ins = nc.vector.scalar_tensor_tensor(score[:, tt, 0:N], relu[:, n % 2, 0:N], w, score[:, tt, 0:N],
                                                             ALU.mult, ALU.add)
                    ins.then_inc(sem("relu_used"), 1)
                    dve.wait_ge(sem("relu_used"), n + 1)
                for tt in range(1, TT):
                    step(nc.vector.memset(score[0:CHUNK, tt, tt * P + CHUNK:(tt + 1) * P], NEG))
                for _ in range(SEL // 8):
                    for tt in range(1, TT):
                        ins = nc.vector.max(top8[:, tt, :], score[:, tt, 0:(tt + 1) * P])
                    step(ins)
                    for tt in range(1, TT):
                        ins = nc.vector.match_replace(score[:, tt, 0:(tt + 1) * P], top8[:, tt, :],
                                                      score[:, tt, 0:(tt + 1) * P], TAKEN)
                    step(ins)
                for tt in range(1, TT):
                    N = (tt + 1) * P
                    ins = nc.vector.tensor_scalar(maskb[:, tt, 0:N], score[:, tt, 0:N], TAKEN / 2, NEG, ALU.is_gt, ALU.mult)
                step(ins)
                sync("heads")
                dve.wait_ge(sem("mask_first"), 1)
                per = {0: 2, 1: 2, 2: 2, 3: 2, "mx": 8, "nmx": 8, "exp": 8, "rinv": 8, "prob": 8}
                with t.loop(HEADS // 2, per):
                    def maxima(n):
                        tt, s = n % TT, n % 4
                        N = (tt + 1) * P
                        full(s)
                        carry()
                        nc.vector.tensor_tensor_reduce(lg[:, s, 0:N], bank[s][:, 0:N], maskb[:, tt, 0:N], 1.0, TAKEN,
                                                       ALU.add, ALU.max, mx[:, s:s + 1]).then_inc(psum_free[s], 1)
                        dve.wait_ge(psum_free[s], t.now(s))
                        nc.vector.tensor_scalar(nmx[:, s:s + 1], mx[:, s:s + 1], -(HD ** -0.5), None, ALU.mult
                                                ).then_inc(sem("nmx_ready"), 1)

                    def normalise(n):
                        tt, s = n % TT, n % 4
                        N = (tt + 1) * P
                        dve.wait_ge(sem("exp_ready"), t.turn("exp") + 1)
                        nc.vector.reciprocal(rinv[:, s:s + 1], rowsum[:, s:s + 1]).then_inc(sem("rinv_ready"), 1)
                        dve.wait_ge(sem("rinv_ready"), t.turn("rinv") + 1)
                        nc.vector.tensor_scalar(prob[:, s, 0:N], prob[:, s, 0:N], rinv[:, s:s + 1], None, ALU.mult
                                                ).then_inc(sem("prob_ready"), 1)

                    for n in range(8):
                        maxima(n)
                        if n >= 1:
                            normalise(n - 1)
                        t.turn("mx"), t.turn("nmx"), t.turn("prob")
                    normalise(7)
                sync("attn_out")
                with t.loop(KD // 2, {0: 1, 1: 1}) as i:
                    for s in range(2):
                        full(s)
                        nc.vector.scalar_tensor_tensor(xT[:, ds(i * 2 + s, 1), :], bank[s][:, :].unsqueeze(1),
                                                       mods[:, 0, ds(i * 2 + s + G_M, 1)], xT[:, ds(i * 2 + s, 1), :],
                                                       ALU.mult, ALU.add).then_inc(psum_free[s], 1)

            def x_updated():
                for b in range(4):
                    if t.n.get(b, 0):
                        dve.wait_ge(psum_free[b], t.now(b))
                dve.sem_inc(sem("x_ready"), 1)

            def peer(l):
                sync(f"router{l}")
                per = {2: 1, 3: 1, "dve_step": 8}
                with t.loop(PM // 2, per) as i:
                    for s in range(2):
                        dve.wait_ge(psum_free[2 + s], t.turn(2 + s) + 1)
                        carry()
                        for tt in range(TT):
                            ins = nc.vector.max(val[:, s, tt, 0:8], sS[:, s, tt, :])
                        step(ins)
                        carry()
                        for tt in range(TT):
                            nc.vector.max_index(idx[:, s, tt, 0:8], val[:, s, tt, 0:8], sS[:, s, tt, :])
                            ins = nc.vector.match_replace(sW[:, tt, :], val[:, s, tt, 0:8], sS[:, s, tt, :], TAKEN)
                        step(ins)
                        dve.sem_inc(sem(f"scores_used{s}"), 1)
                        for tt in range(TT):
                            ins = nc.vector.max(val[:, s, tt, 8:16], sW[:, tt, :])
                        step(ins)
                        carry()
                        for tt in range(TT):
                            ins = nc.vector.max_index(idx[:, s, tt, 8:16], val[:, s, tt, 8:16], sW[:, tt, :])
                        step(ins)
                        nc.vector.tensor_copy(V[:, :, ds(i * 2 + s, 1), :], val[:, s, :, :].unsqueeze(2))
                        nc.vector.tensor_copy(I[:, :, ds(i * 2 + s, 1), :], idx[:, s, :, :].unsqueeze(2)
                                              ).then_inc(sem("lists_done"), 1)
                dve.wait_ge(sem("lists_done"), PM * (l + 1))
                firsts = I[:, :, :, :].rearrange("p t (h q) k -> p (t h) q k", q=2)[:, :, 0, :]
                nc.vector.tensor_scalar(firsts, firsts, float(NK), None, ALU.mult).then_inc(sem("codes_ready"), 1)
                one = V[:, :, :, :].rearrange("p t (h q) k -> p (t h) q k", q=2)
                off = 0
                for a in range(TOPK // 2):
                    n = ROWS[a]
                    nc.vector.tensor_tensor(cand[:, :, off:off + n], one[:, :, 0, a:a + 1].to_broadcast([P, TT * PH, n]),
                                            one[:, :, 1, 0:n], ALU.add)
                    off += n
                step(nc.vector.tensor_tensor(cand[:, :, off:NC_], one[:, :, 0, TOPK // 2:TOPK],
                                             one[:, :, 1, 0:1].to_broadcast([P, TT * PH, TOPK // 2]), ALU.add))
                dve.wait_ge(sem("code_ready"), l + 1)
                dve.wait_ge(sem("iotac_ready"), l + 1)
                with t.loop(2, {"dve_step": 14, "picked": 2}) as i:
                    for e in range(2):
                        step(nc.vector.tensor_copy(cS[:, :, :], cand[:, ds(i * 2 * PH + e * PH, PH), :]))
                        carry()
                        for h in range(PH):
                            ins = nc.vector.max(topv[:, h, 0:8], cS[:, h, :])
                        step(ins)
                        carry()
                        for h in range(PH):
                            nc.vector.max_index(topp[:, e, h, 0:8], topv[:, h, 0:8], cS[:, h, :])
                            ins = nc.vector.match_replace(cW[:, h, :], topv[:, h, 0:8], cS[:, h, :], TAKEN)
                        step(ins)
                        carry()
                        for h in range(PH):
                            ins = nc.vector.max(topv[:, h, 8:16], cW[:, h, :])
                        step(ins)
                        carry()
                        for h in range(PH):
                            ins = nc.vector.max_index(topp[:, e, h, 8:16], topv[:, h, 8:16], cW[:, h, :])
                        step(ins)
                        nc.vector.tensor_copy(TS[:, ds(i * 2 + e, 1), :, :], topv[:, :, :].unsqueeze(1))
                        step(nc.vector.tensor_copy(posf[:, e, :, :], topp[:, e, :, :]))
                        nc.vector.tensor_tensor(eq[:, e, :, :, :].rearrange("p h k c -> p (h k) c"),
                                                posf[:, e, :, :].rearrange("p h k -> p (h k)").unsqueeze(2).to_broadcast([P, P, NC_]),
                                                iotac[:, :].unsqueeze(1).to_broadcast([P, P, NC_]), ALU.is_equal
                                                ).then_inc(sem("eq_ready"), 1)
                    for e in range(2):
                        dve.wait_ge(sem("picked"), t.turn("picked") + 1)
                        step(nc.vector.tensor_reduce(E[:, ds(i * 2 + e, 1), :, :].rearrange("p a h k -> p (a h) k"),
                                                     eq[:, e, :, :, :], AX.X, ALU.add))
                lists = TS[:, :, :, :].rearrange("p t h k -> p (t h) k")
                step(nc.vector.tensor_copy(tsum[:, :].unsqueeze(2), lists[:, :, 0:1]))
                nc.vector.tensor_tensor(lists, lists, tsum[:, :].unsqueeze(2).to_broadcast([P, TT * PH, TOPK]),
                                        ALU.subtract).then_inc(sem("shifted"), 1)
                flat = E[:, :, :, :].rearrange("p t h k -> p (t h k)")
                step(nc.vector.tensor_copy(Ei[:, 0, :], flat))
                step(nc.vector.tensor_scalar(Ei[:, 1, :], Ei[:, 0, :], NK - 1, None, ALU.bitwise_and))
                step(nc.vector.tensor_scalar(Ei[:, 0, :], Ei[:, 0, :], 7, None, ALU.arith_shift_right))
                step(nc.vector.tensor_copy(Ef[:, :, :], Ei[:, :, :]))
                dve.wait_ge(sem("exps"), l + 1)
                step(nc.vector.tensor_reduce(tsum[:, :], lists, AX.X, ALU.add))
                step(nc.vector.reciprocal(tsum[:, :], tsum[:, :]))
                nc.vector.tensor_tensor(lists, lists, tsum[:, :].unsqueeze(2).to_broadcast([P, TT * PH, TOPK]), ALU.mult
                                        ).then_inc(sem("choices_ready"), 1)
                dve.wait_ge(sem("iT_ready"), 3 * l + 3)
                for q in range(3):
                    step(nc.vector.tensor_copy(gb[:, :], gT[:, :]))
                    step(nc.vector.tensor_copy(gp[:, q, :], gb[:, :]))
                    if q < 2:
                        step(nc.vector.tensor_tensor(gT[:, :], gT[:, :], gp[:, q, :], ALU.subtract))
                sync(f"gates{l}")
                with t.loop(2, {2: 32, 3: 32}) as o:
                    for par in range(2):
                        with t.loop(16, {2: 1, 3: 1}) as i:
                            for a in range(2):
                                dve.wait_ge(psum_full[2 + a], t.turn(2 + a))
                                for j in range(4):
                                    tok = o * 2 * P + i * 8 + (par * P + a * 4 + j)
                                    nc.vector.tensor_scalar(oh1[:, a, j, :], iota_b[:, :], iT[:, 0, ds(tok, 1)], None,
                                                            ALU.is_equal)
                                    for q in range(3):
                                        ins = nc.vector.tensor_scalar(oh2[:, a, j, q, :], iota_b[:, :],
                                                                      iT[:, 1, ds(tok, 1)], gp[:, q, ds(tok, 1)],
                                                                      ALU.is_equal, ALU.mult)
                                ins.then_inc(sem("oh2_ready"), 1)
                dve.wait_ge(sem("hx_high"), l + 1)
                nc.vector.tensor_tensor(hx[:, 1, :, :], hT[:, :, :], hx[:, 0, :, :].bitcast(F32), ALU.subtract
                                        ).then_inc(sem("hx_ready"), 1)
                sync(f"experts{l}")

                def low(s):
                    dve.wait_ge(sem(f"high_done{s}"), t.turn(f"high{s}") + 1)
                    nc.vector.tensor_tensor(hl[:, s, 1, :, :], raw[:, s, :, :], hl[:, s, 0, :, :].bitcast(F32), ALU.subtract
                                            ).then_inc(sem(f"split_done{s}"), 1)

                def gate(s, j):
                    dve.wait_ge(psum_free[s], t.turn(s) + 1)
                    dve.wait_ge(sem(f"gt_loaded{j % 4}"), t.turn(f"gt{j % 4}") * 16 + 16)
                    nc.vector.tensor_tensor(wp[:, j % 2, :], ga[:, j % 2, :], gt[:, j % 4, :], ALU.mult
                                            ).then_inc(sem(f"gated{j % 2}"), 1)
                    dve.wait_ge(sem(f"gated{j % 2}"), t.turn(f"gated{j % 2}") + 1)
                    dve.sem_inc(sem(f"gt_used{j % 4}"), 1)

                def w_low(par, j):
                    dve.wait_ge(sem("w_high"), t.turn("w_high") + 1)
                    nc.vector.tensor_tensor(W[:, par, 1, j, :], wp[:, j % 2, :], W[:, par, 0, j, :].bitcast(F32), ALU.subtract
                                            ).then_inc(sem("w_ready"), 1)

                def add(s, j):
                    full(s)
                    nc.vector.scalar_tensor_tensor(xT[:, j, :], bank[s][:, :], mods[:, l, G_F + j:G_F + j + 1], xT[:, j, :],
                                                   ALU.mult, ALU.add).then_inc(psum_free[s], 1)

                def phase(par, nxt=2):
                    for j in range(GT):
                        s = 2 * j % 4
                        if 2 * j + 2 < 2 * GT or nxt > 0:
                            low((s + 2) % 4)
                        gate(s, j)
                        if 2 * j + 3 < 2 * GT or nxt > 1:
                            low((s + 3) % 4)
                        w_low(par, j)
                        add(s + 1, j)

                low(0)
                for j in range(GT):
                    s = 2 * j % 4
                    low((s + 2) % 4 if j < GT - 1 else 0)
                    gate(s, j)
                    w_low(0, j)
                low(1)
                per = {k: 8 for k in (0, 1, 2, 3, "high0", "high1", "high2", "high3", "gated0", "gated1")}
                per |= {"gt0": 4, "gt1": 4, "gt2": 4, "gt3": 4, "w_high": 16}
                with t.loop(NG // 2 - 1, per):
                    phase(1)
                    phase(0)
                phase(1, nxt=0)
                low(1)
                for j in range(GT):
                    s = (2 * j + 1) % 4
                    if j < GT - 1:
                        low((s + 2) % 4)
                    add(s, j)

            def deltanet():
                sync("gdn")
                dve.wait_ge(sem("gdn_params"), 64)
                full(0)
                dve.wait_ge(sem("beta_ready"), 1)
                ba = bank[0][:, 0:TT * 2 * VH].rearrange("p (t c) -> p t c", c=2 * VH)
                rows = [P, TT, VH]
                nc.vector.tensor_tensor(gtmp[:, 0, :, :], ba[:, :, VH:2 * VH], dtb[:, :].unsqueeze(1).to_broadcast(rows),
                                        ALU.add).then_inc(psum_free[0], 1)
                dve.wait_ge(psum_free[0], t.now(0))
                dve.sem_inc(sem("dt_added"), 1)
                step(nc.vector.tensor_scalar(gtmp[:, 2, :, :], gtmp[:, 0, :, :], 0.0, None, ALU.max))
                dve.wait_ge(sem("ln_ready"), 1)
                step(nc.vector.tensor_tensor(gtmp[:, 1, :, :], gtmp[:, 1, :, :], gtmp[:, 2, :, :], ALU.add))
                nc.vector.scalar_tensor_tensor(graw, gtmp[:, 1, :, :], -1.0, alog[:, :].unsqueeze(1).to_broadcast(rows),
                                               ALU.mult, ALU.mult).then_inc(sem("graw_ready"), 1)
                full(2)
                n = TT * VH
                step(nc.vector.tensor_copy(gcum.rearrange("p t h -> p (t h)"), bank[2][:, 0:n]))
                nc.vector.tensor_tensor(gtmp[:, 2, :, :].rearrange("p t h -> p (t h)"), bank[2][:, n:2 * n],
                                        gcum.rearrange("p t h -> p (t h)"), ALU.subtract).then_inc(psum_free[2], 1)
                dve.wait_ge(psum_free[2], t.now(2))
                dve.sem_inc(sem("gdiff_ready"), 1)
                dve.wait_ge(sem("eg_ready"), 1)
                nc.vector.tensor_tensor(bege, beta, eg, ALU.mult).then_inc(sem("gstat_ready"), 1)
                sync("gdn_heads")
                per = {2: 2, 3: 2, 5: 4, 6: 1, 7: 1, "dve_step": 15, "x": 4, "p": 1}
                with t.loop(KH, per) as i:
                    p0 = t.turn("p")

                    def conv(j, tile):
                        s = j % 2
                        t.turn("x")
                        dve.wait_ge(psum_free[s], p0 * 2 + (marks["gdn_heads"][s] + j // 2 + 1))
                        if j == 0:
                            dve.wait_ge(sem("pack_ready"), p0 * 8 + 1)
                        step(nc.vector.tensor_scalar(cy[:, j, :], xs[:, s, 0:T], convw[:, tile, 0], None, ALU.mult))
                        for w in range(1, 4):
                            ins = nc.vector.scalar_tensor_tensor(cy[:, j, :], xs[:, s, w:w + T], convw[:, tile, w],
                                                                 cy[:, j, :], ALU.mult, ALU.add)
                            if w < 3:
                                step(ins)
                        ins.then_inc(sem("conv_done"), 1)

                    conv(0, ds(i, 1))
                    conv(1, ds(i + KH, 1))
                    for q in range(2):
                        full(5)
                        nc.vector.tensor_scalar(rn[:, q, :], bank[5][:, :], EPS, None, ALU.add).then_inc(psum_free[5], 1)
                        dve.wait_ge(psum_free[5], t.now(5))
                        dve.sem_inc(sem("lens_ready"), 1)
                        conv(2 + q, ds(i * 2 + 2 * KH + q, 1))
                    dve.wait_ge(sem("rn_sqrt"), p0 + 1)
                    step(nc.vector.reciprocal(rn[:, :, :], rn[:, :, :]))
                    nc.vector.scalar_tensor_tensor(cy[:, 0, :], cy[:, 0, :], BD ** -0.5, rn[:, 0, :], ALU.mult, ALU.mult
                                                   ).then_inc(sem("qk_ready"), 1)
                    nc.vector.tensor_tensor(cy[:, 1, :], cy[:, 1, :], rn[:, 1, :], ALU.mult).then_inc(sem("qk_ready"), 1)
                    full(6)
                    full(7)
                    dve.wait_ge(sem("BS_ready"), p0 * 2 + 2)
                    for a in range(2):
                        flat = lambda x: x.rearrange("p t c -> p (t c)")
                        dve.wait_ge(psum_free[2], t.turn(2) + 1)
                        dve.wait_ge(sem(f"amat_stored{a}"), p0 * 32 + 16)
                        step(nc.vector.tensor_tensor(flat(amat[:, a, :, :]), bank[6][:, :], flat(eD[:, a, :, :]), ALU.mult))
                        nc.vector.tensor_tensor(flat(amat[:, a, :, :]), flat(amat[:, a, :, :]), flat(BS[:, a, :, :]),
                                                ALU.mult).then_inc(sem("amat_ready"), 1)
                        dve.wait_ge(psum_free[3], t.turn(3) + 1)
                        dve.wait_ge(sem(f"pack_stored{a}"), p0 * 16 + 16)
                        nc.vector.tensor_tensor(pack[:, a, 4, :], bank[7][:, :], flat(eDT[:, a, :, :]), ALU.mult
                                                ).then_inc(sem("attn_raw"), 1)
                    dve.wait_ge(sem("attn_raw"), p0 * 2 + 3)
                    dve.sem_inc(psum_free[6], 1)
                    dve.sem_inc(psum_free[7], 1)
                    for a in range(2):
                        full(5)
                        nc.vector.tensor_tensor(pack[:, a, 0, :].rearrange("p (t c) -> p t c", c=P),
                                                bank[5][:, :].rearrange("p (t c) -> p t c", c=P),
                                                beta[:, :, ds(i * 2 + a, 1)].to_broadcast([P, TT, P]), ALU.mult
                                                ).then_inc(psum_free[5], 1)
                        dve.wait_ge(psum_free[5], t.now(5))
                        dve.sem_inc(sem("pack_v"), 1)
                dve.wait_ge(sem("SA_loaded"), 32)
                step(nc.vector.memset(X[:, :, :, :], 0.0))
                diag = X[:, :, :, :].rearrange("p q i j -> p q (i j)")[:, :, 0:HB * HB:HB + 1]
                step(nc.vector.memset(diag, 1.0))
                step(nc.vector.tensor_scalar(SA[:, :, :, :], SA[:, :, :, :], -1.0, None, ALU.mult))
                for r in range(1, HB):
                    pr = prod[:, 0:2 * r * r].rearrange("p (q c j) -> p q c j", q=2, c=r)
                    step(nc.vector.tensor_tensor(pr, SA[:, :, r, 0:r].unsqueeze(2).to_broadcast([P, 2, r, r]),
                                                 X[:, :, 0:r, 0:r].rearrange("p q j c -> p q c j"), ALU.mult))
                    step(nc.vector.tensor_reduce(X[:, :, r, 0:r], pr, AX.X, ALU.add))
                dve.sem_inc(sem("X_ready"), 1)
                dve.wait_ge(sem("X_stored"), 16)
                sync("gdn_groups")
                per = {2: 14, 4: 14, "g": 1, "S": 9, "dve_step": 3}
                with t.loop(VH // 4, per) as i:
                    g0 = t.turn("g")
                    for a in range(4):
                        full(4)
                        nc.vector.tensor_tensor(Qs[:, a, :, :].rearrange("p t c -> p (t c)"),
                                                Qs[:, a, :, :].rearrange("p t c -> p (t c)"), bank[4][:, :], ALU.subtract
                                                ).then_inc(psum_free[4], 1)
                    for a in range(4):
                        full(2)
                        nc.vector.tensor_copy(us[:, a, :, :].rearrange("p t c -> p (t c)"), bank[2][:, :]
                                              ).then_inc(psum_free[2], 1)
                    nc.vector.memset(S[:, 0, :, :], 0.0).then_inc(sem("state_ready"), 1)
                    t.turn("S")
                    dve.wait_ge(psum_free[2], t.now(2))
                    for n in range(NCH):
                        rows, tt = slice(CHUNK * (n % 2), CHUNK * (n % 2 + 1)), n // 2
                        full(2)
                        nc.vector.tensor_tensor(vn[rows, :, :], us[rows, :, tt, :],
                                                bank[2][rows, :].rearrange("p (a c) -> p a c", c=P), ALU.subtract
                                                ).then_inc(psum_free[2], 1)
                        full(4)
                        dve.wait_ge(sem("state_ready"), t.now("S"))
                        for a in range(4):
                            ins = nc.vector.scalar_tensor_tensor(S[:, (n + 1) % 2, a, :], S[:, n % 2, a, :],
                                                                 decay_last[:, n % 2, tt, ds(i * 4 + a, 1)],
                                                                 bank[4][:, a * P:(a + 1) * P], ALU.mult, ALU.add)
                        ins.then_inc(sem("state_ready"), 1)
                        dve.wait_ge(sem("state_ready"), t.turn("S") + 1)
                        dve.sem_inc(psum_free[4], 1)
                    for a in range(4):
                        b = 2 + 2 * (a % 2)
                        full(b)
                        nc.vector.tensor_scalar(o2[:, a, :], bank[b][:, :], 1.0 / BD, EPS, ALU.mult, ALU.add
                                                ).then_inc(psum_free[b], 1)
                        dve.wait_ge(psum_free[b], t.now(b))
                        dve.sem_inc(sem("o_vars"), 1)
                    dve.wait_ge(sem("o_stds"), g0 + 1)
                    step(nc.vector.reciprocal(o2[:, :, :], o2[:, :, :]))
                    step(nc.vector.scalar_tensor_tensor(oc[:, :, :], oc[:, :, :], onorm[:, 0:1], o2[:, :, :],
                                                        ALU.mult, ALU.mult))
                    for a in range(4):
                        ins = nc.vector.tensor_tensor(OT[:, ds(i * 4 + a, 1), :], oc[:, a:a + 1, :], zs[:, a:a + 1, :], ALU.mult)
                    step(ins)
                    dve.sem_inc(sem("OT_ready"), 4)
                sync("gdn_out")
                with t.loop(KD, {0: 1, 1: 1, "dve_step": 1}) as i:
                    for s in range(2):
                        full(s)
                        ins = nc.vector.scalar_tensor_tensor(xT[:, ds(i, 1), :], bank[s][:, :].unsqueeze(1),
                                                             mods[:, 1, ds(i + G_M, 1)], xT[:, ds(i, 1), :], ALU.mult, ALU.add)
                        if s == 0:
                            step(ins)
                            dve.sem_inc(psum_free[0], 1)
                        else:
                            ins.then_inc(psum_free[1], 1)

            modulations()
            norm("norm0")
            if stop > 0:
                attention()
                x_updated()
            if stop > 1:
                norm("norm1")
                peer(0)
                x_updated()
            if stop > 2:
                norm("norm2")
                deltanet()
                x_updated()
            if stop > 3:
                norm("norm3")
                peer(1)
                x_updated()
                norm("norm4")


def lay_out(a):
    import numpy as np

    cols = lambda v, p=P: np.ascontiguousarray(v.reshape(-1, p).T)
    return {
        "x_t": np.ascontiguousarray(a["x"][0].T),
        "c_t": cols(a["c"][0]),
        "ada_w": a["ada_w"],
        "ada_b": np.ascontiguousarray(a["ada_b"].reshape(2, 6 * KD, P).transpose(2, 0, 1)),
        "a_w_in": a["a_w_in"][0],
        "a_kv_norm": cols(a["a_kv_norm"][0]),
        "a_w_uk": a["a_w_uk"][0].reshape(RANK, HEADS * HD),
        "a_w_uv": a["a_w_uv"][0].reshape(RANK, HEADS * HD),
        "a_w_out": a["a_w_out"][0],
        "b_w_in": a["b_w_in"][0],
        "b_conv": np.ascontiguousarray(a["b_conv"][0, :, 0, :].reshape(4, -1, P).transpose(2, 1, 0)),
        "b_a_log": a["b_a_log"],
        "b_dt_bias": a["b_dt_bias"],
        "b_out_norm": cols(a["b_out_norm"][0]),
        "b_w_out": a["b_w_out"][0],
        "p_w_q": a["p_w_q"],
        "p_keys_t": np.ascontiguousarray(a["p_sub_keys"].reshape(2, PM, NK, P).transpose(0, 1, 3, 2)),
        "p_u_t": np.ascontiguousarray(a["p_u"].reshape(2, NK, NK, KD, P).transpose(0, 2, 4, 3, 1)),
        "p_v": a["p_v"].reshape(2, NK, NK, D),
        "final_norm": cols(a["final_norm"]),
    }


def kernel(**inputs):
    import numpy as np
    import concourse.bacc as bacc
    from concourse.bass_utils import run_bass_kernel_spmd

    a = {k: np.asarray(v) for k, v in inputs.items()}
    arrays = lay_out(a)
    nc = bacc.Bacc("TRN2", target_bir_lowering=False, num_devices=1)
    args = [nc.dram_tensor(n, v.shape, mybir.dt.from_np(v.dtype), kind="ExternalInput").ap() for n, v in arrays.items()]
    out = nc.dram_tensor("out_t", (D, T), F32, kind="ExternalOutput").ap()
    hybrid_trunk(nc, *args, out)
    got = run_bass_kernel_spmd(nc, [arrays], core_ids=[0]).results[0]["out_t"]
    return np.ascontiguousarray(got.T).reshape(1, T, D)
```

```python
import math
from contextlib import ExitStack, contextmanager

import concourse.bass as bass
from concourse import mybir
from concourse.alu_op_type import AluOpType as ALU

F32 = mybir.dt.float32
F32R = mybir.dt.float32r
BF16 = mybir.dt.bfloat16
U32 = mybir.dt.uint32
I32 = mybir.dt.int32
ACT = mybir.ActivationFunctionType
AX = mybir.AxisListType
ds = bass.ds

P = 128
T = 512
TT = T // P
D = 1024
KD = D // P
EPS = 1e-6
CHUNK = 64

HEADS, HD, RANK = 16, 64, 256
IH, ID = 8, 64
SEL = min(256, T // 4)
C_Q, C_KV, C_QI, C_KI = 0, HEADS * HD, HEADS * HD + RANK, HEADS * HD + RANK + IH * ID
C_WI = C_KI + ID
NEG, TAKEN = -1.0e30, -3.0e38

KH, VH, BD = 8, 16, 128
NCH = T // CHUNK
C_BETA = 2 * KH * BD + 2 * VH * BD
HB = 32

PH, NK, TOPK = 8, 128, 16
PM = 2 * PH
ROWS = [TOPK // (a + 1) for a in range(TOPK)]
NC_ = sum(ROWS)
GB = 64
GQ = NK // 4
U_LAST = 8
U_AHEAD = NK - U_LAST - 3 * (T // 16)

FREE_AT_START = {"conv_done": 1, "attn_raw": 1, "pack_ready": 1, "amat_ready": 1, "OT_ready": 1, "w_ready": 1}
FREE_AT_START |= {f"split_done{s}": 1 for s in range(4)} | {f"scores_used{s}": 1 for s in range(2)}
FREE_AT_START |= {f"act_stored{s}": 16 for s in range(3)}
FREE_AT_START |= {f"gst_stored{s}": 64 for s in range(2)}
FREE_AT_START |= {f"{n}{s}": 16 for n in ("pack_stored", "amat_stored") for s in range(2)}

SH_M, SC_M, G_M, SH_F, SC_F, G_F = (KD * n for n in range(6))


def each_slot(n):
    return {k: 1 for s in range(n) for k in (s, f"split{s}")}


class Tally:

    def __init__(self, eng):
        self.eng, self.n, self.loops = eng, {}, []

    def now(self, key):
        v = self.n.get(key, 0)
        for i, per in self.loops:
            if key in per:
                v = i * per[key] + v
        return v

    def turn(self, key, by=1):
        v = self.now(key)
        self.n[key] = self.n.get(key, 0) + by
        return v

    @contextmanager
    def loop(self, times, per):
        start = dict(self.n)
        with self.eng.Fori(0, times) as i:
            self.loops.append((i, per))
            yield i
            had = {k: v - start.get(k, 0) for k, v in self.n.items() if v != start.get(k, 0)}
            assert had == per, (had, per)
            self.loops.pop()
        for k, v in per.items():
            self.n[k] = start.get(k, 0) + times * v
def hybrid_trunk(nc, x_t, c_t, ada_w, ada_b, a_w_in, a_kv_norm, a_w_uk, a_w_uv, a_w_out, b_w_in, b_conv,
                 b_a_log, b_dt_bias, b_out_norm, b_w_out, p_w_q, p_keys_t, p_u_t, p_v, final_norm, out_t):
    ctx = ExitStack()
    sems = {}

    def sem(name):
        if name not in sems:
            sems[name] = ctx.enter_context(nc.semaphore(name))
        return sems[name]

    def sb(name, shape, dt=F32, where=None):
        return (where or ctx).enter_context(nc.sbuf_tensor(name, shape, dt))

    def dram(name, shape, dt=F32):
        return nc.dram_tensor(name, shape, dt).ap()

    with ctx:
        bank = [ctx.enter_context(nc.psum_tensor(f"bank{b}", [P, T], F32)) for b in range(8)]
        psum_full = [sem(f"psum_full{b}") for b in range(8)]
        psum_free = [sem(f"psum_free{b}") for b in range(8)]

        xT = sb("xT", [P, KD, T])
        hT = sb("hT", [P, KD, T])
        rstd = sb("rstd", [P, T])
        mods = sb("mods", [P, 2, 6 * KD])
        ident = sb("ident", [P, P])
        ones = sb("ones", [P, P])
        fnorm = sb("fnorm", [P, KD])
        kvn = sb("kvn", [P, 2])
        w_ring = sb("w_ring", [P, 2, KD, P])
        iota = sb("iota", [P, P])
        iota_b = sb("iota_b", [P, P], BF16)
        iota_i = sb("iota_i", [P, P], I32)

        part = ExitStack()
        condT = sb("condT", [P, KD], where=part)
        ada_ring = sb("ada_ring", [P, 2, KD, T], where=part)
        ada_row = sb("ada_row", [1, 2, 6 * D], where=part)
        ada_sq = sb("ada_sq", [2 * 6 * KD, P], where=part)
        adab = sb("adab", [P, 2, 6 * KD], where=part)
        part.close()
        ada_dram = dram("ada_scratch", [2 * 6 * KD, P])

        part = ExitStack()
        ckvT = sb("ckvT", [P, 2, T], where=part)
        ckv_sq = sb("ckv_sq", [P, 2, T], where=part)
        kidxT = sb("kidxT", [P, T], where=part)
        qidxT = sb("qidxT", [P, 4, T], where=part)
        widx = sb("widx", [P, TT, IH], where=part)
        relu = sb("relu", [P, 2, T], where=part)
        score = sb("score", [P, TT, T], where=part)
        top8 = sb("top8", [P, TT, 8], where=part)
        maskb = sb("maskb", [P, TT, T], where=part)
        w_ukv = sb("w_ukv", [P, 2, 2, HEADS * HD], where=part)
        qT = sb("qT", [P, KD, T], where=part)
        kT = sb("kT", [P, KD, T], where=part)
        vA = sb("vA", [P, TT, HEADS * HD], where=part)
        q_pair = sb("q_pair", [P, T], where=part)
        k_pair = sb("k_pair", [P, T], where=part)
        v_pair = sb("v_pair", [P, TT, P], where=part)
        lg = sb("lg", [P, 4, T], where=part)
        prob = sb("prob", [P, 4, T], where=part)
        mx = sb("mx", [P, 4], where=part)
        nmx = sb("nmx", [P, 4], where=part)
        rowsum = sb("rowsum", [P, 4], where=part)
        rinv = sb("rinv", [P, 4], where=part)
        probT = sb("probT", [P, 2, TT, T], where=part)
        oT = sb("oT", [P, KD, T], where=part)
        part.close()

        part = ExitStack()
        hl = sb("hl", [P, 4, 2, KD, P], F32R, where=part)
        hx = sb("hx", [P, 2, KD, T], F32R, where=part)
        gT = sb("gT", [P, T], where=part)
        iT = sb("iT", [P, 2, T], where=part)
        gp = sb("gp", [P, 3, T], where=part)
        gb = sb("gb", [P, T], BF16, where=part)
        stage_ = ExitStack()
        keys = sb("keys", [P, 2, NK], where=stage_)
        qm = sb("qm", [P, 2, T], where=stage_)
        sS = sb("sS", [P, 2, TT, NK], where=stage_)
        sW = sb("sW", [P, TT, NK], where=stage_)
        val = sb("val", [P, 2, TT, TOPK], where=stage_)
        idx = sb("idx", [P, 2, TT, TOPK], U32, where=stage_)
        V = sb("V", [P, TT, PM, TOPK], where=stage_)
        I = sb("I", [P, TT, PM, TOPK], where=stage_)
        cand = sb("cand", [P, TT * PH, NC_], where=stage_)
        code = sb("code", [P, TT * PH, NC_], where=stage_)
        cS = sb("cS", [P, PH, NC_], where=stage_)
        cW = sb("cW", [P, PH, NC_], where=stage_)
        topv = sb("topv", [P, PH, TOPK], where=stage_)
        topp = sb("topp", [P, PH, TOPK], U32, where=stage_)
        posf = sb("posf", [P, PH, TOPK], where=stage_)
        eq = sb("eq", [P, PH, TOPK, NC_], where=stage_)
        iotac = sb("iotac", [P, NC_], where=stage_)
        iotac_i = sb("iotac_i", [P, NC_], I32, where=stage_)
        TS = sb("TS", [P, TT, PH, TOPK], where=stage_)
        E = sb("E", [P, TT, PH, TOPK], where=stage_)
        Ei = sb("Ei", [P, 2, TT * P], I32, where=stage_)
        Ef = sb("Ef", [P, 2, TT * P], where=stage_)
        tsum = sb("tsum", [P, TT * PH], where=stage_)
        stage_.close()
        stage_ = ExitStack()
        gst = sb("gst", [P, 2, NK, GB], where=stage_)
        oh1 = sb("oh1", [P, 2, 4, P], BF16, where=stage_)
        oh2 = sb("oh2", [P, 2, 4, 3, P], BF16, where=stage_)
        stage_.close()
        stage_ = ExitStack()
        gg = sb("gg", [P, 2, T // GB, 4, GB], where=stage_)
        ua = sb("ua", [P, 4, T], where=stage_)
        W = sb("W", [P, 4, 2, T], F32R, where=stage_)
        wp = sb("wp", [P, 2, T], where=stage_)
        stage_.close()
        part.close()
        g_dram = dram("g_scratch", [T // GB, P, NK, GB])
        act_dram = dram("act_scratch", [NK, P, T])

        def raw(s):
            if s < 2:
                return w_ring[:, s, :, :]
            return hT[:, 2 * s - 4:2 * s - 2, :].rearrange("p a (b c) -> p (a b) c", c=P)

        def ga(s):
            return hT[:, 4 + s, :]

        part = ExitStack()
        tri = sb("tri", [P, P], where=part)
        strict = sb("strict", [P, P], where=part)
        samec = sb("samec", [P, P], where=part)
        decay_last = sb("decay_last", [P, 2, TT, VH], where=part)
        onorm = sb("onorm", [P, 1], where=part)
        OT = sb("OT", [P, VH, T], where=part)
        solve_ = ExitStack()
        gstat = sb("gstat", [P, 6, TT, VH], where=solve_)
        graw, gcum, eg, ekd, beta, bege = (gstat[:, n, :, :] for n in range(6))
        gtmp = sb("gtmp", [P, 3, TT, VH], where=solve_)
        alog = sb("alog", [P, VH], where=solve_)
        dtb = sb("dtb", [P, VH], where=solve_)
        convw = sb("convw", [P, 2 * KH + VH, 4], where=solve_)
        xs = sb("xs", [P, 2, 3 + T], where=solve_)
        cy = sb("cy", [P, 4, T], where=solve_)
        sq = sb("sq", [P, 2, T], where=solve_)
        rn = sb("rn", [P, 2, T], where=solve_)
        gsel = sb("gsel", [P, TT, 2], where=solve_)
        SG = sb("SG", [P, 2, TT, P], where=solve_)
        BS = sb("BS", [P, 2, TT, P], where=solve_)
        eD = sb("eD", [P, 2, TT, P], where=solve_)
        eDT = sb("eDT", [P, 2, TT, P], where=solve_)
        eG = sb("eG", [P, 2, T], where=solve_)
        ktok = sb("ktok", [P, TT, P], where=solve_)
        amat = sb("amat", [P, 2, TT, P], where=solve_)
        pack = sb("pack", [P, 2, 5, T], where=solve_)
        solve_.close()
        solve_ = ExitStack()
        SA = sb("SA", [P, 2, HB, HB], where=solve_)
        X = sb("X", [P, 2, HB, HB], where=solve_)
        prod = sb("prod", [P, 2 * HB * HB], where=solve_)
        solve_.close()
        vkb = sb("vkb", [P, 4, 2, T], where=part)
        kqa = sb("kqa", [P, 4, 3, T], where=part)
        Eb = sb("Eb", [P, 4, TT, P], where=part)
        Pb = sb("Pb", [P, 4, TT, P], where=part)
        Qs = sb("Qs", [P, 4, TT, P], where=part)
        Ys = sb("Ys", [P, 2, TT, P], where=part)
        us = sb("us", [P, 4, TT, P], where=part)
        wTs = sb("wTs", [P, 4, T], where=part)
        vn = sb("vn", [P, 4, P], where=part)
        S = sb("S", [P, 2, 4, P], where=part)
        oc = sb("oc", [P, 4, T], where=part)
        o2 = sb("o2", [P, 4, T], where=part)
        part.close()
        a_dram = dram("a_scratch", [VH, NCH, CHUNK, CHUNK])
        t_dram = dram("t_scratch", [VH * NCH, 2, HB, HB])
        pack_dram = dram("pack_scratch", [VH, P, 5, T])

        block = ctx.enter_context(nc.Block())
        marks = {}

        @block.tensor
        def _(pe):
            t = Tally(pe)

            def mark(stage):
                marks[stage] = {k: v for k, v in t.n.items() if isinstance(k, int) or k.startswith("split")}

            def take(b):
                pe.wait_ge(psum_free[b], t.turn(b))

            def slot_ready(s):
                pe.wait_ge(sem(f"w_loaded{s}"), t.turn(f"w{s}") * 16 + 16)

            def tile_product(s, rhs, out=None, m=P):
                slot_ready(s)
                take(s)
                for k in range(KD):
                    mm = nc.tensor.matmul(bank[s][0:m, :], w_ring[:, s, k, 0:m], rhs[:, k, :],
                                          start=(k == 0), stop=(k == KD - 1))
                mm.then_inc(psum_full[s], 1)

            def modulations():
                mark("mod")
                pe.wait_ge(sem("cond_ready"), 1)
                for n in range(24):
                    s = n % 2
                    pe.wait_ge(sem(f"ada_loaded{s}"), 16 * (n // 2 + 1))
                    take(s)
                    for k in range(KD):
                        mm = nc.tensor.matmul(bank[s][0:1, :], condT[:, k:k + 1], ada_ring[:, s, k, :],
                                              start=(k == 0), stop=(k == KD - 1))
                    mm.then_inc(psum_full[s], 1)
                pe.wait_ge(sem("ada_square"), 16)
                pe.wait_ge(sem("consts"), 2)
                take(2)
                nc.tensor.transpose(bank[2][:, 0:96], ada_sq[:, :], ident[0:96, 0:96]).then_inc(psum_full[2], 1)

            def norm(stage):
                mark(stage)
                take(2)
                for k in range(KD):
                    pe.wait_ge(sem("squares"), t.turn("squares") + 1)
                    mm = nc.tensor.matmul(bank[2][:, :], ones[:, :], hT[:, k, :], start=(k == 0), stop=(k == KD - 1))
                mm.then_inc(psum_full[2], 1)

            def attention():
                mark("attn")
                pe.wait_ge(sem("h_ready"), t.turn("h_ready") + 1)
                tile_product(0, hT)
                tile_product(1, hT)
                tile_product(0, hT)
                pe.wait_ge(sem("ckv_squares"), 1)
                take(2)
                for r in range(2):
                    mm = nc.tensor.matmul(bank[2][:, :], ones[:, :], ckv_sq[:, r, :], start=(r == 0), stop=(r == 1))
                mm.then_inc(psum_full[2], 1)
                slot_ready(1)
                take(1)
                for tt in range(TT):
                    for k in range(KD):
                        mm = nc.tensor.matmul(bank[1][:, tt * IH:(tt + 1) * IH], hT[:, k, tt * P:(tt + 1) * P],
                                              w_ring[:, 1, k, 0:IH], start=(k == 0), stop=(k == KD - 1))
                mm.then_inc(psum_full[1], 1)
                for m in range(4):
                    tile_product(m % 2, hT)
                pe.wait_ge(sem("idx_ready"), 6)
                for n in range(TT * IH):
                    tt, h = n // IH, n % IH
                    r = ID * (h % 2)
                    b = 3 + n % 2
                    take(b)
                    nc.tensor.matmul(bank[b][:, 0:(tt + 1) * P], qidxT[r:r + ID, h // 2, tt * P:(tt + 1) * P],
                                     kidxT[r:r + ID, 0:(tt + 1) * P], start=True, stop=True).then_inc(psum_full[b], 1)
                with t.loop(KD // 2, {"w0": 1, "w1": 1, 0: 1, 1: 1}):
                    tile_product(0, hT)
                    tile_product(1, hT)
                pe.wait_ge(sem("ukv_loaded"), 32)
                pe.wait_ge(sem("ckv_ready"), 1)
                for m in range(KD):
                    b = 5 + m % 2
                    take(b)
                    for r in range(2):
                        mm = nc.tensor.matmul(bank[b][:, :], w_ukv[:, 0, r, m * P:(m + 1) * P], ckvT[:, r, :],
                                              start=(r == 0), stop=(r == 1))
                    mm.then_inc(psum_full[b], 1)
                for m in range(KD):
                    tt, c = m // 2, m % 2
                    b = 6 + m % 2
                    take(b)
                    for r in range(2):
                        mm = nc.tensor.matmul(bank[b][:, :], ckvT[:, r, tt * P:(tt + 1) * P],
                                              w_ukv[:, 1, r, c * T:(c + 1) * T], start=(r == 0), stop=(r == 1))
                    mm.then_inc(psum_full[b], 1)
                mark("heads")
                per = {0: 2, 1: 2, 2: 2, 3: 2, 4: 4, 5: 4, 6: 1, 7: 1, "pair": 1, "prob": 8, "probT": 8}
                with t.loop(HEADS // 2, per) as hp:
                    n0 = t.turn("pair")
                    pe.wait_ge(sem("qk_pair_ready"), n0 * 2 + 2)

                    def logits(n):
                        a, tt = n // TT, n % TT
                        r, b = HD * a, n % 4
                        take(b)
                        nc.tensor.matmul(bank[b][:, 0:(tt + 1) * P], q_pair[r:r + HD, tt * P:(tt + 1) * P],
                                         k_pair[r:r + HD, 0:(tt + 1) * P],
                                         start=True, stop=True).then_inc(psum_full[b], 1)

                    def turn_probs(n):
                        tt, b = n % TT, 4 + n % 2
                        pe.wait_ge(sem("prob_ready"), t.turn("prob") + 1)
                        take(b)
                        for st in range(tt + 1):
                            mm = nc.tensor.transpose(bank[b][:, st * P:(st + 1) * P], prob[:, n % 4, st * P:(st + 1) * P],
                                                     ident[:, :])
                        mm.then_inc(psum_full[b], 1)

                    def outputs(a):
                        r, b = HD * a, 6 + a
                        pe.wait_ge(sem("v_pair_ready"), n0 + 1)
                        pe.wait_ge(sem("probT_ready"), t.turn("probT", 4) + 4)
                        take(b)
                        for st in range(TT):
                            mm = nc.tensor.matmul(bank[b][r:r + HD, st * P:], v_pair[:, st, r:r + HD],
                                                  probT[:, a, st, st * P:], start=(st == 0), stop=(st == TT - 1))
                        mm.then_inc(psum_full[b], 1)

                    for n in range(8):
                        logits(n)
                        if n >= 3:
                            turn_probs(n - 3)
                        if n - 3 == 4:
                            outputs(0)
                    for n in range(5, 8):
                        turn_probs(n)
                    outputs(1)
                mark("attn_out")
                pe.wait_ge(sem("oT_ready"), HEADS)
                with t.loop(KD // 2, {"w0": 1, "w1": 1, 0: 1, 1: 1}):
                    tile_product(0, oT)
                    tile_product(1, oT)

            def peer(l):
                mark(f"router{l}")
                t.turn("h_ready")
                pe.wait_ge(sem("hx_ready"), l + 1)

                def split_product(s):
                    pe.wait_ge(sem(f"split_done{s}"), t.turn(f"split{s}") + 2)
                    take(s)
                    for k in range(KD):
                        hi, lo = hl[:, s, 0, k, :], hl[:, s, 1, k, :]
                        nc.tensor.matmul(bank[s][:, :], hi, hx[:, 0, k, :], start=(k == 0), stop=False)
                        nc.tensor.matmul(bank[s][:, :], hi, hx[:, 1, k, :], start=False, stop=False)
                        mm = nc.tensor.matmul(bank[s][:, :], lo, hx[:, 0, k, :], start=False, stop=(k == KD - 1))
                    mm.then_inc(psum_full[s], 1)

                def scores(s):
                    pe.wait_ge(psum_free[s], t.now(s))
                    pe.wait_ge(sem(f"keys_loaded{s % 2}"), t.turn(f"keys{s % 2}") * 16 + 16)
                    take(4 + s % 2)
                    for tt in range(TT):
                        mm = nc.tensor.matmul(bank[4 + s % 2][:, tt * NK:(tt + 1) * NK], qm[:, s % 2, tt * P:(tt + 1) * P],
                                              keys[:, s % 2, :], start=True, stop=True)
                    mm.then_inc(psum_full[4 + s % 2], 1)

                with t.loop(PM // 4, {"keys0": 2, "keys1": 2, 4: 2, 5: 2} | each_slot(4)):
                    for s in range(4):
                        split_product(s)
                        if s > 0:
                            scores(s - 1)
                    scores(3)
                with t.loop(U_AHEAD // 3 - 1, each_slot(3)):
                    for s in range(3):
                        split_product(s)
                for s in range(3):
                    split_product(s)
                pe.wait_ge(sem("choices_ready"), l + 1)
                for n, src in enumerate((TS[:, :, :, :].rearrange("p t h k -> p (t h k)"), Ef[:, 0, :], Ef[:, 1, :])):
                    take(4 + n)
                    for tt in range(TT):
                        mm = nc.tensor.transpose(bank[4 + n][:, tt * P:(tt + 1) * P], src[:, tt * P:(tt + 1) * P], ident[:, :])
                    mm.then_inc(psum_full[4 + n], 1)
                mark(f"gates{l}")

                def dense_gates(a):
                    pe.wait_ge(sem("oh2_ready"), t.turn("oh2") + 1)
                    take(6 + a)
                    for j in range(4):
                        for q in range(3):
                            mm = nc.tensor.matmul(bank[6 + a][:, j * NK:(j + 1) * NK], oh1[:, a, j, :],
                                                  oh2[:, a, j, q, :], start=(q == 0), stop=(q == 2))
                    mm.then_inc(psum_full[6 + a], 1)

                with t.loop(T // 16, {6: 2, 7: 2, "oh2": 4} | each_slot(3)):
                    for s in range(3):
                        split_product(s)
                        dense_gates(s % 2)
                    dense_gates(1)
                for n in range(U_LAST):
                    split_product(n % 3)
                mark(f"down{l}")
                for s in range(4):
                    pe.wait_ge(psum_full[s], t.now(s))
                    pe.sem_inc(sem(f"down_used{s}"), 1)

                def down(s, first=False, last=False):
                    pe.wait_ge(sem(f"split_done{s}"), t.turn(f"split{s}") + 2)
                    pe.wait_ge(sem("w_ready"), t.turn("w_tile") + 2)
                    for j in range(KD):
                        if first:
                            take(j)
                        hi, lo = hl[:, s, 0, j, :], hl[:, s, 1, j, :]
                        nc.tensor.matmul(bank[j][:, :], hi, W[:, s, 0, :], start=first, stop=False)
                        nc.tensor.matmul(bank[j][:, :], hi, W[:, s, 1, :], start=False, stop=False)
                        mm = nc.tensor.matmul(bank[j][:, :], lo, W[:, s, 0, :], start=False, stop=last)
                        if last:
                            mm.then_inc(psum_full[j], 1)
                    if not last:
                        mm.then_inc(sem(f"down_used{s}"), 1)

                for s in range(4):
                    down(s, first=(s == 0))
                with t.loop(NK // 4 - 2, {"w_tile": 4, "split0": 1, "split1": 1, "split2": 1, "split3": 1}):
                    for s in range(4):
                        down(s)
                for s in range(4):
                    down(s, last=(s == 3))

            def deltanet():
                mark("gdn")
                pe.wait_ge(sem("h_ready"), t.turn("h_ready") + 1)
                slot_ready(0)
                take(0)
                for tt in range(TT):
                    for k in range(KD):
                        mm = nc.tensor.matmul(bank[0][:, tt * 2 * VH:(tt + 1) * 2 * VH], hT[:, k, tt * P:(tt + 1) * P],
                                              w_ring[:, 0, k, 0:2 * VH], start=(k == 0), stop=(k == KD - 1))
                mm.then_inc(psum_full[0], 1)
                pe.wait_ge(sem("graw_ready"), 1)
                pe.wait_ge(sem("gdn_masks"), 3)
                g_all = graw.rearrange("p t h -> p (t h)")
                n = TT * VH
                take(2)
                nc.tensor.matmul(bank[2][:, 0:n], tri[:, :], g_all, start=True, stop=True)
                nc.tensor.matmul(bank[2][:, n:2 * n], samec[:, :], g_all, start=True, stop=True).then_inc(psum_full[2], 1)
                take(3)
                nc.tensor.matmul(bank[3][:, 0:n], ones[0:CHUNK, :], g_all[0:CHUNK, :], start=True, stop=True
                                 ).then_inc(psum_full[3], 1)
                take(4)
                nc.tensor.matmul(bank[4][:, 0:n], ones[CHUNK:P, :], g_all[CHUNK:P, :], start=True, stop=True
                                 ).then_inc(psum_full[4], 1)
                mark("gdn_heads")
                per = {"w0": 2, "w1": 2, 0: 2, 1: 2, 2: 2, 3: 2, 4: 3, 5: 4, 6: 1, 7: 1, "gsel": 1, "gsq": 2, "qk": 1,
                       "ktok": 1, "vs": 2}
                with t.loop(KH, per):
                    tile_product(0, hT)
                    tile_product(1, hT)
                    tile_product(0, hT)
                    for q in range(2):
                        pe.wait_ge(sem("gdn_squares"), t.turn("gsq") + 1)
                        take(5)
                        nc.tensor.matmul(bank[5][:, :], ones[:, :], sq[:, q, :], start=True, stop=True
                                         ).then_inc(psum_full[5], 1)
                    tile_product(1, hT)
                    pe.wait_ge(sem("gsel_ready"), t.turn("gsel") * 3 + 3)
                    for a in range(2):
                        take(2)
                        nc.tensor.matmul(bank[2][:, :], tri[:, :], SG[:, a, :, :].rearrange("p t c -> p (t c)"),
                                         start=True, stop=True).then_inc(psum_full[2], 1)
                        take(3)
                        for tt in range(TT):
                            mm = nc.tensor.matmul(bank[3][:, tt * P:(tt + 1) * P], SG[:, a, tt, :], tri[:, :],
                                                  start=True, stop=True)
                        mm.then_inc(psum_full[3], 1)
                        take(4)
                        for tt in range(TT):
                            mm = nc.tensor.matmul(bank[4][:, tt * P:(tt + 1) * P],
                                                  gsel[:, tt, a:a + 1].to_broadcast([P, P]), tri[:, :],
                                                  start=True, stop=True)
                        mm.then_inc(psum_full[4], 1)
                    pe.wait_ge(sem("qk_ready"), t.turn("qk") * 2 + 2)
                    for b, rhs in ((6, 1), (7, 0)):
                        take(b)
                        for tt in range(TT):
                            c = slice(tt * P, (tt + 1) * P)
                            mm = nc.tensor.matmul(bank[b][:, c], cy[:, 1, c], cy[:, rhs, c], start=True, stop=True)
                        mm.then_inc(psum_full[b], 1)
                    take(4)
                    for tt in range(TT):
                        mm = nc.tensor.transpose(bank[4][:, tt * P:(tt + 1) * P], cy[:, 1, tt * P:(tt + 1) * P], ident[:, :])
                    mm.then_inc(psum_full[4], 1)
                    t.turn("ktok")
                    for a in range(2):
                        pe.wait_ge(sem("v_silu"), t.turn("vs") + 1)
                        take(5)
                        for tt in range(TT):
                            mm = nc.tensor.transpose(bank[5][:, tt * P:(tt + 1) * P], cy[:, 2 + a, tt * P:(tt + 1) * P],
                                                     ident[:, :])
                        mm.then_inc(psum_full[5], 1)
                mark("gdn_z")
                with t.loop(VH // 2, {"w0": 1, "w1": 1, 0: 1, 1: 1}):
                    tile_product(0, hT)
                    tile_product(1, hT)
                mark("gdn_groups")
                per = {2: 14, 3: 8, 4: 14, 5: 4, 6: 4, 7: 4, "grp": 1, "S": 9}
                with t.loop(VH // 4, per):
                    g0 = t.turn("grp")
                    pe.wait_ge(sem("Pb_loaded"), g0 * 256 + 256)
                    pe.wait_ge(sem("Eb_loaded"), g0 * 128 + 128)
                    pe.wait_ge(sem("vkb_loaded"), g0 * 16 + 16)

                    def four(b, left, right, is_t=False):
                        take(b)
                        for tt in range(TT):
                            c = slice(tt * P, (tt + 1) * P)
                            if is_t:
                                mm = nc.tensor.transpose(bank[b][:, c], left(tt), right(tt))
                            else:
                                mm = nc.tensor.matmul(bank[b][:, c], left(tt), right(tt), start=True, stop=True)
                        mm.then_inc(psum_full[b], 1)

                    def turned(a):
                        four(5, lambda tt: Pb[:, a, tt, :], lambda tt: ident[:, :], True)

                    turned(0)
                    for a in range(4):
                        if a < 3:
                            turned(a + 1)
                        pe.wait_ge(psum_free[5], t.now(5) - (1 if a < 3 else 0))
                        four(6, lambda tt: Eb[:, a, tt, :], lambda tt: Qs[:, a, tt, :])
                        pe.wait_ge(psum_free[6], t.now(6))
                        four(4, lambda tt: Pb[:, a, tt, :], lambda tt: Ys[:, a % 2, tt, :])
                    for a in range(4):
                        pe.wait_ge(psum_free[4], t.now(4) - (3 - a))
                        four(2, lambda tt: Qs[:, a, tt, :], lambda tt: vkb[:, a, 0, tt * P:(tt + 1) * P])
                        four(7, lambda tt: vkb[:, a, 1, tt * P:(tt + 1) * P], lambda tt: Qs[:, a, tt, :])
                    pe.wait_ge(psum_free[7], t.now(7))
                    pe.wait_ge(sem("kqa_loaded"), g0 * 16 + 16)
                    for n in range(NCH):
                        r, tt, s = CHUNK * (n % 2), n // 2, n % 2
                        rows = slice(r, r + CHUNK)
                        tok = slice(n * CHUNK, (n + 1) * CHUNK)
                        pe.wait_ge(sem("state_ready"), t.turn("S") + 1)
                        take(2)
                        for a in range(4):
                            mm = nc.tensor.matmul(bank[2][rows, a * P:(a + 1) * P], wTs[:, a, tok], S[:, s, a, :],
                                                  start=True, stop=True)
                        mm.then_inc(psum_full[2], 1)
                        pe.wait_ge(psum_free[2], t.now(2))
                        take(4)
                        for a in range(4):
                            mm = nc.tensor.matmul(bank[4][:, a * P:(a + 1) * P], kqa[rows, a, 0, tt * P:(tt + 1) * P],
                                                  vn[rows, a, :], start=True, stop=True)
                        mm.then_inc(psum_full[4], 1)
                        take(3)
                        for a in range(4):
                            nc.tensor.matmul(bank[3][:, a * CHUNK:(a + 1) * CHUNK], S[:, s, a, :], kqa[:, a, 1, tok],
                                             start=True, stop=False)
                            mm = nc.tensor.matmul(bank[3][:, a * CHUNK:(a + 1) * CHUNK], vn[rows, a, :],
                                                  kqa[rows, a, 2, tt * P + r:tt * P + r + CHUNK], start=False, stop=True)
                        mm.then_inc(psum_full[3], 1)
                    t.turn("S")
                    pe.wait_ge(sem("o_squares"), g0 + 1)
                    for a in range(4):
                        b = 2 + 2 * (a % 2)
                        take(b)
                        nc.tensor.matmul(bank[b][:, :], ones[:, :], o2[:, a, :], start=True, stop=True
                                         ).then_inc(psum_full[b], 1)
                mark("gdn_out")
                pe.wait_ge(sem("OT_ready"), VH + 1)
                with t.loop(KD, {"w0": 1, "w1": 1, 0: 1, 1: 1}):
                    tile_product(0, OT[:, 0:KD, :])
                    tile_product(1, OT[:, KD:VH, :])

            modulations()
            norm("norm0")
            attention()
            norm("norm1")
            peer(0)
            norm("norm2")
            deltanet()
            norm("norm3")
            peer(1)
            norm("norm4")

        @block.sync
        def _(sp):
            t = Tally(sp)
            for name, turn in FREE_AT_START.items():
                sp.sem_inc(sem(name), turn)

            def load(s, src, cols=P):
                n = t.turn(f"w{s}")
                sp.wait_ge(psum_full[s], n + w_base[s])
                sp.dma_start(w_ring[:, s, :, 0:cols], src).then_inc(sem(f"w_loaded{s}"), 16)

            w_base = [12, 12]

            def tile_of(w, m0, cols=P):
                return w[:, m0:m0 + cols].rearrange("(k p) c -> p k c", p=P)

            def tile_at(w, i, first=0):
                return w[:, ds(i * P + first, P)].rearrange("(k p) c -> p k c", p=P)

            sp.dma_start(condT[:, :], c_t).then_inc(sem("c_loaded"), 16)
            sp.dma_start(adab[:, :, :], ada_b).then_inc(sem("adab_loaded"), 16)
            for n in range(24):
                l, j, s = n // 12, n % 12, n % 2
                if n >= 2:
                    sp.wait_ge(psum_full[s], n // 2)
                sp.dma_start(ada_ring[:, s, :, :], ada_w[l, :, j * T:(j + 1) * T].rearrange("(k p) c -> p k c", p=P)
                             ).then_inc(sem(f"ada_loaded{s}"), 16)
                if n == 1:
                    sp.dma_start(xT[:, :, :], x_t.rearrange("(k p) t -> p k t", p=P)).then_inc(sem("x_loaded"), 16)
                    sp.dma_start(fnorm[:, :], final_norm).then_inc(sem("fnorm_loaded"), 16)
                    sp.dma_start(kvn[:, :], a_kv_norm).then_inc(sem("kvn_loaded"), 16)
            sp.wait_ge(sem("ada_rows"), 24)
            sp.dma_start(ada_dram.rearrange("(a r) c -> a (r c)", a=1), ada_row[:, :, :].rearrange("a l c -> a (l c)")
                         ).then_inc(sem("ada_stored"), 16)
            sp.wait_ge(sem("ada_stored"), 16)
            sp.dma_start(ada_sq[:, :], ada_dram).then_inc(sem("ada_square"), 16)

            def attention():
                load(0, tile_of(a_w_in, C_KV))
                load(1, tile_of(a_w_in, C_KV + P))
                n = t.turn("w0")
                sp.wait_ge(psum_full[0], n + w_base[0])
                kcols = a_w_in[:, C_KI:C_KI + ID].rearrange("(k p) c -> p k c", p=P)
                sp.dma_start(w_ring[:, 0, :, 0:ID], kcols).then_inc(sem("kidx_half"), 16)
                sp.dma_start(w_ring[:, 0, :, ID:P], kcols).then_inc(sem("w_loaded0"), 16)
                load(1, tile_of(a_w_in, C_WI, IH), cols=IH)
                for m in range(4):
                    load(m % 2, tile_of(a_w_in, C_QI + m * P))
                sp.dma_start(w_ukv[:, 0, :, :], a_w_uk.rearrange("(r p) c -> p r c", p=P)).then_inc(sem("ukv_loaded"), 16)
                sp.dma_start(w_ukv[:, 1, :, :], a_w_uv.rearrange("(r p) c -> p r c", p=P)).then_inc(sem("ukv_loaded"), 16)
                with t.loop(KD // 2, {"w0": 1, "w1": 1}) as i:
                    for s in range(2):
                        load(s, a_w_in[:, ds(i * 2 * P + s * P, P)].rearrange("(k p) c -> p k c", p=P))
                for s in range(2):
                    w_base[s] += HEADS
                with t.loop(KD // 2, {"w0": 1, "w1": 1}) as i:
                    for s in range(2):
                        load(s, a_w_out[:, ds(i * 2 * P + s * P, P)].rearrange("(k p) c -> p k c", p=P))

            def peer(l):
                sp.wait_ge(sem("x_ready"), 2 * l + 1)

                def slot(s):
                    sp.wait_ge(sem(f"split_done{s}"), t.turn(f"raw{s}") + 1)
                    return raw(s)

                def load_query(s, i):
                    sp.dma_start(slot(s), p_w_q[l, :, ds(i * P, P)].rearrange("(k p) c -> p k c", p=P)
                                 ).then_inc(sem(f"raw_loaded{s}"), 16)
                    n, h = t.turn(f"keys{s % 2}"), s % 2
                    sp.wait_ge(psum_full[4 + h], n + marks[f"router{l}"].get(4 + h, 0) - l * PM // 2)
                    sp.dma_start(keys[:, h, :], p_keys_t[l, ds(i, 1)].rearrange("m c k -> c (m k)")
                                 ).then_inc(sem(f"keys_loaded{h}"), 16)

                def load_up(s, tile):
                    sp.dma_start(slot(s), p_u_t[l, ds(tile, 1)].rearrange("a p k c -> (a p) k c")
                                 ).then_inc(sem(f"raw_loaded{s}"), 16)

                def load_down(s, tile):
                    sp.dma_start(slot(s), p_v[l][:, ds(tile, 1), :].rearrange("p a (k c) -> p (a k) c", c=P)
                                 ).then_inc(sem(f"raw_loaded{s}"), 16)

                def store_activations(s, tile):
                    sp.wait_ge(sem(f"gelu_done{s}"), t.turn(f"gelu{s}") + 1)
                    sp.dma_start(act_dram[ds(tile, 1)].rearrange("a p t -> (a p) t"), ga(s)
                                 ).then_inc(sem(f"act_stored{s}"), 16)

                for s in range(4):
                    if s == 2:
                        sp.wait_ge(sem("hx_ready"), l + 1)
                    load_query(s, s)
                with t.loop(PM // 4 - 1, {"raw0": 1, "raw1": 1, "raw2": 1, "raw3": 1, "keys0": 2, "keys1": 2}) as i:
                    for s in range(4):
                        load_query(s, i * 4 + (4 + s))
                for s in range(3):
                    load_up(s, s)
                per = {f"{name}{s}": 1 for name in ("raw", "gelu") for s in range(3)}

                def three_tiles(first, between=None):
                    for s in range(3):
                        load_up(s, first + (s + 3))
                        store_activations(s, first + s)
                        if between and s != 1:
                            between(s // 2)

                def store_gates(par, block, piece):
                    sp.dma_start(g_dram[ds(block, 1), :, ds(piece * GQ, GQ), :].rearrange("a p n t -> (a p) n t"),
                                 gst[:, par, ds(piece * GQ, GQ), :]).then_inc(sem(f"gst_stored{par}"), 16)

                def block(par, n, first, last_block=True):
                    if last_block:
                        sp.wait_ge(sem("gst_ready"), t.turn("gst") + 1)
                        sp.sem_inc(sem("seen"), 1)
                    with t.loop(2, per) as i:
                        three_tiles(first + i * 3, last_block and (lambda c: store_gates(1 - par, n - 1, i * 2 + c)))
                    with t.loop(2, per) as i:
                        three_tiles(first + 6 + i * 3)

                with t.loop(U_AHEAD // 3, per) as i:
                    three_tiles(i * 3)
                block(0, 0, U_AHEAD, last_block=False)
                with t.loop(T // GB // 2 - 1, {k: v * 8 for k, v in per.items()} | {"gst": 2}) as o:
                    block(1, o * 2 + 1, o * 24 + (U_AHEAD + 12))
                    block(0, o * 2 + 2, o * 24 + (U_AHEAD + 24))
                block(1, T // GB - 1, NK - U_LAST - 12)

                def load_activations(s, tile):
                    sp.wait_ge(sem(f"act_used{s}"), t.turn(f"act{s}"))
                    sp.dma_start(ua[:, s, :], act_dram[ds(tile, 1)].rearrange("a p t -> (a p) t")
                                 ).then_inc(sem(f"act_loaded{s}"), 16)

                def load_gates(par, group):
                    sp.wait_ge(sem(f"gg_used{par}"), t.turn(f"gg{par}"))
                    sp.dma_start(gg[:, par, :, :, :], g_dram[:, :, ds(group * 4, 4), :].rearrange("b p n t -> p b n t")
                                 ).then_inc(sem(f"gg_loaded{par}"), 16)

                sp.wait_ge(sem("gst_ready"), t.turn("gst") + 1)
                for n in range(U_LAST):
                    if n + 3 < U_LAST:
                        load_up(n % 3, NK - U_LAST + n + 3)
                    else:
                        load_down(n + 3 - U_LAST, n + 3 - U_LAST)
                    store_activations(n % 3, NK - U_LAST + n)
                    if n < 4:
                        store_gates(1, T // GB - 1, n)
                    if n == 5:
                        for par in range(2):
                            sp.wait_ge(sem(f"gst_stored{par}"), 64 * 4 * (l + 1) + 64)
                        for s in range(3):
                            sp.wait_ge(sem(f"act_stored{s}"), 16 * (t.n[f"gelu{s}"] - 1) + 16)
                        load_gates(0, 0)
                        for s in range(4):
                            load_activations(s, s)
                load_gates(1, 1)
                for s in range(3):
                    sp.wait_ge(sem(f"act_stored{s}"), 16 * t.n[f"gelu{s}"] + 16)

                def four_tiles(first, last=False):
                    for s in range(4):
                        if not last or s < 1:
                            load_down((s + 3) % 4, first + (s + 3))
                        if not last:
                            load_activations(s, first + (s + 4))

                per = {f"{name}{s}": 2 for name in ("raw", "act") for s in range(4)} | {"gg0": 1, "gg1": 1}
                with t.loop(NK // 8 - 1, per) as i:
                    for par in range(2):
                        four_tiles(i * 8 + 4 * par)
                        load_gates(par, i * 2 + (2 + par))
                four_tiles(NK - 8)
                four_tiles(NK - 4, last=True)

            def deltanet():
                for s in range(2):
                    w_base[s] = marks["gdn"][s] - t.n[f"w{s}"]
                sp.wait_ge(sem("x_ready"), 2)
                load(0, tile_of(b_w_in, C_BETA, 2 * VH), cols=2 * VH)
                sp.dma_start(alog[:, :], b_a_log.partition_broadcast(P).rearrange("p a h -> p (a h)")
                             ).then_inc(sem("gdn_params"), 16)
                sp.dma_start(dtb[:, :], b_dt_bias.partition_broadcast(P).rearrange("p a h -> p (a h)")
                             ).then_inc(sem("gdn_params"), 16)
                sp.dma_start(convw[:, :, :], b_conv).then_inc(sem("gdn_params"), 16)
                sp.dma_start(onorm[:, :], b_out_norm).then_inc(sem("gdn_params"), 16)

                def load_qk(i):
                    load(0, tile_at(b_w_in, i))
                    load(1, tile_at(b_w_in, i, KH * BD))

                def load_values(i):
                    load(0, tile_at(b_w_in, i * 2, 2 * KH * BD))
                    load(1, tile_at(b_w_in, i * 2, 2 * KH * BD + P))

                def store(a, i):
                    n = t.turn("packs")
                    head = ds(i * 2 + a, 1)
                    sp.wait_ge(sem("amat_ready"), n + 2)
                    for half in range(2):
                        rows = slice(half * CHUNK, (half + 1) * CHUNK)
                        sp.dma_start(a_dram[head].rearrange("a (t u) c s -> u c (a t) s", u=2)[half],
                                     amat[rows, a, :, half * CHUNK:(half + 1) * CHUNK]
                                     ).then_inc(sem(f"amat_stored{a}"), 16)
                    sp.wait_ge(sem("pack_v"), n + 1)
                    sp.wait_ge(sem("pack_ready"), n * 4 + 5)
                    sp.dma_start(pack_dram[head].rearrange("a p f t -> p (a f) t"), pack[:, a, :, :]
                                 ).then_inc(sem(f"pack_stored{a}"), 16)

                load_qk(0)
                with t.loop(KH - 1, {"w0": 2, "w1": 2, "packs": 2}) as i:
                    load_values(i)
                    load_qk(i + 1)
                    store(0, i)
                    store(1, i)
                load_values(KH - 1)
                store(0, KH - 1)
                store(1, KH - 1)
                for a in range(2):
                    sp.wait_ge(sem(f"amat_stored{a}"), 32 * KH + 16)
                    sp.wait_ge(sem(f"pack_stored{a}"), 16 * KH + 16)
                for q in range(2):
                    c = slice(q * HB, (q + 1) * HB)
                    sp.dma_start(SA[:, q, :, :], a_dram.rearrange("h n c s -> (h n) c s")[:, c, c]).then_inc(sem("SA_loaded"), 16)

                def load_gate(s, i):
                    load(s, b_w_in[:, ds(i * P + 2 * KH * BD + VH * BD, P)].rearrange("(k p) c -> p k c", p=P))

                with t.loop(VH // 2 - 2, {"w0": 1, "w1": 1}) as i:
                    for s in range(2):
                        load_gate(s, i * 2 + s)
                sp.wait_ge(sem("X_ready"), 1)
                sp.dma_start(t_dram, X[:, :, :, :]).then_inc(sem("X_stored"), 16)
                for n in range(VH - 4, VH):
                    load_gate(n % 2, n)
                sp.wait_ge(sem("X_stored"), 16)
                sp.wait_ge(sem("blocks_zero"), 2)
                T_v = t_dram.rearrange("(h t u) q i j -> u q i h t j", u=2, t=TT)
                E_v = a_dram.rearrange("h (t u) c s -> u c h t s", u=2)
                pv = pack_dram.rearrange("h p f t -> p h f t")
                with t.loop(VH // 4, {"grp": 1}) as i:
                    g0 = t.turn("grp")
                    hs = ds(i * 4, 4)
                    sp.wait_ge(psum_full[7], g0 * 4 + marks["gdn_groups"][7])
                    for half in range(2):
                        for q in range(2):
                            r = half * CHUNK + q * HB
                            for a in range(4):
                                sp.dma_start(Pb[r:r + HB, a, :, r:r + HB],
                                             T_v[half, q][:, ds(i * 4 + a, 1)].rearrange("i a t j -> i (a t) j")
                                             ).then_inc(sem("Pb_loaded"), 16)
                    for half in range(2):
                        r = half * CHUNK
                        for a in range(4):
                            sp.dma_start(Eb[r + HB:r + 2 * HB, a, :, r:r + HB],
                                         E_v[half][HB:, ds(i * 4 + a, 1), :, 0:HB].rearrange("c a t s -> c (a t) s")
                                         ).then_inc(sem("Eb_loaded"), 16)
                    sp.dma_start(vkb[:, :, :, :], pv[:, hs, 0:2, :]).then_inc(sem("vkb_loaded"), 16)
                    sp.wait_ge(psum_full[3], g0 * NCH + marks["gdn_groups"][3])
                    sp.dma_start(kqa[:, :, :, :], pv[:, hs, 2:5, :]).then_inc(sem("kqa_loaded"), 16)
                with t.loop(KD, {"w0": 1, "w1": 1}) as i:
                    for s in range(2):
                        load(s, b_w_out[s * D:(s + 1) * D, ds(i * P, P)].rearrange("(k p) c -> p k c", p=P))

            attention()
            peer(0)
            deltanet()
            peer(1)
            sp.wait_ge(sem("h_ready"), 5)
            sp.dma_start(out_t.rearrange("(k p) t -> p k t", p=P), hT[:, :, :]).then_inc(sem("out_stored"), 16)
            sp.wait_ge(sem("out_stored"), 16)

        @block.gpsimd
        def _(pool):
            nc.gpsimd.memset(ones[:, :], 1.0).then_inc(sem("consts"), 1)
            nc.gpsimd.memset(ident[:, :], 0.0).then_inc(sem("ident_zero"), 1)
            pool.wait_ge(sem("ident_zero"), 1)
            nc.gpsimd.affine_select(out=ident[:, :], in_=ident[:, :], compare_op=ALU.not_equal, fill=1.0, base=0,
                                    pattern=[[-1, P]], channel_multiplier=1).then_inc(sem("consts"), 1)
            nc.gpsimd.iota(iota_i[:, :], [[1, P]], base=0, channel_multiplier=0).then_inc(sem("iota_int"), 1)
            pool.wait_ge(sem("iota_int"), 1)
            nc.gpsimd.tensor_copy(iota[:, :], iota_i[:, :]).then_inc(sem("iota_ready"), 1)
            nc.gpsimd.tensor_copy(iota_b[:, :], iota_i[:, :]).then_inc(sem("iota_ready"), 1)
            pool.wait_ge(sem("mods_ready"), 1)
            nc.gpsimd.memset(maskb[:, 0, 0:P], 0.0).then_inc(sem("mask_zero"), 1)
            pool.wait_ge(sem("mask_zero"), 1)
            nc.gpsimd.memset(maskb[0:CHUNK, 0, CHUNK:P], NEG).then_inc(sem("mask_first"), 1)

            t = Tally(pool)

            def attention():
                t.n.update(marks["heads"])
                pool.wait_ge(sem("qkv_ready"), 1)
                with t.loop(HEADS // 2, {3: 2, "v": 1}) as hp:
                    pool.wait_ge(psum_full[3], t.turn(3, 2))
                    nc.gpsimd.tensor_copy(q_pair[:, :], qT[:, ds(hp, 1), :]).then_inc(sem("qk_pair_ready"), 1)
                    nc.gpsimd.tensor_copy(k_pair[:, :], kT[:, ds(hp, 1), :]).then_inc(sem("qk_pair_ready"), 1)
                    pool.wait_ge(psum_full[7], t.turn("v") + marks["heads"][7])
                    nc.gpsimd.tensor_copy(v_pair[:, :, :], vA[:, :, ds(hp * P, P)]).then_inc(sem("v_pair_ready"), 1)

            def step(ins):
                ins.then_inc(sem("pool_step"), 1)
                pool.wait_ge(sem("pool_step"), t.turn("pool_step") + 1)

            def peer(l):
                pool.wait_ge(sem("x_ready"), 2 * l + 1)
                step(nc.gpsimd.iota(iotac_i[:, :], [[1, NC_]], base=0, channel_multiplier=0))
                nc.gpsimd.tensor_copy(iotac[:, :], iotac_i[:, :]).then_inc(sem("iotac_ready"), 1)
                t.n.update({k: v for k, v in marks[f"router{l}"].items() if str(k).startswith("split")})

                def low(s):
                    pool.wait_ge(sem(f"high_done{s}"), t.turn(f"split{s}") + 1)
                    nc.gpsimd.tensor_tensor(hl[:, s, 1, :, :], raw(s), hl[:, s, 0, :, :].bitcast(F32), ALU.subtract
                                            ).then_inc(sem(f"split_done{s}"), 1)

                with t.loop(PM // 4, {"split0": 1, "split1": 1, "split2": 1, "split3": 1}):
                    for s in range(4):
                        low(s)
                with t.loop(NK // 3, {"split0": 1, "split1": 1, "split2": 1}):
                    for s in range(3):
                        low(s)
                for s in range(NK % 3):
                    low(s)

            def deltanet():
                pool.wait_ge(sem("x_ready"), 2)
                for m in (tri, strict, samec):
                    ins = nc.gpsimd.memset(m[:, :], 1.0)
                step(ins)
                step(nc.gpsimd.affine_select(out=tri[:, :], in_=tri[:, :], compare_op=ALU.is_ge, fill=0.0, base=0,
                                             pattern=[[1, P]], channel_multiplier=-1))
                step(nc.gpsimd.affine_select(out=strict[:, :], in_=strict[:, :], compare_op=ALU.is_gt, fill=0.0, base=0,
                                             pattern=[[-1, P]], channel_multiplier=1))
                step(nc.gpsimd.memset(samec[0:CHUNK, CHUNK:P], 0.0))
                step(nc.gpsimd.memset(samec[CHUNK:P, 0:CHUNK], 0.0))
                step(nc.gpsimd.memset(tri[0:CHUNK, CHUNK:P], 0.0))
                step(nc.gpsimd.memset(strict[CHUNK:P, 0:CHUNK], 0.0))
                pool.sem_inc(sem("gdn_masks"), 3)
                nc.gpsimd.memset(xs[:, :, 0:3], 0.0).then_inc(sem("xs_pad"), 1)
                pool.wait_ge(sem("gdn_masks"), 3)
                pool.wait_ge(sem("gstat_ready"), 1)
                t.n.update(marks["gdn_heads"])
                per = {3: 2, 4: 3, "gsq": 1, "kt": 1, "at": 2, "stored0": 1, "stored1": 1, "BS": 1}
                wide = [P, TT, P]

                with t.loop(KH, per) as i:
                    def column(of, a):
                        return of[:, :, ds(i * 2 + a, 1)].to_broadcast(wide)

                    pool.wait_ge(psum_full[3], t.turn(3, 2))
                    pool.wait_ge(psum_full[4], t.now(4))
                    nc.gpsimd.tensor_copy(gsel[:, :, :], graw[:, :, ds(i * 2, 2)]).then_inc(sem("gsel_ready"), 1)
                    for a in range(2):
                        nc.gpsimd.tensor_tensor(SG[:, a, :, :], strict[:, :].unsqueeze(1).to_broadcast(wide),
                                                column(graw, a), ALU.mult).then_inc(sem("gsel_ready"), 1)
                    pool.wait_ge(sem("amat_ready"), t.turn("BS") * 2 + 1)
                    for a in range(2):
                        nc.gpsimd.tensor_tensor(BS[:, a, :, :], strict[:, :].unsqueeze(1).to_broadcast(wide),
                                                column(beta, a), ALU.mult).then_inc(sem("BS_ready"), 1)
                    pool.wait_ge(sem("ktok_ready"), t.turn("kt") + 1)
                    for a in range(2):
                        pool.wait_ge(sem(f"pack_stored{a}"), t.turn(f"stored{a}") * 16 + 16)
                        for f, by in ((1, bege), (2, ekd)):
                            nc.gpsimd.tensor_tensor(pack[:, a, f, :].rearrange("p (t c) -> p t c", c=P), ktok[:, :, :],
                                                    column(by, a), ALU.mult).then_inc(sem("pack_ready"), 1)
                        nc.gpsimd.tensor_tensor(pack[:, a, 3, :], cy[:, 0, :], eG[:, a, :], ALU.mult
                                                ).then_inc(sem("pack_ready"), 1)
                        pool.wait_ge(sem("attn_raw"), t.turn("at") + 2)
                        at = pack[:, a, 4, :].rearrange("p (t c) -> p t c", c=P)
                        nc.gpsimd.tensor_tensor(at, at, tri[:, :].unsqueeze(1).to_broadcast(wide), ALU.mult
                                                ).then_inc(sem("pack_ready"), 1)
                    t.turn(4, 3), t.turn("gsq")
                for a in range(2):
                    pool.wait_ge(sem(f"pack_stored{a}"), 16 * KH + 16)
                    pool.wait_ge(sem(f"amat_stored{a}"), 32 * KH + 16)
                pool.wait_ge(sem("X_stored"), 16)
                nc.gpsimd.memset(Eb[:, :, :, :], 0.0).then_inc(sem("blocks_zero"), 1)
                nc.gpsimd.memset(Pb[:, :, :, :], 0.0).then_inc(sem("blocks_zero"), 1)

            attention()
            peer(0)
            deltanet()
            peer(1)

        @block.scalar
        def _(act):
            t = Tally(act)

            def sync(stage):
                t.n.update(marks[stage])

            def full(b):
                act.wait_ge(psum_full[b], t.turn(b) + 1)

            def step(ins):
                ins.then_inc(sem("act_step"), 1)
                act.wait_ge(sem("act_step"), t.turn("act_step") + 1)

            def modulations():
                sync("mod")
                act.wait_ge(sem("c_loaded"), 16)
                nc.scalar.activation(condT[:, :], condT[:, :], ACT.Silu).then_inc(sem("cond_ready"), 1)
                for n in range(24):
                    l, j, s = n // 12, n % 12, n % 2
                    full(s)
                    nc.scalar.activation(ada_row[0:1, l, j * T:(j + 1) * T], bank[s][0:1, :], ACT.Copy
                                         ).then_inc(psum_free[s], 1)
                act.wait_ge(psum_free[1], 12)
                act.sem_inc(sem("ada_rows"), 24)

            def norm(stage, gain=None, l=0, sh=0, sc=0, split=False):
                sync(stage)
                for k in range(KD):
                    nc.scalar.activation(hT[:, k, :], xT[:, k, :], ACT.Square).then_inc(sem("squares"), 1)
                act.wait_ge(sem("var_ready"), t.turn("var") + 1)
                nc.scalar.activation(rstd[:, :], rstd[:, :], ACT.Sqrt).then_inc(sem("std_ready"), 1)

                def high_of_input(k):
                    act.wait_ge(sem("act_step"), t.turn("act_step") + 1)
                    nc.scalar.activation(hx[:, 0, k, :], hT[:, k, :], ACT.Copy).then_inc(sem("hx_high"), 1)

                for k in range(KD):
                    act.wait_ge(sem("hn_ready"), t.turn("hn") + 1)
                    if gain is None:
                        ins = nc.scalar.activation(hT[:, k, :], hT[:, k, :], ACT.Identity,
                                                   bias=mods[:, l, sh + k:sh + k + 1], scale=mods[:, l, sc + k:sc + k + 1])
                    else:
                        ins = nc.scalar.activation(hT[:, k, :], hT[:, k, :], ACT.Copy, scale=gain[:, k:k + 1])
                    if split:
                        ins.then_inc(sem("act_step"), 1)
                        if k > 0:
                            high_of_input(k - 1)
                if split:
                    high_of_input(KD - 1)
                    act.sem_inc(sem("h_ready"), 1)
                else:
                    ins.then_inc(sem("h_ready"), 1)

            def evac(b, dst, src=None, func=ACT.Copy):
                full(b)
                nc.scalar.activation(dst, bank[b][:, :] if src is None else src, func).then_inc(psum_free[b], 1)

            def attention():
                sync("attn")
                evac(0, ckvT[:, 0, :])
                evac(1, ckvT[:, 1, :])
                act.wait_ge(psum_free[0], t.now(0))
                act.wait_ge(psum_free[1], t.now(1))
                nc.scalar.activation(ckv_sq[:, :, :], ckvT[:, :, :], ACT.Square).then_inc(sem("ckv_squares"), 1)
                full(0)
                nc.scalar.activation(kidxT[:, :], bank[0][:, :], ACT.Copy).then_inc(sem("idx_ready"), 1)
                act.wait_ge(sem("idx_ready"), 1)
                act.sem_inc(psum_free[0], 1)
                act.wait_ge(sem("ckv_var"), 1)
                nc.scalar.activation(rstd[:, :], rstd[:, :], ACT.Sqrt).then_inc(sem("ckv_std"), 1)
                full(1)
                nc.scalar.activation(widx[:, :, :], bank[1][:, 0:TT * IH].rearrange("p (t h) -> p t h", h=IH), ACT.Copy,
                                     scale=(IH ** -0.5) * (ID ** -0.5)).then_inc(sem("idx_ready"), 1)
                act.wait_ge(sem("idx_ready"), 2)
                act.sem_inc(psum_free[1], 1)
                for m in range(4):
                    b = m % 2
                    full(b)
                    nc.scalar.activation(qidxT[:, m, :], bank[b][:, :], ACT.Copy).then_inc(sem("idx_ready"), 1)
                    act.wait_ge(sem("idx_ready"), 3 + m)
                    act.sem_inc(psum_free[b], 1)
                for n in range(TT * IH):
                    N = (n // IH + 1) * P
                    b = 3 + n % 2
                    full(b)
                    if n >= 2:
                        act.wait_ge(sem("relu_used"), n - 1)
                    nc.scalar.activation(relu[:, n % 2, 0:N], bank[b][:, 0:N], ACT.Relu).then_inc(psum_free[b], 1)
                with t.loop(KD // 2, {0: 1, 1: 1}) as i:
                    evac(0, qT[:, ds(i * 2, 1), :])
                    evac(1, qT[:, ds(i * 2 + 1, 1), :])
                for m in range(KD):
                    evac(5 + m % 2, kT[:, m, :])
                for m in range(KD):
                    evac(6 + m % 2, vA[:, m // 2, (m % 2) * T:(m % 2 + 1) * T])
                sync("heads")
                act.wait_ge(psum_free[0], t.now(0))
                act.wait_ge(psum_free[1], t.now(1))
                act.wait_ge(psum_free[5], t.now(5))
                act.wait_ge(psum_free[6], t.now(6))
                act.wait_ge(psum_free[7], t.now(7))
                act.sem_inc(sem("qkv_ready"), 1)
                per = {4: 4, 5: 4, 6: 1, 7: 1, "pair": 1, "nmx": 8, "expd": 8}
                with t.loop(HEADS // 2, per) as hp:
                    n0 = t.turn("pair")

                    def exponentials(n):
                        tt, s = n % TT, n % 4
                        N = (tt + 1) * P
                        act.wait_ge(sem("nmx_ready"), t.turn("nmx") + 1)
                        nc.scalar.activation(prob[:, s, 0:N], lg[:, s, 0:N], ACT.Exp, bias=nmx[:, s:s + 1],
                                             scale=HD ** -0.5, accum_out=rowsum[:, s:s + 1]).then_inc(sem("exp_ready"), 1)

                    def turned(n):
                        a, tt = n // TT, n % TT
                        b = 4 + n % 2
                        full(b)
                        nc.scalar.activation(probT[:, a, 0:tt + 1, tt * P:(tt + 1) * P],
                                             bank[b][:, 0:(tt + 1) * P].rearrange("p (s c) -> p s c", c=P), ACT.Copy
                                             ).then_inc(sem("probT_ready"), 1)
                        act.wait_ge(sem("probT_ready"), t.turn("expd") + 1)
                        act.sem_inc(psum_free[b], 1)

                    def outputs(a):
                        b, r = 6 + a, HD * a
                        full(b)
                        nc.scalar.activation(oT[r:r + HD, ds(hp, 1), :], bank[b][r:r + HD, :], ACT.Copy
                                             ).then_inc(sem("oT_ready"), 1)
                        act.wait_ge(sem("oT_ready"), n0 * 2 + a + 1)
                        act.sem_inc(psum_free[b], 1)

                    for n in range(8):
                        exponentials(n)
                        if n >= 2:
                            turned(n - 2)
                        if n == 6:
                            outputs(0)
                    turned(6)
                    turned(7)
                    outputs(1)

            def peer(l):
                sync(f"router{l}")
                used0 = {s: marks[f"router{l}"].get(s, 0) - t.n.get(f"raw{s}", 0) for s in range(4)}

                def high(s, used=None):
                    n = t.turn(f"raw{s}")
                    act.wait_ge(sem(f"raw_loaded{s}"), n * 16 + 16)
                    if used is None:
                        act.wait_ge(psum_full[s], n + used0[s])
                    else:
                        act.wait_ge(sem(f"down_used{s}"), t.turn(f"down{s}") + 1)
                    nc.scalar.activation(hl[:, s, 0, :, :], raw(s), ACT.Copy).then_inc(sem(f"high_done{s}"), 1)

                def scores_out(s):
                    h = s % 2
                    act.wait_ge(sem(f"scores_used{h}"), t.turn(f"top{h}") + 1)
                    evac(4 + h, sS[:, h, :, :].rearrange("p t k -> p (t k)"))

                high(0)
                high(1)
                per = {0: 1, 1: 1, 2: 1, 3: 1, 4: 2, 5: 2, "top0": 2, "top1": 2, "raw0": 1, "raw1": 1, "raw2": 1, "raw3": 1}
                with t.loop(PM // 4, per):
                    for s in range(4):
                        high((s + 2) % 4)
                        evac(s, qm[:, s % 2, :])
                        if s > 0:
                            scores_out(s - 1)
                    scores_out(3)

                def activations(s):
                    act.wait_ge(sem(f"act_stored{s}"), t.turn(f"out_{s}") * 16 + 16)
                    full(s)
                    nc.scalar.activation(ga(s), bank[s][:, :], ACT.Gelu).then_inc(psum_free[s], 1)
                    act.wait_ge(psum_free[s], t.now(s))
                    act.sem_inc(sem(f"gelu_done{s}"), 1)

                per = {k: 1 for k in (0, 1, 2, "raw0", "raw1", "raw2", "out_0", "out_1", "out_2")}
                with t.loop(U_AHEAD // 3 - 1, per):
                    for s in range(3):
                        high((s + 2) % 3)
                        activations(s)
                for s in range(3):
                    if s == 1:
                        act.wait_ge(sem("shifted"), l + 1)
                        nc.scalar.activation(TS[:, :, :, :], TS[:, :, :, :], ACT.Exp).then_inc(sem("exps"), 1)
                    high((s + 2) % 3)
                    activations(s)
                for n, dst in enumerate((gT[:, :], iT[:, 0, :], iT[:, 1, :])):
                    full(4 + n)
                    nc.scalar.activation(dst, bank[4 + n][:, :], ACT.Copy).then_inc(sem("iT_ready"), 1)
                    act.wait_ge(sem("iT_ready"), 3 * l + n + 1)
                    act.sem_inc(psum_free[4 + n], 1)

                def gates_out(a, par, i, g):
                    full(6 + a)
                    nc.scalar.activation(gst[:, par, :, ds(i * 16 + g * 4, 4)],
                                         bank[6 + a][:, :].rearrange("p (t c) -> p c t", c=NK), ACT.Copy
                                         ).then_inc(psum_free[6 + a], 1)

                with t.loop(T // GB // 2, {k: v * 8 for k, v in per.items()} | {6: 16, 7: 16, "out0": 1, "out1": 1}):
                    for par in range(2):
                        act.wait_ge(sem(f"gst_stored{par}"), t.turn(f"out{par}") * 64 + 64)
                        with t.loop(4, per | {6: 2, 7: 2}) as i:
                            for s in range(3):
                                high((s + 2) % 3)
                                activations(s)
                                gates_out(s % 2, par, i, s)
                            gates_out(1, par, i, 3)
                        for a in range(2):
                            act.wait_ge(psum_free[6 + a], t.now(6 + a))
                        act.sem_inc(sem("gst_ready"), 1)
                for s in range(4):
                    base = l * (NK // 4 + (1 if s < 3 else 0))
                    t.n[f"w_high{s}"] = base
                    t.n[f"down{s}"] = base + (1 if s < 2 else 0)

                def w_high(s, first=False):
                    act.wait_ge(sem("gated"), t.turn("gated") + 1)
                    n = t.turn(f"w_high{s}")
                    if not first:
                        act.wait_ge(sem(f"down_used{s}"), n + 1)
                    nc.scalar.activation(W[:, s, 0, :], wp[:, s % 2, :], ACT.Copy).then_inc(sem("w_high"), 1)

                for n in range(U_LAST):
                    high((n + 2) % 3 if n + 2 < U_LAST else n + 2 - U_LAST)
                    if n == U_LAST - 1:
                        w_high(0, first=True)
                    activations(n % 3)
                for s in range(4):
                    if s > 0:
                        w_high(s, first=True)
                    high((s + 2) % 4, used="down")
                per = {f"{name}{s}": 1 for name in ("raw", "down", "w_high") for s in range(4)}
                with t.loop(NK // 4 - 2, per | {"gated": 4}):
                    for s in range(4):
                        w_high(s)
                        high((s + 2) % 4, used="down")
                for s in range(4):
                    w_high(s)
                    if s < 2:
                        high((s + 2) % 4, used="down")

            def deltanet():
                sync("gdn")
                act.wait_ge(sem("gdn_params"), 64)
                full(0)
                ba = bank[0][:, 0:TT * 2 * VH].rearrange("p (t c) -> p t c", c=2 * VH)
                step(nc.scalar.activation(beta, ba[:, :, 0:VH], ACT.Sigmoid))
                step(nc.scalar.activation(alog[:, :], alog[:, :], ACT.Exp))
                act.sem_inc(sem("beta_ready"), 1)
                act.wait_ge(sem("dt_added"), 1)
                step(nc.scalar.activation(gtmp[:, 1, :, :], gtmp[:, 0, :, :], ACT.Abs))
                step(nc.scalar.activation(gtmp[:, 1, :, :], gtmp[:, 1, :, :], ACT.Exp, scale=-1.0))
                nc.scalar.activation(gtmp[:, 1, :, :], gtmp[:, 1, :, :], ACT.Ln, bias=1.0).then_inc(sem("ln_ready"), 1)
                act.wait_ge(sem("gdiff_ready"), 1)
                nc.scalar.activation(eg, gcum, ACT.Exp)
                nc.scalar.activation(ekd, gtmp[:, 2, :, :], ACT.Exp)
                for u in range(2):
                    full(3 + u)
                    nc.scalar.activation(decay_last[:, u, :, :].rearrange("p t h -> p (t h)"),
                                         bank[3 + u][:, 0:TT * VH], ACT.Exp).then_inc(psum_free[3 + u], 1)
                act.wait_ge(psum_free[3], t.now(3))
                act.wait_ge(psum_free[4], t.now(4))
                act.sem_inc(sem("eg_ready"), 1)
                act.wait_ge(sem("xs_pad"), 1)
                act.wait_ge(sem("gstat_ready"), 1)
                sync("gdn_heads")
                per = {0: 2, 1: 2, 2: 2, 3: 2, 4: 3, "conv": 4, "lens": 1, "act_step": 3, "exps": 1}
                with t.loop(KH, per):
                    def tile_in(i):
                        s = i % 2
                        full(s)
                        act.wait_ge(sem("conv_done"), (c0 if i < 2 else c0 + i - 1) + 1)
                        nc.scalar.activation(xs[:, s, 3:3 + T], bank[s][:, :], ACT.Copy).then_inc(psum_free[s], 1)

                    def silu(i):
                        act.wait_ge(sem("conv_done"), c0 + i + 2)
                        ins = nc.scalar.activation(cy[:, i, :], cy[:, i, :], ACT.Silu)
                        if i < 2:
                            step(ins)
                            nc.scalar.activation(sq[:, i, :], cy[:, i, :], ACT.Square).then_inc(sem("gdn_squares"), 1)
                        else:
                            ins.then_inc(sem("v_silu"), 1)

                    c0 = t.turn("conv", 4)
                    tile_in(0)
                    tile_in(1)
                    silu(0)
                    silu(1)
                    tile_in(2)
                    tile_in(3)
                    silu(2)
                    silu(3)
                    act.wait_ge(sem("lens_ready"), t.turn("lens") * 2 + 2)
                    step(nc.scalar.activation(rn[:, :, :], rn[:, :, :], ACT.Sqrt))
                    act.sem_inc(sem("rn_sqrt"), 1)
                    x0 = t.turn("exps")
                    act.wait_ge(sem("attn_raw"), x0 * 2 + 1)
                    act.wait_ge(sem("pack_ready"), x0 * 8 + 1)
                    for a in range(2):
                        for b, dst in ((2, eD), (3, eDT)):
                            full(b)
                            nc.scalar.activation(dst[:, a, :, :].rearrange("p t c -> p (t c)"), bank[b][:, :], ACT.Exp
                                                 ).then_inc(psum_free[b], 1)
                        full(4)
                        nc.scalar.activation(eG[:, a, :], bank[4][:, :], ACT.Exp).then_inc(psum_free[4], 1)
                    full(4)
                    nc.scalar.activation(ktok[:, :, :].rearrange("p t c -> p (t c)"), bank[4][:, :], ACT.Copy
                                         ).then_inc(psum_free[4], 1)
                    act.wait_ge(psum_free[4], t.now(4))
                    act.wait_ge(psum_free[3], t.now(3))
                    act.sem_inc(sem("ktok_ready"), 1)
                sync("gdn_z")
                with t.loop(VH // 2, {0: 1, 1: 1}) as i:
                    for s in range(2):
                        full(s)
                        nc.scalar.activation(OT[:, ds(i * 2 + s, 1), :], bank[s][:, :].unsqueeze(1), ACT.Silu
                                             ).then_inc(psum_free[s], 1)
                sync("gdn_groups")
                per = {3: 8, 5: 4, 6: 4, 7: 4, "grp": 1}
                with t.loop(VH // 4, per):
                    g0 = t.turn("grp")

                    def copy(b, dst):
                        full(b)
                        nc.scalar.activation(dst, bank[b][:, :], ACT.Copy).then_inc(psum_free[b], 1)

                    def flat(x):
                        return x.rearrange("p t c -> p (t c)")

                    copy(5, flat(Qs[:, 0, :, :]))
                    for a in range(4):
                        if a < 3:
                            copy(5, flat(Qs[:, a + 1, :, :]))
                        copy(6, flat(Ys[:, a % 2, :, :]))
                    for a in range(4):
                        copy(7, wTs[:, a, :])
                    act.wait_ge(sem("OT_ready"), g0 * 4 + 1)
                    for n in range(NCH):
                        full(3)
                        nc.scalar.activation(oc[:, :, n * CHUNK:(n + 1) * CHUNK],
                                             bank[3][:, 0:4 * CHUNK].rearrange("p (a c) -> p a c", c=CHUNK), ACT.Copy
                                             ).then_inc(psum_free[3], 1)
                    act.wait_ge(psum_free[3], t.now(3))
                    nc.scalar.activation(o2[:, :, :], oc[:, :, :], ACT.Square).then_inc(sem("o_squares"), 1)
                    act.wait_ge(sem("o_vars"), g0 * 4 + 4)
                    nc.scalar.activation(o2[:, :, :], o2[:, :, :], ACT.Sqrt).then_inc(sem("o_stds"), 1)

            modulations()
            act.wait_ge(sem("x_loaded"), 16)
            act.wait_ge(sem("mods_ready"), 1)
            norm("norm0", l=0, sh=SH_M, sc=SC_M)
            attention()
            act.wait_ge(sem("x_ready"), 1)
            norm("norm1", l=0, sh=SH_F, sc=SC_F, split=True)
            peer(0)
            act.wait_ge(sem("x_ready"), 2)
            norm("norm2", l=1, sh=SH_M, sc=SC_M)
            deltanet()
            act.wait_ge(sem("x_ready"), 3)
            norm("norm3", l=1, sh=SH_F, sc=SC_F, split=True)
            peer(1)
            act.wait_ge(sem("x_ready"), 4)
            act.wait_ge(sem("fnorm_loaded"), 16)
            norm("norm4", gain=fnorm)

        @block.vector
        def _(dve):
            t = Tally(dve)

            def sync(stage):
                t.n.update(marks[stage])

            def full(b):
                dve.wait_ge(psum_full[b], t.turn(b) + 1)

            def step(ins):
                ins.then_inc(sem("dve_step"), 1)
                dve.wait_ge(sem("dve_step"), t.turn("dve_step") + 1)

            def carry():
                dve.sem_inc(sem("seen"), 1)

            def modulations():
                sync("mod")
                full(2)
                dve.wait_ge(sem("adab_loaded"), 16)
                nc.vector.tensor_tensor(mods[:, :, :], bank[2][:, 0:96].rearrange("p (l c) -> p l c", l=2), adab[:, :, :],
                                        ALU.add).then_inc(psum_free[2], 1)
                dve.wait_ge(psum_free[2], t.now(2))
                step(nc.vector.tensor_scalar(mods[:, :, SC_M:SC_M + KD], mods[:, :, SC_M:SC_M + KD], 1.0, None, ALU.add))
                nc.vector.tensor_scalar(mods[:, :, SC_F:SC_F + KD], mods[:, :, SC_F:SC_F + KD], 1.0, None, ALU.add
                                        ).then_inc(sem("mods_ready"), 1)

            def norm(stage):
                sync(stage)
                full(2)
                nc.vector.tensor_scalar(rstd[:, :], bank[2][:, :], 1.0 / D, EPS, ALU.mult, ALU.add
                                        ).then_inc(sem("var_ready"), 1)
                dve.wait_ge(sem("var_ready"), t.turn("var") + 1)
                dve.sem_inc(psum_free[2], 1)
                dve.wait_ge(sem("std_ready"), t.turn("std") + 1)
                step(nc.vector.reciprocal(rstd[:, :], rstd[:, :]))
                for k in range(KD):
                    nc.vector.tensor_tensor(hT[:, k, :], xT[:, k, :], rstd[:, :], ALU.mult).then_inc(sem("hn_ready"), 1)

            def attention():
                sync("attn")
                full(2)
                nc.vector.tensor_scalar(rstd[:, :], bank[2][:, :], 1.0 / RANK, EPS, ALU.mult, ALU.add
                                        ).then_inc(sem("ckv_var"), 1)
                dve.wait_ge(sem("ckv_var"), 1)
                dve.sem_inc(psum_free[2], 1)
                dve.wait_ge(sem("ckv_std"), 1)
                step(nc.vector.reciprocal(rstd[:, :], rstd[:, :]))
                dve.wait_ge(sem("kvn_loaded"), 16)
                for r in range(2):
                    ins = nc.vector.scalar_tensor_tensor(ckvT[:, r, :], ckvT[:, r, :], kvn[:, r:r + 1], rstd[:, :],
                                                         ALU.mult, ALU.mult)
                ins.then_inc(sem("ckv_ready"), 1)
                for n in range(TT * IH):
                    tt, h = n // IH, n % IH
                    N = (tt + 1) * P
                    b = 3 + n % 2
                    dve.wait_ge(psum_free[b], t.turn(b) + 1)
                    if n == 0:
                        dve.wait_ge(sem("idx_ready"), 6)
                    w = widx[:, tt, h:h + 1]
                    if h == 0:
                        ins = nc.vector.tensor_scalar(score[:, tt, 0:N], relu[:, n % 2, 0:N], w, None, ALU.mult)
                    else:
                        ins = nc.vector.scalar_tensor_tensor(score[:, tt, 0:N], relu[:, n % 2, 0:N], w, score[:, tt, 0:N],
                                                             ALU.mult, ALU.add)
                    ins.then_inc(sem("relu_used"), 1)
                    dve.wait_ge(sem("relu_used"), n + 1)
                for tt in range(1, TT):
                    step(nc.vector.memset(score[0:CHUNK, tt, tt * P + CHUNK:(tt + 1) * P], NEG))
                for _ in range(SEL // 8):
                    for tt in range(1, TT):
                        ins = nc.vector.max(top8[:, tt, :], score[:, tt, 0:(tt + 1) * P])
                    step(ins)
                    for tt in range(1, TT):
                        ins = nc.vector.match_replace(score[:, tt, 0:(tt + 1) * P], top8[:, tt, :],
                                                      score[:, tt, 0:(tt + 1) * P], TAKEN)
                    step(ins)
                for tt in range(1, TT):
                    N = (tt + 1) * P
                    ins = nc.vector.tensor_scalar(maskb[:, tt, 0:N], score[:, tt, 0:N], TAKEN / 2, NEG, ALU.is_gt, ALU.mult)
                step(ins)
                sync("heads")
                dve.wait_ge(sem("mask_first"), 1)
                per = {0: 2, 1: 2, 2: 2, 3: 2, "mx": 8, "nmx": 8, "exp": 8, "rinv": 8, "prob": 8}
                with t.loop(HEADS // 2, per):
                    def maxima(n):
                        tt, s = n % TT, n % 4
                        N = (tt + 1) * P
                        full(s)
                        carry()
                        nc.vector.tensor_tensor_reduce(lg[:, s, 0:N], bank[s][:, 0:N], maskb[:, tt, 0:N], 1.0, TAKEN,
                                                       ALU.add, ALU.max, mx[:, s:s + 1]).then_inc(psum_free[s], 1)
                        dve.wait_ge(psum_free[s], t.now(s))
                        nc.vector.tensor_scalar(nmx[:, s:s + 1], mx[:, s:s + 1], -(HD ** -0.5), None, ALU.mult
                                                ).then_inc(sem("nmx_ready"), 1)

                    def normalise(n):
                        tt, s = n % TT, n % 4
                        N = (tt + 1) * P
                        dve.wait_ge(sem("exp_ready"), t.turn("exp") + 1)
                        nc.vector.reciprocal(rinv[:, s:s + 1], rowsum[:, s:s + 1]).then_inc(sem("rinv_ready"), 1)
                        dve.wait_ge(sem("rinv_ready"), t.turn("rinv") + 1)
                        nc.vector.tensor_scalar(prob[:, s, 0:N], prob[:, s, 0:N], rinv[:, s:s + 1], None, ALU.mult
                                                ).then_inc(sem("prob_ready"), 1)

                    for n in range(8):
                        maxima(n)
                        if n >= 1:
                            normalise(n - 1)
                        t.turn("mx"), t.turn("nmx"), t.turn("prob")
                    normalise(7)
                sync("attn_out")
                with t.loop(KD // 2, {0: 1, 1: 1}) as i:
                    for s in range(2):
                        full(s)
                        nc.vector.scalar_tensor_tensor(xT[:, ds(i * 2 + s, 1), :], bank[s][:, :].unsqueeze(1),
                                                       mods[:, 0, ds(i * 2 + s + G_M, 1)], xT[:, ds(i * 2 + s, 1), :],
                                                       ALU.mult, ALU.add).then_inc(psum_free[s], 1)

            def x_updated():
                for b in range(8):
                    if t.n.get(b, 0):
                        dve.wait_ge(psum_free[b], t.now(b))
                dve.sem_inc(sem("x_ready"), 1)

            def peer(l):
                for k in range(KD):
                    dve.wait_ge(sem("hx_high"), KD * l + k + 1)
                    ins = nc.vector.tensor_tensor(hx[:, 1, k, :], hT[:, k, :], hx[:, 0, k, :].bitcast(F32), ALU.subtract)
                ins.then_inc(sem("hx_ready"), 1)
                sync(f"router{l}")
                with t.loop(PM // 4, {4: 2, 5: 2, "dve_step": 16}) as i:
                    for m in range(4):
                        s = m % 2
                        dve.wait_ge(psum_free[4 + s], t.turn(4 + s) + 1)
                        carry()
                        for tt in range(TT):
                            ins = nc.vector.max(val[:, s, tt, 0:8], sS[:, s, tt, :])
                        step(ins)
                        carry()
                        for tt in range(TT):
                            nc.vector.max_index(idx[:, s, tt, 0:8], val[:, s, tt, 0:8], sS[:, s, tt, :])
                            ins = nc.vector.match_replace(sW[:, tt, :], val[:, s, tt, 0:8], sS[:, s, tt, :], TAKEN)
                        step(ins)
                        dve.sem_inc(sem(f"scores_used{s}"), 1)
                        for tt in range(TT):
                            ins = nc.vector.max(val[:, s, tt, 8:16], sW[:, tt, :])
                        step(ins)
                        carry()
                        for tt in range(TT):
                            ins = nc.vector.max_index(idx[:, s, tt, 8:16], val[:, s, tt, 8:16], sW[:, tt, :])
                        step(ins)
                        nc.vector.tensor_copy(V[:, :, ds(i * 4 + m, 1), :], val[:, s, :, :].unsqueeze(2))
                        nc.vector.tensor_copy(I[:, :, ds(i * 4 + m, 1), :], idx[:, s, :, :].unsqueeze(2)
                                              ).then_inc(sem("lists_done"), 1)
                dve.wait_ge(sem("lists_done"), PM * (l + 1))
                firsts = I[:, :, :, :].rearrange("p t (h q) k -> p (t h) q k", q=2)[:, :, 0, :]
                step(nc.vector.tensor_scalar(firsts, firsts, float(NK), None, ALU.mult))

                def candidates(out, lists):
                    one = lists[:, :, :, :].rearrange("p t (h q) k -> p (t h) q k", q=2)
                    off = 0
                    for a in range(TOPK // 2):
                        n = ROWS[a]
                        nc.vector.tensor_tensor(out[:, :, off:off + n], one[:, :, 0, a:a + 1].to_broadcast([P, TT * PH, n]),
                                                one[:, :, 1, 0:n], ALU.add)
                        off += n
                    return nc.vector.tensor_tensor(out[:, :, off:NC_], one[:, :, 0, TOPK // 2:TOPK],
                                                   one[:, :, 1, 0:1].to_broadcast([P, TT * PH, TOPK // 2]), ALU.add)

                candidates(cand, V)
                step(candidates(code, I))
                dve.wait_ge(sem("iotac_ready"), l + 1)
                with t.loop(TT, {"dve_step": 9}) as i:
                    step(nc.vector.tensor_copy(cS[:, :, :], cand[:, ds(i * PH, PH), :]))
                    carry()
                    for h in range(PH):
                        ins = nc.vector.max(topv[:, h, 0:8], cS[:, h, :])
                    step(ins)
                    carry()
                    for h in range(PH):
                        nc.vector.max_index(topp[:, h, 0:8], topv[:, h, 0:8], cS[:, h, :])
                        ins = nc.vector.match_replace(cW[:, h, :], topv[:, h, 0:8], cS[:, h, :], TAKEN)
                    step(ins)
                    carry()
                    for h in range(PH):
                        ins = nc.vector.max(topv[:, h, 8:16], cW[:, h, :])
                    step(ins)
                    carry()
                    for h in range(PH):
                        ins = nc.vector.max_index(topp[:, h, 8:16], topv[:, h, 8:16], cW[:, h, :])
                    step(ins)
                    nc.vector.tensor_copy(TS[:, ds(i, 1), :, :], topv[:, :, :].unsqueeze(1))
                    step(nc.vector.tensor_copy(posf[:, :, :], topp[:, :, :]))
                    step(nc.vector.tensor_tensor(eq[:, :, :, :].rearrange("p h k c -> p (h k) c"),
                                                 posf[:, :, :].rearrange("p h k -> p (h k)").unsqueeze(2).to_broadcast([P, P, NC_]),
                                                 iotac[:, :].unsqueeze(1).to_broadcast([P, P, NC_]), ALU.is_equal))
                    step(nc.vector.tensor_tensor(eq[:, :, :, :], eq[:, :, :, :],
                                                 code[:, ds(i * PH, PH), :].unsqueeze(2).to_broadcast([P, PH, TOPK, NC_]),
                                                 ALU.mult))
                    step(nc.vector.tensor_reduce(E[:, ds(i, 1), :, :].rearrange("p a h k -> p (a h) k"),
                                                 eq[:, :, :, :], AX.X, ALU.add))
                lists = TS[:, :, :, :].rearrange("p t h k -> p (t h) k")
                step(nc.vector.tensor_copy(tsum[:, :].unsqueeze(2), lists[:, :, 0:1]))
                nc.vector.tensor_tensor(lists, lists, tsum[:, :].unsqueeze(2).to_broadcast([P, TT * PH, TOPK]),
                                        ALU.subtract).then_inc(sem("shifted"), 1)
                flat = E[:, :, :, :].rearrange("p t h k -> p (t h k)")
                step(nc.vector.tensor_copy(Ei[:, 0, :], flat))
                step(nc.vector.tensor_scalar(Ei[:, 1, :], Ei[:, 0, :], NK - 1, None, ALU.bitwise_and))
                step(nc.vector.tensor_scalar(Ei[:, 0, :], Ei[:, 0, :], 7, None, ALU.arith_shift_right))
                step(nc.vector.tensor_copy(Ef[:, :, :], Ei[:, :, :]))
                dve.wait_ge(sem("exps"), l + 1)
                step(nc.vector.tensor_reduce(tsum[:, :], lists, AX.X, ALU.add))
                step(nc.vector.reciprocal(tsum[:, :], tsum[:, :]))
                nc.vector.tensor_tensor(lists, lists, tsum[:, :].unsqueeze(2).to_broadcast([P, TT * PH, TOPK]), ALU.mult
                                        ).then_inc(sem("choices_ready"), 1)
                dve.wait_ge(sem("iT_ready"), 3 * l + 3)
                for q in range(3):
                    step(nc.vector.tensor_copy(gb[:, :], gT[:, :]))
                    step(nc.vector.tensor_copy(gp[:, q, :], gb[:, :]))
                    if q < 2:
                        step(nc.vector.tensor_tensor(gT[:, :], gT[:, :], gp[:, q, :], ALU.subtract))
                sync(f"gates{l}")
                with t.loop(T // 16, {6: 2, 7: 2}) as i:
                    for g in range(4):
                        a = g % 2
                        dve.wait_ge(psum_full[6 + a], t.turn(6 + a))
                        for j in range(4):
                            tok = i * 16 + (g * 4 + j)
                            nc.vector.tensor_scalar(oh1[:, a, j, :], iota_b[:, :], iT[:, 0, ds(tok, 1)], None,
                                                    ALU.is_equal)
                            for q in range(3):
                                ins = nc.vector.tensor_scalar(oh2[:, a, j, q, :], iota_b[:, :],
                                                              iT[:, 1, ds(tok, 1)], gp[:, q, ds(tok, 1)],
                                                              ALU.is_equal, ALU.mult)
                        ins.then_inc(sem("oh2_ready"), 1)
                sync(f"down{l}")

                def low(s):
                    dve.wait_ge(sem(f"high_done{s}"), t.turn(f"split{s}") + 1)
                    nc.vector.tensor_tensor(hl[:, s, 1, :, :], raw(s), hl[:, s, 0, :, :].bitcast(F32), ALU.subtract
                                            ).then_inc(sem(f"split_done{s}"), 1)

                def gate(s, par):
                    dve.wait_ge(sem(f"act_loaded{s}"), t.turn(f"act{s}") * 16 + 16)
                    dve.wait_ge(sem("w_ready"), t.now("gated") + 1)
                    nc.vector.tensor_tensor(wp[:, s % 2, :].rearrange("p (b t) -> p b t", t=GB),
                                            ua[:, s, :].rearrange("p (b t) -> p b t", t=GB), gg[:, par, :, s, :],
                                            ALU.mult).then_inc(sem("gated"), 1)
                    dve.wait_ge(sem("gated"), t.turn("gated") + 1)
                    dve.sem_inc(sem(f"act_used{s}"), 1)

                def w_low(s):
                    dve.wait_ge(sem("w_high"), t.turn("w_high") + 1)
                    nc.vector.tensor_tensor(W[:, s, 1, :], wp[:, s % 2, :], W[:, s, 0, :].bitcast(F32), ALU.subtract
                                            ).then_inc(sem("w_ready"), 1)

                per = {f"{name}{s}": 2 for name in ("split", "act") for s in range(4)}
                with t.loop(NK // 8, per | {"gg0": 1, "gg1": 1, "gated": 8, "w_high": 8}):
                    for par in range(2):
                        dve.wait_ge(sem(f"gg_loaded{par}"), t.turn(f"gg{par}") * 16 + 16)
                        for s in range(4):
                            gate(s, par)
                            if s == 3:
                                dve.sem_inc(sem(f"gg_used{par}"), 1)
                            low(s)
                            w_low(s)
                for j in range(KD):
                    full(j)
                    nc.vector.scalar_tensor_tensor(xT[:, j, :], bank[j][:, :], mods[:, l, G_F + j:G_F + j + 1], xT[:, j, :],
                                                   ALU.mult, ALU.add).then_inc(psum_free[j], 1)

            def deltanet():
                sync("gdn")
                dve.wait_ge(sem("gdn_params"), 64)
                full(0)
                dve.wait_ge(sem("beta_ready"), 1)
                ba = bank[0][:, 0:TT * 2 * VH].rearrange("p (t c) -> p t c", c=2 * VH)
                rows = [P, TT, VH]
                nc.vector.tensor_tensor(gtmp[:, 0, :, :], ba[:, :, VH:2 * VH], dtb[:, :].unsqueeze(1).to_broadcast(rows),
                                        ALU.add).then_inc(psum_free[0], 1)
                dve.wait_ge(psum_free[0], t.now(0))
                dve.sem_inc(sem("dt_added"), 1)
                step(nc.vector.tensor_scalar(gtmp[:, 2, :, :], gtmp[:, 0, :, :], 0.0, None, ALU.max))
                dve.wait_ge(sem("ln_ready"), 1)
                step(nc.vector.tensor_tensor(gtmp[:, 1, :, :], gtmp[:, 1, :, :], gtmp[:, 2, :, :], ALU.add))
                nc.vector.scalar_tensor_tensor(graw, gtmp[:, 1, :, :], -1.0, alog[:, :].unsqueeze(1).to_broadcast(rows),
                                               ALU.mult, ALU.mult).then_inc(sem("graw_ready"), 1)
                full(2)
                n = TT * VH
                step(nc.vector.tensor_copy(gcum.rearrange("p t h -> p (t h)"), bank[2][:, 0:n]))
                nc.vector.tensor_tensor(gtmp[:, 2, :, :].rearrange("p t h -> p (t h)"), bank[2][:, n:2 * n],
                                        gcum.rearrange("p t h -> p (t h)"), ALU.subtract).then_inc(psum_free[2], 1)
                dve.wait_ge(psum_free[2], t.now(2))
                dve.sem_inc(sem("gdiff_ready"), 1)
                dve.wait_ge(sem("eg_ready"), 1)
                nc.vector.tensor_tensor(bege, beta, eg, ALU.mult).then_inc(sem("gstat_ready"), 1)
                sync("gdn_heads")
                per = {2: 2, 3: 2, 5: 4, 6: 1, 7: 1, "dve_step": 15, "x": 4, "p": 1}
                with t.loop(KH, per) as i:
                    p0 = t.turn("p")

                    def conv(j, tile):
                        s = j % 2
                        t.turn("x")
                        dve.wait_ge(psum_free[s], p0 * 2 + (marks["gdn_heads"][s] + j // 2 + 1))
                        if j == 0:
                            dve.wait_ge(sem("pack_ready"), p0 * 8 + 1)
                        step(nc.vector.tensor_scalar(cy[:, j, :], xs[:, s, 0:T], convw[:, tile, 0], None, ALU.mult))
                        for w in range(1, 4):
                            ins = nc.vector.scalar_tensor_tensor(cy[:, j, :], xs[:, s, w:w + T], convw[:, tile, w],
                                                                 cy[:, j, :], ALU.mult, ALU.add)
                            if w < 3:
                                step(ins)
                        ins.then_inc(sem("conv_done"), 1)

                    conv(0, ds(i, 1))
                    conv(1, ds(i + KH, 1))
                    for q in range(2):
                        full(5)
                        nc.vector.tensor_scalar(rn[:, q, :], bank[5][:, :], EPS, None, ALU.add).then_inc(psum_free[5], 1)
                        dve.wait_ge(psum_free[5], t.now(5))
                        dve.sem_inc(sem("lens_ready"), 1)
                        conv(2 + q, ds(i * 2 + 2 * KH + q, 1))
                    dve.wait_ge(sem("rn_sqrt"), p0 + 1)
                    step(nc.vector.reciprocal(rn[:, :, :], rn[:, :, :]))
                    nc.vector.scalar_tensor_tensor(cy[:, 0, :], cy[:, 0, :], BD ** -0.5, rn[:, 0, :], ALU.mult, ALU.mult
                                                   ).then_inc(sem("qk_ready"), 1)
                    nc.vector.tensor_tensor(cy[:, 1, :], cy[:, 1, :], rn[:, 1, :], ALU.mult).then_inc(sem("qk_ready"), 1)
                    full(6)
                    full(7)
                    dve.wait_ge(sem("BS_ready"), p0 * 2 + 2)
                    for a in range(2):
                        flat = lambda x: x.rearrange("p t c -> p (t c)")
                        dve.wait_ge(psum_free[2], t.turn(2) + 1)
                        dve.wait_ge(sem(f"amat_stored{a}"), p0 * 32 + 16)
                        step(nc.vector.tensor_tensor(flat(amat[:, a, :, :]), bank[6][:, :], flat(eD[:, a, :, :]), ALU.mult))
                        nc.vector.tensor_tensor(flat(amat[:, a, :, :]), flat(amat[:, a, :, :]), flat(BS[:, a, :, :]),
                                                ALU.mult).then_inc(sem("amat_ready"), 1)
                        dve.wait_ge(psum_free[3], t.turn(3) + 1)
                        dve.wait_ge(sem(f"pack_stored{a}"), p0 * 16 + 16)
                        nc.vector.tensor_tensor(pack[:, a, 4, :], bank[7][:, :], flat(eDT[:, a, :, :]), ALU.mult
                                                ).then_inc(sem("attn_raw"), 1)
                    dve.wait_ge(sem("attn_raw"), p0 * 2 + 3)
                    dve.sem_inc(psum_free[6], 1)
                    dve.sem_inc(psum_free[7], 1)
                    for a in range(2):
                        full(5)
                        nc.vector.tensor_tensor(pack[:, a, 0, :].rearrange("p (t c) -> p t c", c=P),
                                                bank[5][:, :].rearrange("p (t c) -> p t c", c=P),
                                                beta[:, :, ds(i * 2 + a, 1)].to_broadcast([P, TT, P]), ALU.mult
                                                ).then_inc(psum_free[5], 1)
                        dve.wait_ge(psum_free[5], t.now(5))
                        dve.sem_inc(sem("pack_v"), 1)
                dve.wait_ge(sem("SA_loaded"), 32)
                step(nc.vector.memset(X[:, :, :, :], 0.0))
                diag = X[:, :, :, :].rearrange("p q i j -> p q (i j)")[:, :, 0:HB * HB:HB + 1]
                step(nc.vector.memset(diag, 1.0))
                step(nc.vector.tensor_scalar(SA[:, :, :, :], SA[:, :, :, :], -1.0, None, ALU.mult))
                for r in range(1, HB):
                    pr = prod[:, 0:2 * r * r].rearrange("p (q c j) -> p q c j", q=2, c=r)
                    step(nc.vector.tensor_tensor(pr, SA[:, :, r, 0:r].unsqueeze(2).to_broadcast([P, 2, r, r]),
                                                 X[:, :, 0:r, 0:r].rearrange("p q j c -> p q c j"), ALU.mult))
                    step(nc.vector.tensor_reduce(X[:, :, r, 0:r], pr, AX.X, ALU.add))
                dve.sem_inc(sem("X_ready"), 1)
                dve.wait_ge(sem("X_stored"), 16)
                for s in range(2):
                    dve.wait_ge(psum_free[s], marks["gdn_groups"][s])
                sync("gdn_groups")
                per = {2: 14, 4: 14, "g": 1, "S": 9, "dve_step": 3}
                with t.loop(VH // 4, per) as i:
                    g0 = t.turn("g")
                    for a in range(4):
                        full(4)
                        nc.vector.tensor_tensor(Qs[:, a, :, :].rearrange("p t c -> p (t c)"),
                                                Qs[:, a, :, :].rearrange("p t c -> p (t c)"), bank[4][:, :], ALU.subtract
                                                ).then_inc(psum_free[4], 1)
                    for a in range(4):
                        full(2)
                        nc.vector.tensor_copy(us[:, a, :, :].rearrange("p t c -> p (t c)"), bank[2][:, :]
                                              ).then_inc(psum_free[2], 1)
                    nc.vector.memset(S[:, 0, :, :], 0.0).then_inc(sem("state_ready"), 1)
                    t.turn("S")
                    dve.wait_ge(psum_free[2], t.now(2))
                    for n in range(NCH):
                        rows, tt = slice(CHUNK * (n % 2), CHUNK * (n % 2 + 1)), n // 2
                        full(2)
                        nc.vector.tensor_tensor(vn[rows, :, :], us[rows, :, tt, :],
                                                bank[2][rows, :].rearrange("p (a c) -> p a c", c=P), ALU.subtract
                                                ).then_inc(psum_free[2], 1)
                        full(4)
                        dve.wait_ge(sem("state_ready"), t.now("S"))
                        for a in range(4):
                            ins = nc.vector.scalar_tensor_tensor(S[:, (n + 1) % 2, a, :], S[:, n % 2, a, :],
                                                                 decay_last[:, n % 2, tt, ds(i * 4 + a, 1)],
                                                                 bank[4][:, a * P:(a + 1) * P], ALU.mult, ALU.add)
                        ins.then_inc(sem("state_ready"), 1)
                        dve.wait_ge(sem("state_ready"), t.turn("S") + 1)
                        dve.sem_inc(psum_free[4], 1)
                    for a in range(4):
                        b = 2 + 2 * (a % 2)
                        full(b)
                        nc.vector.tensor_scalar(o2[:, a, :], bank[b][:, :], 1.0 / BD, EPS, ALU.mult, ALU.add
                                                ).then_inc(psum_free[b], 1)
                        dve.wait_ge(psum_free[b], t.now(b))
                        dve.sem_inc(sem("o_vars"), 1)
                    dve.wait_ge(sem("o_stds"), g0 + 1)
                    step(nc.vector.reciprocal(o2[:, :, :], o2[:, :, :]))
                    step(nc.vector.scalar_tensor_tensor(oc[:, :, :], oc[:, :, :], onorm[:, 0:1], o2[:, :, :],
                                                        ALU.mult, ALU.mult))
                    for a in range(4):
                        ins = nc.vector.tensor_tensor(OT[:, ds(i * 4 + a, 1), :], oc[:, a:a + 1, :],
                                                      OT[:, ds(i * 4 + a, 1), :], ALU.mult)
                    step(ins)
                    dve.sem_inc(sem("OT_ready"), 4)
                sync("gdn_out")
                with t.loop(KD, {0: 1, 1: 1, "dve_step": 1}) as i:
                    for s in range(2):
                        full(s)
                        ins = nc.vector.scalar_tensor_tensor(xT[:, ds(i, 1), :], bank[s][:, :].unsqueeze(1),
                                                             mods[:, 1, ds(i + G_M, 1)], xT[:, ds(i, 1), :], ALU.mult, ALU.add)
                        if s == 0:
                            step(ins)
                            dve.sem_inc(psum_free[0], 1)
                        else:
                            ins.then_inc(psum_free[1], 1)

            modulations()
            norm("norm0")
            attention()
            x_updated()
            norm("norm1")
            peer(0)
            x_updated()
            norm("norm2")
            deltanet()
            x_updated()
            norm("norm3")
            peer(1)
            x_updated()
            norm("norm4")


def lay_out(a):
    import numpy as np

    cols = lambda v, p=P: np.ascontiguousarray(v.reshape(-1, p).T)
    return {
        "x_t": np.ascontiguousarray(a["x"][0].T),
        "c_t": cols(a["c"][0]),
        "ada_w": a["ada_w"],
        "ada_b": np.ascontiguousarray(a["ada_b"].reshape(2, 6 * KD, P).transpose(2, 0, 1)),
        "a_w_in": a["a_w_in"][0],
        "a_kv_norm": cols(a["a_kv_norm"][0]),
        "a_w_uk": a["a_w_uk"][0].reshape(RANK, HEADS * HD),
        "a_w_uv": a["a_w_uv"][0].reshape(RANK, HEADS * HD),
        "a_w_out": a["a_w_out"][0],
        "b_w_in": a["b_w_in"][0],
        "b_conv": np.ascontiguousarray(a["b_conv"][0, :, 0, :].reshape(4, -1, P).transpose(2, 1, 0)),
        "b_a_log": a["b_a_log"],
        "b_dt_bias": a["b_dt_bias"],
        "b_out_norm": cols(a["b_out_norm"][0]),
        "b_w_out": a["b_w_out"][0],
        "p_w_q": a["p_w_q"],
        "p_keys_t": np.ascontiguousarray(a["p_sub_keys"].reshape(2, PM, NK, P).transpose(0, 1, 3, 2)),
        "p_u_t": np.ascontiguousarray(a["p_u"].reshape(2, NK, NK, KD, P).transpose(0, 2, 4, 3, 1)),
        "p_v": a["p_v"].reshape(2, NK, NK, D),
        "final_norm": cols(a["final_norm"]),
    }


def kernel(**inputs):
    import numpy as np
    import concourse.bacc as bacc
    from concourse.bass_utils import run_bass_kernel_spmd

    a = {k: np.asarray(v) for k, v in inputs.items()}
    arrays = lay_out(a)
    nc = bacc.Bacc("TRN2", target_bir_lowering=False, num_devices=1)
    args = [nc.dram_tensor(n, v.shape, mybir.dt.from_np(v.dtype), kind="ExternalInput").ap() for n, v in arrays.items()]
    out = nc.dram_tensor("out_t", (D, T), F32, kind="ExternalOutput").ap()
    hybrid_trunk(nc, *args, out)
    got = run_bass_kernel_spmd(nc, [arrays], core_ids=[0]).results[0]["out_t"]
    return np.ascontiguousarray(got.T).reshape(1, T, D)
```
